# Optimizing a Trainium2 kernel written in Bass

```python
import math
import jax, jax.numpy as jnp
from jax import lax
import numpy as np

D_MODEL = 1024
BATCH = 1
SEQ = 2048
DEPTH = 1

N_META = 16
D_SSM = D_MODEL // 2
D_POOL = D_MODEL - D_SSM
SSM_GROUP = 16
SSM_GROUPS = D_SSM // SSM_GROUP
SSM_STATE = 64
POOL_WINDOWS = (2, 4, 8, 16)
POOL_GROUPS = len(POOL_WINDOWS)
POOL_GROUP_DIM = D_POOL // POOL_GROUPS
D_FF = ((8 * D_MODEL // 3 + 255) // 256) * 256
STEP_MIN = 1e-3
STEP_MAX = 1e-1
EPS = 1e-6


def rmsnorm(x, g):
    xf = x.astype(jnp.float32)
    return xf * lax.rsqrt(jnp.mean(xf * xf, axis=-1, keepdims=True) + EPS) * g.astype(jnp.float32)

def _complex_affine_combine(e1, e2):
    a1r, a1i, b1r, b1i = e1
    a2r, a2i, b2r, b2i = e2
    ar = a2r * a1r - a2i * a1i
    ai = a2r * a1i + a2i * a1r
    br = a2r * b1r - a2i * b1i + b2r
    bi = a2r * b1i + a2i * b1r + b2i
    return (ar, ai, br, bi)

def s5_mixer(u, lam_re, lam_im, log_step, b_re, b_im, c_re, c_im, d, glu_w, glu_b):
    L = u.shape[1]
    lr = jnp.minimum(lam_re.astype(jnp.float32), -1e-4)
    li = lam_im.astype(jnp.float32)
    step = jnp.exp(log_step.astype(jnp.float32))[:, None]
    mag = jnp.exp(lr * step)
    ang = li * step
    abr = mag * jnp.cos(ang)
    abi = mag * jnp.sin(ang)
    nr = abr - 1.0
    ni = abi
    den = lr * lr + li * li
    cr = ((nr * lr + ni * li) / den)[..., None]
    ci = ((ni * lr - nr * li) / den)[..., None]
    br = b_re.astype(jnp.float32)
    bi = b_im.astype(jnp.float32)
    bbr = cr * br - ci * bi
    bbi = cr * bi + ci * br
    uf = u.astype(jnp.float32)
    bu_r = jnp.einsum('blgh,gph->blgp', uf, bbr)
    bu_i = jnp.einsum('blgh,gph->blgp', uf, bbi)
    a_r = jnp.broadcast_to(abr[None, None], (1, L) + abr.shape)
    a_i = jnp.broadcast_to(abi[None, None], (1, L) + abi.shape)
    _, _, sr, si = lax.associative_scan(_complex_affine_combine, (a_r, a_i, bu_r, bu_i), axis=1)
    y = (jnp.einsum('blgp,ghp->blgh', sr, c_re.astype(jnp.float32))
         - jnp.einsum('blgp,ghp->blgh', si, c_im.astype(jnp.float32))
         + d.astype(jnp.float32) * uf)
    g = jax.nn.gelu(y)
    gate = jnp.einsum('blgh,ghk->blgk', g, glu_w.astype(jnp.float32)) + glu_b.astype(jnp.float32)
    return g * jax.nn.sigmoid(gate)

def pool_mixer(v, pool_w, pool_scale):
    L = v.shape[1]
    vf = v.astype(jnp.float32)
    cs = jnp.cumsum(vf, axis=1)
    t = jnp.arange(1, L + 1, dtype=jnp.float32)
    outs = []
    for k, w in enumerate(POOL_WINDOWS):
        ck = cs[:, :, k]
        lower = jnp.pad(ck, ((0, 0), (w, 0), (0, 0)))[:, :L]
        cnt = jnp.minimum(t, float(w))[None, :, None]
        outs.append((ck - lower) / cnt - vf[:, :, k])
    p = jnp.stack(outs, axis=2)
    p = jnp.einsum('blkc,kcd->blkd', p, pool_w.astype(jnp.float32))
    return p * pool_scale.astype(jnp.float32)

def first_inputs(seed: int = 0) -> dict:
    key = jax.random.key(seed)
    ks = jax.random.split(key, 24)
    f32 = jnp.float32
    G, H, P = SSM_GROUPS, SSM_GROUP, SSM_STATE
    n = jnp.arange(P, dtype=f32)
    x = jax.random.normal(ks[0], (BATCH, SEQ, D_MODEL), f32)
    meta_tokens = jax.random.normal(ks[1], (N_META, D_MODEL), f32)
    norm1_g = 1.0 + 0.02 * jax.random.normal(ks[2], (DEPTH, D_MODEL), f32)
    w_in = jax.random.normal(ks[3], (DEPTH, D_MODEL, D_MODEL), f32) * D_MODEL ** -0.5
    ssm_lambda_re = -0.5 + 0.01 * jax.random.normal(ks[4], (DEPTH, G, P), f32)
    ssm_lambda_im = math.pi * n + 0.01 * jax.random.normal(ks[5], (DEPTH, G, P), f32)
    ssm_log_step = jax.random.uniform(ks[6], (DEPTH, G), f32, math.log(STEP_MIN), math.log(STEP_MAX))
    ssm_b_re = jax.random.normal(ks[7], (DEPTH, G, P, H), f32) * (2.0 * H) ** -0.5
    ssm_b_im = jax.random.normal(ks[8], (DEPTH, G, P, H), f32) * (2.0 * H) ** -0.5
    ssm_c_re = jax.random.normal(ks[9], (DEPTH, G, H, P), f32) * (2.0 * P) ** -0.5 * 4.0
    ssm_c_im = jax.random.normal(ks[10], (DEPTH, G, H, P), f32) * (2.0 * P) ** -0.5 * 4.0
    ssm_d = jax.random.normal(ks[11], (DEPTH, G, H), f32)
    ssm_glu_w = jax.random.normal(ks[12], (DEPTH, G, H, H), f32) * H ** -0.5
    ssm_glu_b = 0.02 * jax.random.normal(ks[13], (DEPTH, G, H), f32)
    ssm_norm_g = 1.0 + 0.02 * jax.random.normal(ks[14], (DEPTH, D_SSM), f32)
    pool_w = jax.random.normal(ks[15], (DEPTH, POOL_GROUPS, POOL_GROUP_DIM, POOL_GROUP_DIM), f32) * POOL_GROUP_DIM ** -0.5
    pool_scale = 1.0 + 0.1 * jax.random.normal(ks[16], (DEPTH, POOL_GROUPS, POOL_GROUP_DIM), f32)
    pool_norm_g = 1.0 + 0.02 * jax.random.normal(ks[17], (DEPTH, D_POOL), f32)
    w_out = jax.random.normal(ks[18], (DEPTH, D_MODEL, D_MODEL), f32) * D_MODEL ** -0.5
    norm2_g = 1.0 + 0.02 * jax.random.normal(ks[19], (DEPTH, D_MODEL), f32)
    w_gate = jax.random.normal(ks[20], (DEPTH, D_MODEL, D_FF), f32) * D_MODEL ** -0.5
    w_up = jax.random.normal(ks[21], (DEPTH, D_MODEL, D_FF), f32) * D_MODEL ** -0.5
    w_down = jax.random.normal(ks[22], (DEPTH, D_FF, D_MODEL), f32) * D_FF ** -0.5
    final_norm_g = 1.0 + 0.02 * jax.random.normal(ks[23], (D_MODEL,), f32)
    return {"x": x, "meta_tokens": meta_tokens, "norm1_g": norm1_g, "w_in": w_in,
            "ssm_lambda_re": ssm_lambda_re, "ssm_lambda_im": ssm_lambda_im,
            "ssm_log_step": ssm_log_step, "ssm_b_re": ssm_b_re, "ssm_b_im": ssm_b_im,
            "ssm_c_re": ssm_c_re, "ssm_c_im": ssm_c_im, "ssm_d": ssm_d,
            "ssm_glu_w": ssm_glu_w, "ssm_glu_b": ssm_glu_b, "ssm_norm_g": ssm_norm_g,
            "pool_w": pool_w, "pool_scale": pool_scale, "pool_norm_g": pool_norm_g,
            "w_out": w_out, "norm2_g": norm2_g, "w_gate": w_gate, "w_up": w_up,
            "w_down": w_down, "final_norm_g": final_norm_g}

def first_block(x, meta_tokens, norm1_g, w_in, ssm_lambda_re, ssm_lambda_im, ssm_log_step,
              ssm_b_re, ssm_b_im, ssm_c_re, ssm_c_im, ssm_d, ssm_glu_w, ssm_glu_b,
              ssm_norm_g, pool_w, pool_scale, pool_norm_g, w_out, norm2_g, w_gate, w_up,
              w_down, final_norm_g):
    B = x.shape[0]
    meta = jnp.broadcast_to(meta_tokens.astype(jnp.float32)[None], (B, N_META, D_MODEL))
    h = jnp.concatenate([meta, x.astype(jnp.float32)], axis=1)
    L = h.shape[1]
    for i in range(DEPTH):
        n1 = rmsnorm(h, norm1_g[i])
        proj = n1 @ w_in[i].astype(jnp.float32)
        u = proj[..., :D_SSM].reshape(B, L, SSM_GROUPS, SSM_GROUP)
        v = proj[..., D_SSM:].reshape(B, L, POOL_GROUPS, POOL_GROUP_DIM)
        ys = s5_mixer(u, ssm_lambda_re[i], ssm_lambda_im[i], ssm_log_step[i], ssm_b_re[i],
                      ssm_b_im[i], ssm_c_re[i], ssm_c_im[i], ssm_d[i], ssm_glu_w[i],
                      ssm_glu_b[i]).reshape(B, L, D_SSM)
        yp = pool_mixer(v, pool_w[i], pool_scale[i]).reshape(B, L, D_POOL)
        mixed = jnp.concatenate([rmsnorm(ys, ssm_norm_g[i]), rmsnorm(yp, pool_norm_g[i])], axis=-1)
        h = h + mixed @ w_out[i].astype(jnp.float32)
        n2 = rmsnorm(h, norm2_g[i])
        ff = jax.nn.silu(n2 @ w_gate[i].astype(jnp.float32)) * (n2 @ w_up[i].astype(jnp.float32))
        h = h + ff @ w_down[i].astype(jnp.float32)
    out = rmsnorm(h, final_norm_g)[:, N_META:]
    return out.astype(x.dtype)


_first_inputs = first_inputs


def first_inputs(seed=0):
    import zlib

    import numpy as np

    out = dict(_first_inputs(seed))
    spreads = {}
    factors = {'meta_tokens': 4.078,
     'norm1_g': 3.5,
     'ssm_lambda_re': 8.0,
     'ssm_glu_b': 8.0,
     'ssm_norm_g': 5.805,
     'pool_norm_g': 5.506,
     'norm2_g': 5.088,
     'final_norm_g': 2.905}
    for name, (base, spread) in spreads.items():
        noise = np.random.default_rng([zlib.crc32(name.encode()), seed]).standard_normal(out[name].shape)
        drawn = base * np.exp(spread * noise) if base else spread * noise
        out[name] = __import__('jax').numpy.asarray(drawn.astype(out[name].dtype))
    for name, factor in factors.items():
        out[name] = (out[name] * factor).astype(out[name].dtype)
    return out


_narrow_inputs = first_inputs


def first_inputs(seed=0):
    out = dict(_narrow_inputs(seed))
    wider = {'meta_tokens': 4.11,
     'ssm_lambda_re': 12.0,
     'ssm_norm_g': 3.51,
     'pool_norm_g': 3.53,
     'final_norm_g': 3.27}
    for name, times in wider.items():
        mean = out[name].mean()
        out[name] = (mean + times * (out[name] - mean)).astype(out[name].dtype)
    return out


CHUNK = 64
D_MIX = D_MODEL
D_ATT = D_MIX // 2
N_ATT_HEADS = 8
ATT_HEAD_DIM = D_ATT // N_ATT_HEADS
LEFT_CHUNKS = 8
BAND = (LEFT_CHUNKS + 1) * CHUNK
REL_CLIP = 128
D_GLA_V = D_MIX - D_ATT
N_GLA_HEADS = 4
D_GLA_K = D_GLA_V // 2
GLA_HEAD_K = D_GLA_K // N_GLA_HEADS
GLA_HEAD_V = D_GLA_V // N_GLA_HEADS
GLA_LOW_RANK = 16
GLA_TAU = 16.0
D_PLE = 256
LN_EPS = 1e-5
RMS_EPS = 1e-6
DEEPNORM_ALPHA = (2.0 * DEPTH) ** 0.25
DEEPNORM_BETA = (8.0 * DEPTH) ** -0.25
D_IN_PROJ = 4 * D_ATT + 2 * D_GLA_K + 2 * D_GLA_V + GLA_LOW_RANK


def _split_sizes():
    return (D_ATT, D_ATT, D_ATT, D_ATT, D_GLA_K, D_GLA_K, D_GLA_V, D_GLA_V, GLA_LOW_RANK)

def layer_norm(x, g, b):
    xf = x.astype(jnp.float32)
    mu = jnp.mean(xf, axis=-1, keepdims=True)
    xc = xf - mu
    var = jnp.mean(xc * xc, axis=-1, keepdims=True)
    y = xc * lax.rsqrt(var + LN_EPS) * g.astype(jnp.float32) + b.astype(jnp.float32)
    return y.astype(x.dtype)

def chunk_band_attention(q, k, v, rel_table):
    b, s, h, dh = q.shape
    nc = s // CHUNK
    q = jnp.transpose(q, (0, 2, 1, 3))
    k = jnp.transpose(k, (0, 2, 1, 3))
    v = jnp.transpose(v, (0, 2, 1, 3))
    left = LEFT_CHUNKS * CHUNK
    k_pad = jnp.pad(k, ((0, 0), (0, 0), (left, 0), (0, 0)))
    v_pad = jnp.pad(v, ((0, 0), (0, 0), (left, 0), (0, 0)))
    q_chunks = jnp.moveaxis(q.reshape(b, h, nc, CHUNK, dh), 2, 0)
    qi = jnp.arange(CHUNK)[:, None]
    kj = jnp.arange(BAND)[None, :]
    rel = qi + left - kj
    rel_idx = jnp.clip(rel, -REL_CLIP, REL_CLIP) + REL_CLIP
    bias = rel_table.astype(jnp.float32)[:, rel_idx]
    scale = ATT_HEAD_DIM ** -0.5

    def one_chunk(args):
        c, q_blk = args
        start = c * CHUNK
        k_blk = lax.dynamic_slice_in_dim(k_pad, start, BAND, axis=2)
        v_blk = lax.dynamic_slice_in_dim(v_pad, start, BAND, axis=2)
        sc = jnp.einsum('bhqd,bhkd->bhqk', q_blk, k_blk).astype(jnp.float32) * scale + bias
        valid = (start - left + kj) >= 0
        sc = jnp.where(valid, sc, -1e30)
        pr = jax.nn.softmax(sc, axis=-1)
        return jnp.einsum('bhqk,bhkd->bhqd', pr.astype(v_blk.dtype), v_blk)

    out = lax.map(one_chunk, (jnp.arange(nc), q_chunks))
    out = jnp.transpose(out, (1, 0, 3, 2, 4))
    return out.reshape(b, s, h * dh)

def gla_chunked(q, k, v, log_a):
    b, s, h, dk = q.shape
    dv = v.shape[-1]
    nc = s // CHUNK
    f32 = jnp.float32
    qf = q.astype(f32).reshape(b, nc, CHUNK, h, dk) * (dk ** -0.5)
    kf = k.astype(f32).reshape(b, nc, CHUNK, h, dk)
    vf = v.astype(f32).reshape(b, nc, CHUNK, h, dv)
    L = jnp.cumsum(log_a.astype(f32).reshape(b, nc, CHUNK, h, dk), axis=2)
    L_end = L[:, :, -1:]
    eL = jnp.exp(L)
    e_negL = jnp.exp(-L)
    q_fwd = qf * eL
    a_causal = jnp.einsum('bnthd,bnshd->bnhts', q_fwd, kf * e_negL)
    a_anti = jnp.einsum('bnthd,bnshd->bnhts', qf * e_negL, kf * eL)
    tril = jnp.tril(jnp.ones((CHUNK, CHUNK), dtype=bool))
    att = jnp.where(tril, a_causal, a_anti)
    o_intra = jnp.einsum('bnhts,bnshv->bnthv', att, vf)
    kv = jnp.einsum('bnshd,bnshv->bnhdv', kf * jnp.exp(L_end - L), vf)
    chunk_decay = jnp.exp(L_end[:, :, 0])

    def step(state, inp):
        dec, kv_c = inp
        return dec[..., None] * state + kv_c, state

    init = jnp.zeros((b, h, dk, dv), f32)
    _, s_prev = lax.scan(step, init, (jnp.moveaxis(chunk_decay, 1, 0), jnp.moveaxis(kv, 1, 0)))
    s_prev = jnp.moveaxis(s_prev, 0, 1)
    o_inter = jnp.einsum('bnthd,bnhdv->bnthv', q_fwd, s_prev)
    return (o_intra + o_inter).reshape(b, s, h, dv)

def second_inputs(seed: int = 0) -> dict:
    key = jax.random.key(seed)
    ks = jax.random.split(key, 20)
    f32 = jnp.float32
    n = jax.random.normal
    x = n(ks[0], (BATCH, SEQ, D_MODEL), f32)
    p = n(ks[1], (DEPTH, BATCH, SEQ, D_PLE), f32)
    ln_in_g = 1.0 + 0.02 * n(ks[2], (D_MODEL,), f32)
    ln_in_b = 0.02 * n(ks[3], (D_MODEL,), f32)
    w_in = n(ks[4], (DEPTH, D_MODEL, D_IN_PROJ), f32) * D_MODEL ** -0.5
    w_gla_gate = n(ks[5], (DEPTH, GLA_LOW_RANK, D_GLA_K), f32) * GLA_LOW_RANK ** -0.5
    b_gla_gate = 0.1 * n(ks[6], (DEPTH, D_GLA_K), f32) + 1.0
    rel_bias = 0.1 * n(ks[7], (DEPTH, N_ATT_HEADS, 2 * REL_CLIP + 1), f32)
    gla_norm_g = 1.0 + 0.02 * n(ks[8], (DEPTH, N_GLA_HEADS, GLA_HEAD_V), f32)
    w_out = n(ks[9], (DEPTH, D_MIX, D_MODEL), f32) * (D_MIX ** -0.5) * DEEPNORM_BETA
    w_ple = n(ks[10], (DEPTH, D_PLE, D_MODEL), f32) * D_PLE ** -0.5
    w_ple_gate = n(ks[11], (DEPTH, D_MODEL, D_MODEL), f32) * D_MODEL ** -0.5
    b_ple_gate = 0.02 * n(ks[12], (DEPTH, D_MODEL), f32)
    ln_g = 1.0 + 0.02 * n(ks[13], (DEPTH, D_MODEL), f32)
    ln_b = 0.02 * n(ks[14], (DEPTH, D_MODEL), f32)
    return {"x": x, "p": p, "ln_in_g": ln_in_g, "ln_in_b": ln_in_b, "w_in": w_in,
            "w_gla_gate": w_gla_gate, "b_gla_gate": b_gla_gate, "rel_bias": rel_bias,
            "gla_norm_g": gla_norm_g, "w_out": w_out, "w_ple": w_ple,
            "w_ple_gate": w_ple_gate, "b_ple_gate": b_ple_gate, "ln_g": ln_g, "ln_b": ln_b}

def second_block(x, p, ln_in_g, ln_in_b, w_in, w_gla_gate, b_gla_gate, rel_bias,
              gla_norm_g, w_out, w_ple, w_ple_gate, b_ple_gate, ln_g, ln_b):
    b, s, _ = x.shape
    split_points = np.cumsum(np.array(_split_sizes()))[:-1].tolist()
    h = layer_norm(x, ln_in_g, ln_in_b)
    for i in range(DEPTH):
        proj = h @ w_in[i]
        (aq, ak, av, ag, gq, gk, gv, gg, glr) = jnp.split(proj, split_points, axis=-1)
        att = chunk_band_attention(
            aq.reshape(b, s, N_ATT_HEADS, ATT_HEAD_DIM),
            ak.reshape(b, s, N_ATT_HEADS, ATT_HEAD_DIM),
            av.reshape(b, s, N_ATT_HEADS, ATT_HEAD_DIM),
            rel_bias[i])
        att = att * jax.nn.silu(ag)
        gate_logit = (glr @ w_gla_gate[i] + b_gla_gate[i]).astype(jnp.float32)
        log_a = jax.nn.log_sigmoid(gate_logit) / GLA_TAU
        o = gla_chunked(
            gq.reshape(b, s, N_GLA_HEADS, GLA_HEAD_K),
            gk.reshape(b, s, N_GLA_HEADS, GLA_HEAD_K),
            gv.reshape(b, s, N_GLA_HEADS, GLA_HEAD_V),
            log_a.reshape(b, s, N_GLA_HEADS, GLA_HEAD_K))
        o = o * lax.rsqrt(jnp.mean(o * o, axis=-1, keepdims=True) + RMS_EPS) \
            * gla_norm_g[i].astype(jnp.float32)
        gla = o.reshape(b, s, D_GLA_V).astype(h.dtype) * jax.nn.silu(gg)
        mix = jnp.concatenate([att.astype(h.dtype), gla], axis=-1) @ w_out[i]
        r = DEEPNORM_ALPHA * h + mix
        ple_gate = jax.nn.sigmoid(r @ w_ple_gate[i] + b_ple_gate[i])
        r = r + ple_gate * (p[i] @ w_ple[i])
        h = layer_norm(r, ln_g[i], ln_b[i])
    return h


_first_inputs_2 = second_inputs


def second_inputs(seed=0):
    import zlib

    import numpy as np

    out = dict(_first_inputs_2(seed))
    spreads = {}
    factors = {'ln_in_g': 2.803,
     'ln_in_b': 2.977,
     'w_gla_gate': 3.024,
     'b_gla_gate': 6.109,
     'rel_bias': 8.0,
     'gla_norm_g': 8.0,
     'b_ple_gate': 8.0,
     'ln_g': 2.74,
     'ln_b': 2.873}
    for name, (base, spread) in spreads.items():
        noise = np.random.default_rng([zlib.crc32(name.encode()), seed]).standard_normal(out[name].shape)
        drawn = base * np.exp(spread * noise) if base else spread * noise
        out[name] = __import__('jax').numpy.asarray(drawn.astype(out[name].dtype))
    for name, factor in factors.items():
        out[name] = (out[name] * factor).astype(out[name].dtype)
    return out


_narrow_inputs_2 = second_inputs


def second_inputs(seed=0):

    out = dict(_narrow_inputs_2(seed))
    wider = {'gla_norm_g': 3.91, 'b_ple_gate': 12.0, 'ln_g': 3.09, 'ln_b': 3.08}
    for name, times in wider.items():
        mean = out[name].mean()
        out[name] = (mean + times * (out[name] - mean)).astype(out[name].dtype)
    return out


def setup_inputs(seed=0):
    out = dict(first_inputs(seed))
    for name, value in second_inputs(seed + 1).items():
        if name != "x":
            out[name + "_2"] = value
    return out


def reference(
    x, meta_tokens, norm1_g, w_in, ssm_lambda_re, ssm_lambda_im, ssm_log_step, ssm_b_re,
    ssm_b_im, ssm_c_re, ssm_c_im, ssm_d, ssm_glu_w, ssm_glu_b, ssm_norm_g, pool_w, pool_scale,
    pool_norm_g, w_out, norm2_g, w_gate, w_up, w_down, final_norm_g, p_2, ln_in_g_2, ln_in_b_2,
    w_in_2, w_gla_gate_2, b_gla_gate_2, rel_bias_2, gla_norm_g_2, w_out_2, w_ple_2,
    w_ple_gate_2, b_ple_gate_2, ln_g_2, ln_b_2,
):
    x = first_block(
        x, meta_tokens, norm1_g, w_in, ssm_lambda_re, ssm_lambda_im, ssm_log_step, ssm_b_re,
        ssm_b_im, ssm_c_re, ssm_c_im, ssm_d, ssm_glu_w, ssm_glu_b, ssm_norm_g, pool_w,
        pool_scale, pool_norm_g, w_out, norm2_g, w_gate, w_up, w_down, final_norm_g,
    )
    return second_block(
        x, p_2, ln_in_g_2, ln_in_b_2, w_in_2, w_gla_gate_2, b_gla_gate_2, rel_bias_2,
        gla_norm_g_2, w_out_2, w_ple_2, w_ple_gate_2, b_ple_gate_2, ln_g_2, ln_b_2,
    )


_drawn_inputs = setup_inputs


def setup_inputs(seed=0):
    import zlib

    import numpy as np

    out = dict(_drawn_inputs(seed))
    spreads = {}
    factors = {}
    for name, (base, spread) in spreads.items():
        noise = np.random.default_rng([zlib.crc32(name.encode()), seed]).standard_normal(out[name].shape)
        drawn = base * np.exp(spread * noise) if base else spread * noise
        out[name] = __import__('jax').numpy.asarray(drawn.astype(out[name].dtype))
    for name, factor in factors.items():
        out[name] = (out[name] * factor).astype(out[name].dtype)
    return out
```

```python
import math
from contextlib import ExitStack

import numpy as np

import concourse.bass as bass
from concourse import mybir

F32 = mybir.dt.float32
F32R = mybir.dt.float32r
U32 = mybir.dt.uint32
ALU = mybir.AluOpType
ACT = mybir.ActivationFunctionType
AX = mybir.AxisListType

P = 128
D = 1024
KT = D // P
TOK = 2048
META = 16
NT = TOK // P
CH = 8
NCH = (TOK + META) // CH
MCH = META // CH
G, H, PS = 32, 16, 64
NQ = G // 2
W5 = 512
DFF = 2816
NJ = DFF // P
HALF = TOK // 2
HT = HALF // P
NWIN = 4
EPS = 1e-6
LN_EPS = 1e-5
BAND_T = 5
BAND_W = BAND_T * P
NHEAD = 8
CLIP = 128
EXT = 768
ALPHA = 2.0 ** 0.25
NEG = -1e30
TWO_PI_HI = 6.28125
TWO_PI_LO = 2 * math.pi - TWO_PI_HI
ROUND = 1.5 * 2.0 ** 23
PI_LOW = 3.1415925


def flat(waits):
    for w in waits:
        if isinstance(w, list):
            yield from flat(w)
        elif w is not None:
            yield w


class Program:

    def __init__(self, nc, ctx):
        self.nc, self.ctx = nc, ctx
        self.sems, self.count, self.waited = [], [], {}
        self.idle = {}
        self.fresh()

    def fresh(self):
        self.queue = {e: [] for e in ("pe", "act", "dve", "pool", "sp")}
        self.at = {}

    def _sem(self, engine, name, by):
        kind = (engine, by)
        if name in self.at:
            assert self.at[name][1] == kind, name
            return self.at[name][0]
        if self.idle.get(kind):
            n = self.idle[kind].pop(0)
        else:
            n = len(self.sems)
            self.sems.append(self.ctx.enter_context(self.nc.semaphore(
                f"{engine}_{'dma' if by == 16 else 'step'}{n}")))
            self.count.append(0)
        self.at[name] = (n, kind)
        return n

    def step(self, engine, name, run, waits, by=1):
        n = self._sem(engine, name, by)
        self.queue[engine].append((self.needed(engine, waits), run, self.sems[n], by))
        self.count[n] += by
        return (n, self.count[n])

    def needed(self, engine, waits):
        top = {}
        for n, value in flat(waits):
            top[n] = max(value, top.get(n, 0))
        need = [(n, v) for n, v in top.items() if v > self.waited.get((engine, n), 0)]
        for n, v in need:
            self.waited[(engine, n)] = v
        return [(self.sems[n], v) for n, v in need]

    def hold(self, engine, *waits):
        self.queue[engine].append((self.needed(engine, waits), None, None, 0))

    def pe(self, name, run, *waits):
        return self.step("pe", name, run, waits)

    def act(self, name, run, *waits):
        return self.step("act", name, run, waits)

    def dve(self, name, run, *waits):
        return self.step("dve", name, run, waits)

    def pool(self, name, run, *waits):
        return self.step("pool", name, run, waits)

    def load(self, name, out, in_, *waits, q="sp"):
        return self.step(q, name, lambda e: e.dma_start(out, in_), waits, 16)

    def emit(self):
        queue = self.queue

        def play(items):
            def body(eng):
                for need, run, sem, by in items:
                    for s, v in need:
                        eng.wait_ge(s, v)
                    if run is not None:
                        run(eng).then_inc(sem, by)
            return body

        with self.nc.Block() as block:
            block.sync(play(queue["sp"]))
            block.gpsimd(play(queue["pool"]))
            block.scalar(play(queue["act"]))
            block.vector(play(queue["dve"]))
            block.tensor(play(queue["pe"]))
        for n, kind in self.at.values():
            self.idle.setdefault(kind, []).append(n)
        self.fresh()


def products(e, out, lhs, rhs, first, last):
    e.matmul(out, lhs[1], rhs[0], start=first, stop=False)
    e.matmul(out, lhs[0], rhs[1], start=False, stop=False)
    return e.matmul(out, lhs[0], rhs[0], start=False, stop=last)


def contraction(out, lhs, rhs):
    def run(e):
        n = len(lhs)
        for k in range(n):
            ins = products(e, out, lhs[k], rhs[k], k == 0, k == n - 1)
        return ins
    return run


def turns(out, tiles, ident):
    def run(e):
        for j, tile in enumerate(tiles):
            ins = e.transpose(out[:, j * P:(j + 1) * P], tile, ident[:, :])
        return ins
    return run


def split_pair(pr, tag, hi, lo, src, *waits):
    a = pr.act(f"{tag}_hi", lambda e: e.activation(hi, src, ACT.Copy), *waits)
    return pr.dve(f"{tag}_lo", lambda e: e.tensor_tensor(lo, src, hi.bitcast(F32), ALU.subtract),
                  a, *waits)


def spread(ap, n):
    return bass.AP(tensor=ap.tensor, offset=ap.offset, ap=[list(x) for x in ap.ap] + [[0, n]])


def last_of(fns):
    def run(e):
        for f in fns:
            ins = f(e)
        return ins
    return run


def mm(out, l, r, first=True, last=True):
    return lambda e: e.matmul(out, l, r, start=first, stop=last)


def over_partitions(ap, width):
    return bass.AP(tensor=ap.tensor, offset=ap.offset, ap=[[0, P], [1, width]])


def build(nc, t, upto=99):
    ctx = ExitStack()
    with ctx:
        pr = Program(nc, ctx)
        dram = {}

        def scratch(name, shape):
            dram[name] = nc.dram_tensor(name, shape, F32, kind=("ExternalOutput" if name in t.get("_show", ()) else "Internal"))
            return dram[name]

        uses = {}

        def sb(stack, name, shape, dt=F32, side=None):
            uses[name] = uses.get(name, 0) + 1
            n = name if uses[name] == 1 else f"{name}_{uses[name]}"
            return stack.enter_context(nc.sbuf_tensor(n, shape, dt, side=side))

        h1 = scratch("h1", [TOK, D])
        h2 = scratch("h2", [TOK, D])
        u_meta = scratch("u_meta", [META, W5])
        banks = [ctx.enter_context(nc.psum_tensor(f"bank{i}", [P, 2, W5], F32)) for i in range(4)]

        def bank(i):
            return banks[i // 2][:, i % 2, :]

        ident = sb(ctx, "ident", [P, P])
        cols = sb(ctx, "cols", [P, t["cols"].shape[1]])
        c_at = t["_cols"]

        def col(name, i=0, n=1):
            return cols[:, c_at[name] + i:c_at[name] + i + n]

        z0 = pr.pool("ident_zero", lambda e: e.memset(ident[:, :], 0.0))
        ident_ok = pr.pool("ident", lambda e: e.affine_select(
            out=ident[:, :], in_=ident[:, :], compare_op=ALU.not_equal, fill=1.0, base=0,
            pattern=[[-1, P]], channel_multiplier=1), z0)
        cols_ok = pr.load("cols_in", cols[:, :], t["cols"])
        env = dict(pr=pr, sb=sb, scratch=scratch, dram=dram, bank=bank, banks=banks, ident=ident,
                   col=col, t=t, ident_ok=ident_ok, cols_ok=cols_ok, h1=h1, h2=h2, u_meta=u_meta,
                   nc=nc, ctx=ctx)
        block1_mixers(env, upto)
        if upto >= 4:
            feed_forward(env)
        if upto >= 5:
            project(env)
        if upto >= 6:
            band_attention(env)
        if upto >= 7:
            gated_linear_attention(env)
        if upto >= 8:
            output_block(env)


def rstd_from_sums(pr, tag, out, tmp, scale, eps, *waits):
    a = pr.dve(f"{tag}_ms", lambda e: e.tensor_scalar(tmp, tmp, scale, eps, ALU.mult, ALU.add), *waits)
    b = pr.act(f"{tag}_root", lambda e: e.activation(tmp, tmp, ACT.Sqrt), a)
    return pr.dve(f"{tag}_rstd", lambda e: e.reciprocal(out, tmp), b)


def block1_mixers(env, upto):
    sb, nc = env["sb"], env["nc"]
    with ExitStack() as right:
        with ExitStack() as left:
            rs = sb(left, "rs_mix", [P, 2, NT])
            with ExitStack() as keep_v:
                vT = sb(keep_v, "vT", [P, NWIN, META + TOK])
                with ExitStack() as keep_u:
                    u_grp = sb(keep_u, "u_grp", [P, 2, G, CH, H])
                    input_projection(env, u_grp, vT)
                    if upto < 2:
                        return
                    g_tok = ssm(env, right, u_grp)
                    if upto < 3:
                        return
                pool_pair = pool_mixer(env, right, vT, rs)
            ssm_pair = ssm_gate(env, right, g_tok, rs)
            w_out_stage(env, rs, ssm_pair, pool_pair)


def input_projection(env, u_grp, vT):
    pr, sb, t, bank, ident, col = (env[k] for k in ("pr", "sb", "t", "bank", "ident", "col"))
    ident_ok, cols_ok = env["ident_ok"], env["cols_ok"]
    NX = 3
    with ExitStack() as st:
        w_hi = sb(st, "win_hi", [P, KT, D], F32R)
        w_lo = sb(st, "win_lo", [P, KT, D], F32R)
        w_st = sb(st, "win_stage", [P, 2, D])
        xr = sb(st, "x_ring", [P, NX, D])
        xT_hi = sb(st, "xT_hi", [P, 2, KT, P], F32R)
        xT_lo = sb(st, "xT_lo", [P, 2, KT, P], F32R)
        v_tok = sb(st, "v_tok", [P, 2, W5])
        um = sb(st, "um", [P, W5])
        junk = sb(st, "sq_junk", [P, D])
        ss = sb(st, "ss", [P, NT + 1])
        rs = sb(st, "rs", [P, NT + 1])

        xv = t["x"][0].rearrange("(b p s) d -> b s p d", b=2, s=CH)
        meta_zero = pr.dve("meta_zero", lambda e: e.memset(xr[:, 0, :], 0.0))
        split = []

        def split_w(k):
            i = k % 2
            ld = pr.load(f"win_in{i}", w_st[:, i, :], t["w_in"][0, k * P:(k + 1) * P, :],
                         split[k - 2] if k >= 2 else None)
            hi = pr.act("win_hi", lambda e: e.activation(
                w_hi[:, k, :], w_st[:, i, :], ACT.Copy, scale=col("g1", k)), ld, cols_ok)
            split.append(pr.dve("win_lo", lambda e: e.scalar_tensor_tensor(
                w_lo[:, k, :], w_st[:, i, :], col("g1", k), w_hi[:, k, :].bitcast(F32),
                ALU.mult, ALU.subtract), hi, ld, cols_ok))

        tiles = [-1] + list(range(NT))
        loaded, slot_free, rs_ok = {}, {}, {}
        turned, xT_free, xT_ok = [None, None], [None, None], {}
        uv_free, v_ok, v_free, vt_free = [None, None], {}, [None, None], [None, None]

        def fetch(n):
            i, r = n % NX, tiles[n]
            if r < 0:
                loaded[n] = pr.load(f"x_in{i}", xr[0:META, i, :], t["meta_tokens"], meta_zero)
            else:
                loaded[n] = pr.load(f"x_in{i}", xr[:, i, :], xv[r // CH, r % CH], slot_free.get(i))

        def turn(n):
            i, x2 = n % NX, n % 2
            ready = [loaded[n], meta_zero]
            sq = pr.act("x_sq", lambda e: e.activation(
                junk[:, :], xr[:, i, :], ACT.Square, accum_out=ss[:, n:n + 1]), ready)
            oks = []
            for g in range(2):
                tr = pr.pe("x_turn", turns(bank(g), [xr[:, i, k * P:(k + 1) * P]
                                                     for k in range(4 * g, 4 * g + 4)], ident),
                           ready, ident_ok, turned[g])
                src = bank(g).rearrange("p (j c) -> p j c", j=4)
                turned[g] = split_pair(pr, "xT", xT_hi[:, x2, 4 * g:4 * g + 4, :],
                                       xT_lo[:, x2, 4 * g:4 * g + 4, :], src, tr, xT_free[x2])
                oks.append(turned[g])
            slot_free[i] = [sq, tr]
            xT_ok[n] = oks
            rs_ok[n] = sq

        def roots(ns):
            a, b = ns[0], ns[-1] + 1
            ok = rstd_from_sums(pr, "n1", rs[:, a:b], ss[:, a:b], 1.0 / D, EPS, rs_ok[ns[-1]])
            for n in ns:
                rs_ok[n] = ok

        def multiply(n):
            x2, r = n % 2, tiles[n]
            outs = [bank(2 + 2 * x2), bank(3 + 2 * x2)]
            done = []
            for part in range(2):
                cs = slice(part * W5, (part + 1) * W5)
                done.append(pr.pe("win_mm", contraction(
                    outs[part], [(xT_hi[:, x2, k, :], xT_lo[:, x2, k, :]) for k in range(KT)],
                    [(w_hi[:, k, cs], w_lo[:, k, cs]) for k in range(KT)]),
                    xT_ok[n], split, uv_free[x2]))
            xT_free[x2] = done[1]
            scale = rs[:, n:n + 1]
            dst, src = um[:, :], outs[0]
            if r >= 0:
                dst = u_grp[:, r // CH, :, r % CH, :]
                src = src.rearrange("p (g h) -> p g h", h=H)
            u = pr.act("u_out", lambda e: e.activation(dst, src, ACT.Copy, scale=scale),
                       done[0], rs_ok[n])
            if r < 0:
                env["u_meta_ok"] = pr.load("u_meta_st", env["u_meta"][:, :], um[0:META, :], u,
                                           q="pool")
            v_ok[n] = pr.dve("v_out", lambda e: e.tensor_scalar(
                v_tok[:, x2, :], outs[1], scale, None, ALU.mult), done[1], rs_ok[n], v_free[x2])
            uv_free[x2] = [u, v_ok[n]]

        def turn_v(n):
            x2, r = n % 2, tiles[n]
            tb = bank(6 + x2)
            vt = pr.pe("v_turn", turns(tb, [v_tok[:, x2, j * P:(j + 1) * P] for j in range(NWIN)],
                                       ident), v_ok[n], vt_free[x2])
            src = tb.rearrange("p (j c) -> p j c", j=NWIN)
            if r < 0:
                dst, src = vT[:, :, 0:META], src[:, :, 0:META]
            else:
                lo = META + (r // CH) * HALF + r % CH
                dst = vT[:, :, lo:lo + CH * (P - 1) + 1:CH]
            v_free[x2] = vt
            vt_free[x2] = pr.dve("vT_out", lambda e: e.tensor_copy(dst, src), vt)

        n_all = len(tiles)
        fetch(0)
        fetch(1)
        for k in range(KT):
            split_w(k)
            if k == 2:
                turn(0)
                fetch(2)
        for n in range(1, n_all + 2):
            if n < n_all:
                turn(n)
                if n + 2 < n_all:
                    fetch(n + 2)
            if n == 1:
                roots([0, 1])
            elif n < n_all:
                roots([n])
            if 1 <= n <= n_all:
                multiply(n - 1)
            if n >= 2:
                turn_v(n - 2)
        pr.hold("sp", env["u_meta_ok"])
        pr.emit()


def ssm(env, right, u_grp):
    with ExitStack() as st:
        pr, sb = env["pr"], env["sb"]
        tab = dict(
            Vr=sb(st, "Vr", [P, NQ, (CH + 1) * H]), Vi=sb(st, "Vi", [P, NQ, (CH + 1) * H]),
            Er=sb(st, "Er", [P, NQ, P]), Ei=sb(st, "Ei", [P, NQ, P]),
            M=sb(st, "M_intra", [P, G, P]),
            Tc=sb(st, "Tc", [P, NQ, NCH]), Ts=sb(st, "Ts", [P, NQ, NCH]),
            rho=sb(st, "rho", [P, NQ]))
        ssm_tables(env, tab)
        g_tok = sb(right, "g_tok", [P, 2, CH, W5], F32, "right")
        ssm_run(env, tab, u_grp, g_tok)
    return g_tok


def ssm_tables(env, tab):
    pr, sb, t, bank, ident, col = (env[k] for k in ("pr", "sb", "t", "bank", "ident", "col"))
    with ExitStack() as st:
        W = [sb(st, f"W{c}", [P, NQ, CH, H]) for c in "ri"]
        tmp = sb(st, "tab_tmp", [P, 4, NQ * P])
        B = [sb(st, f"B{c}", [P, NQ, H]) for c in "ri"]
        bb = [sb(st, f"Bbar{c}", [P, NQ, H]) for c in "ri"]
        sm = sb(st, "tab_small", [P, 24, NQ])
        d_sb = sb(st, "d_sb", [H, G])
        dd = sb(st, "d_diag", [H, G, H])
        s_ = [sm[:, i, :] for i in range(24)]
        (step, mag, ang, c1, sn, ar, ai, nai, nr, den, cr, ci, t1, t2, t3, t4, rd, r1, r2, kq, lr,
         wr, wi, _) = s_
        Vr, Vi = (tab[k][:, :, :].rearrange("p q (j h) -> p q j h", h=H) for k in ("Vr", "Vi"))
        in_ok = [pr.load("B_in", B[0][:, :, :], t["B_re"]), pr.load("B_in", B[1][:, :, :], t["B_im"]),
                 pr.load("B_in", Vr[:, :, 0, :], t["C_re"]), pr.load("B_in", Vi[:, :, 0, :], t["C_im"]),
                 pr.load("B_in", d_sb[:, :], t["d"])]
        chain = [None]

        def v(fn, *waits):
            chain[0] = pr.dve("tables", fn, chain[0], *waits)

        def a(fn, *waits):
            chain[0] = pr.act("tables_act", fn, chain[0], *waits)

        def tt(o, x, y, op, *waits):
            v(lambda e: e.tensor_tensor(o, x, y, op), *waits)

        def ts(o, x, k1, k2, op1, op2, *waits):
            v(lambda e: e.tensor_scalar(o, x, k1, k2, op1, op2), *waits)

        def stt(o, x, k, y, op1, op2):
            v(lambda e: e.scalar_tensor_tensor(o, x, k, y, op1, op2))

        def complex_product(outr, outi, xr, xi, yr, yi, tmps):
            p1, p2, p3, p4 = tmps
            tt(p1, xr, yr, ALU.mult)
            tt(p2, xi, yi, ALU.mult)
            tt(p3, xr, yi, ALU.mult)
            tt(p4, xi, yr, ALU.mult)
            tt(outr, p1, p2, ALU.subtract)
            tt(outi, p3, p4, ALU.add)

        def reduced_sin(out, shift):
            ts(kq, ang, shift, 1 / (2 * math.pi), ALU.add, ALU.mult)
            ts(kq, kq, ROUND, None, ALU.add, ALU.bypass)
            ts(kq, kq, ROUND, None, ALU.subtract, ALU.bypass)
            stt(r1, kq, -TWO_PI_HI, ang, ALU.mult, ALU.add)
            stt(r1, kq, -TWO_PI_LO, r1, ALU.mult, ALU.add)
            ts(r1, r1, shift, None, ALU.add, ALU.bypass)
            ts(r1, r1, PI_LOW, -PI_LOW, ALU.min, ALU.max)
            a(lambda e: e.activation(out, r1, ACT.Sin))

        ts(lr, col("lr", 0, NQ), -1e-4, None, ALU.min, ALU.bypass, env["cols_ok"])
        li = col("li", 0, NQ)
        a(lambda e: e.activation(step, col("log_step", 0, NQ), ACT.Exp))
        tt(t1, lr, step, ALU.mult)
        a(lambda e: e.activation(mag, t1, ACT.Exp))
        a(lambda e: e.activation(tab["rho"][:, :], t1, ACT.Exp, scale=float(CH)))
        tt(ang, li, step, ALU.mult)
        reduced_sin(sn, 0.0)
        reduced_sin(c1, math.pi / 2)
        tt(ar, mag, c1, ALU.mult)
        tt(ai, mag, sn, ALU.mult)
        ts(nai, ai, -1.0, None, ALU.mult, ALU.bypass)
        ts(nr, ar, -1.0, None, ALU.add, ALU.bypass)
        tt(den, lr, lr, ALU.mult)
        tt(t1, li, li, ALU.mult)
        tt(den, den, t1, ALU.add)
        v(lambda e: e.reciprocal(rd, den))
        tt(t1, nr, lr, ALU.mult)
        tt(t2, ai, li, ALU.mult)
        tt(t1, t1, t2, ALU.add)
        tt(cr, t1, rd, ALU.mult)
        tt(t1, ai, lr, ALU.mult)
        tt(t2, nr, li, ALU.mult)
        tt(t1, t1, t2, ALU.subtract)
        tt(ci, t1, rd, ALU.mult)

        def over(x, n):
            return spread(x, n)

        def tmps(n, k):
            return [tmp[:, i, 0:NQ * n].rearrange("p (q n) -> p q n", q=NQ) for i in range(4)]

        t16 = tmps(H, 4)
        pr_wait = in_ok
        tt(bb[0][:, :, :], B[0][:, :, :], over(cr, H), ALU.mult, pr_wait)
        complex_product(bb[0][:, :, :], bb[1][:, :, :], over(cr, H), over(ci, H),
                        B[0][:, :, :], B[1][:, :, :], t16)
        for c in range(2):
            v(lambda e, c=c: e.tensor_copy(W[c][:, :, CH - 1, :], bb[c][:, :, :]))
        for s in range(CH - 1, 0, -1):
            complex_product(W[0][:, :, s - 1, :], W[1][:, :, s - 1, :], over(ar, H), over(ai, H),
                            W[0][:, :, s, :], W[1][:, :, s, :], t16)
        w_ok = chain[0]
        ts(Vi[:, :, 0, :], Vi[:, :, 0, :], -1.0, None, ALU.mult, ALU.bypass)
        for j in range(CH):
            complex_product(Vr[:, :, j + 1, :], Vi[:, :, j + 1, :], over(ar, H), over(nai, H),
                            Vr[:, :, j, :], Vi[:, :, j, :], t16)
        v_ok = chain[0]
        free = [None] * 4
        n = 0
        e_ok = []
        for c, E in ((0, tab["Er"]), (1, tab["Ei"])):
            for q0 in range(0, NQ, 4):
                b = n % 4
                tr = pr.pe("E_turn", turns(bank(b), [W[c][:, q, :, :] for q in range(q0, q0 + 4)],
                                           ident), w_ok, env["ident_ok"], free[b])
                free[b] = pr.act("E_out", lambda e, E=E, q0=q0, b=b: e.activation(
                    E[:, q0:q0 + 4, :], bank(b).rearrange("p (j c) -> p j c", j=4), ACT.Copy), tr)
                n += 1
        e_ok = free[(n - 1) % 4]
        complex_product(wr, wi, c1, sn, c1, sn, (t1, t2, t3, t4))
        complex_product(wr, wi, wr, wi, wr, wi, (t1, t2, t3, t4))
        complex_product(wr, wi, wr, wi, wr, wi, (t1, t2, t3, t4))
        Tc, Ts = tab["Tc"], tab["Ts"]
        v(lambda e: e.memset(Tc[:, :, 0], 1.0))
        v(lambda e: e.memset(Ts[:, :, 0], 0.0))
        v(lambda e: e.tensor_copy(Tc[:, :, 1], wr))
        v(lambda e: e.tensor_copy(Ts[:, :, 1], wi))
        n = 2
        while n < NCH:
            h = n // 2
            complex_product(Tc[:, :, n], Ts[:, :, n], Tc[:, :, h], Ts[:, :, h], Tc[:, :, h],
                            Ts[:, :, h], (t1, t2, t3, t4))
            m = min(n, NCH - n)
            complex_product(Tc[:, :, n + 1:n + m], Ts[:, :, n + 1:n + m], Tc[:, :, 1:m],
                            Ts[:, :, 1:m], over(Tc[:, :, n], m - 1), over(Ts[:, :, n], m - 1),
                            tmps(m - 1, 4))
            n *= 2
        K = tmp[:, 0:2, :].rearrange("p a (g n) -> p (a g) n", n=P)
        t_ok = chain[0]
        k_ok = []
        kfree = [None, None]
        for g0 in range(0, G, 8):
            b = 4 + 2 * ((g0 // 8) % 2)
            for side in range(2):
                fns = []
                rows = slice(PS * side, PS * (side + 1))
                for j in range(4):
                    o, q = bank(b + side)[0:H, j * P:(j + 1) * P], g0 // 2 + j
                    for c, V in ((0, tab["Vr"]), (1, tab["Vi"])):
                        fns.append(mm(o, bb[c][rows, q, :], V[rows, q, 0:P], c == 0, c == 1))
                done = pr.pe("K_mm", last_of(fns), v_ok, kfree[(g0 // 8) % 2])
                k_ok.append(pr.act("K_out", lambda e, b=b, g0=g0, side=side: e.activation(
                    K[0:H, g0 + side:g0 + 8:2, :],
                    bank(b + side)[0:H, :].rearrange("p (j c) -> p j c", j=4), ACT.Copy),
                    done, t_ok))
            kfree[(g0 // 8) % 2] = k_ok[-2:]
        k_all = list(k_ok)
        tt(dd[:, :, :], over(d_sb[:, :], H), bass.AP(
            tensor=ident[:, :].tensor, offset=ident[:, :].offset,
            ap=[list(ident[0:H, :].ap[0]), [0, G], [1, H]]), ALU.mult)
        tt(K[0:H, :, 0:H], K[0:H, :, 0:H], dd[:, :, :], ALU.add, k_all)
        k_ok = chain[0]
        m_zero = pr.pool("M_zero", lambda e: e.memset(tab["M"][:, :, :], 0.0))
        for s in range(CH):
            tab["M_ok"] = pr.load("M_in", tab["M"][H * s:H * (s + 1), :, H * s:P],
                                  K[0:H, :, 0:P - H * s], k_ok, m_zero, k_all)
        tab.update(ok=chain[0], e_ok=e_ok)
        pr.hold("sp", tab["M_ok"])
        pr.emit()


def ssm_run(env, tab, u_grp, g_tok):
    pr, sb, t, bank, ident = (env[k] for k in ("pr", "sb", "t", "bank", "ident"))
    with ExitStack() as st:
        um8 = sb(st, "um8", [P, MCH, G])
        U = sb(st, "U_ring", [P, 2, 2, NCH])
        z = sb(st, "z", [P, 4, NCH])
        R = sb(st, "R_ring", [P, 2, 2, NCH])
        S = sb(st, "S_ring", [P, 2, 2, NCH])
        zz = sb(st, "S_tmp", [P, 4, NCH])
        y = sb(st, "y_ring", [P, 2, 2, 2 * P])
        um = env["u_meta"]
        for c in range(MCH):
            for s in range(CH):
                um_ok = pr.load("um8_in", um8[H * s:H * (s + 1), c, :], bass.AP(
                    tensor=um[:, :].tensor, offset=(c * CH + s) * W5, ap=[[1, H], [H, G]]))
        NX1 = NCH - 1
        Ur, X_ok, U_ok, S_ok, y_ok, z_ok = {}, {}, {}, {}, {}, {}
        U_free, x_free, R_free, S_free = [None] * 2, [None] * 2, [None] * 2, [None] * 2
        y_free, ut_free, yb_free, yt_free = [None] * 2, [None] * 2, [None], [None]
        last = [None]

        def enter(q):
            i = q % 2
            ub = bank(0)
            tiles = [u_grp[:, b, g, :, :] for g in (2 * q, 2 * q + 1) for b in range(2)]
            tr = pr.pe("U_turn", turns(ub, tiles, ident), ut_free[0])
            c = pr.act("U_out", lambda e: e.activation(
                U[:, i, :, MCH:NCH], ub.rearrange("p (g c) -> p g c", g=2), ACT.Copy),
                tr, U_free[i])
            m = pr.dve("U_meta", lambda e: e.tensor_copy(
                U[:, i, :, 0:MCH], um8[:, :, 2 * q:2 * q + 2].rearrange("p c g -> p g c")), um_ok, U_free[i])
            ut_free[0] = c
            U_ok[q] = [c, m]
            Ur[q] = tr
            fns = []
            for r, E in ((0, tab["Er"]), (1, tab["Ei"])):
                for g in range(2):
                    fns.append(mm(bank(2 + 2 * i + r)[PS * g:PS * (g + 1), 0:NX1],
                                  E[:, q, PS * g:PS * (g + 1)], U[:, i, g, 0:NX1]))
            X_ok[q] = pr.pe("X_mm", last_of(fns), U_ok[q], x_free[i])

        def recur(q):
            i = q % 2
            xr, xi = bank(2 + 2 * i)[:, 0:NX1], bank(3 + 2 * i)[:, 0:NX1]
            c, s = tab["Tc"][:, q, 1:NCH], tab["Ts"][:, q, 1:NCH]
            z_ = [z[:, k, 0:NX1] for k in range(4)]

            def tt(o, a, b, op, *w):
                return pr.dve("turn_in", lambda e: e.tensor_tensor(o, a, b, op), *w)

            tt(z_[0], xr, c, ALU.mult, X_ok[q], tab["ok"])
            a2 = tt(z_[1], xi, s, ALU.mult)
            tt(z_[2], xi, c, ALU.mult)
            x_free[i] = a4 = tt(z_[3], xr, s, ALU.mult)
            tt(z_[0], z_[0], z_[1], ALU.add, a2)
            a6 = tt(z_[2], z_[2], z_[3], ALU.subtract, a4)
            rho = bass.AP(tensor=tab["rho"][:, :].tensor, offset=tab["rho"][:, q:q + 1].offset,
                          ap=[list(tab["rho"][:, q:q + 1].ap[0]), [0, NX1]])
            for k in range(2):
                r_ok = pr.dve("scan", lambda e, k=k: e.tensor_tensor_scan(
                    R[:, i, k, 0:NX1], rho, z_[2 * k], 0.0, ALU.mult, ALU.add), a6, R_free[i])
            c2, s2 = tab["Tc"][:, q, MCH:NCH], tab["Ts"][:, q, MCH:NCH]
            Rr, Ri = R[:, i, 0, 1:NX1], R[:, i, 1, 1:NX1]
            w = [zz[:, k, 0:NCH - MCH] for k in range(4)]

            def gt(o, a, b, op, *ws):
                last[0] = pr.pool("turn_back", lambda e: e.tensor_tensor(o, a, b, op), last[0], *ws)
                return last[0]

            gt(w[0], Rr, c2, ALU.mult, r_ok)
            g2 = gt(w[1], Ri, s2, ALU.mult)
            gt(w[2], Rr, s2, ALU.mult)
            R_free[i] = g4 = gt(w[3], Ri, c2, ALU.mult)
            gt(S[:, i, 0, 0:NCH - MCH], w[0], w[1], ALU.subtract, g2, S_free[i])
            S_ok[q] = gt(S[:, i, 1, 0:NCH - MCH], w[2], w[3], ALU.add, g4)

        def leave(q):
            i = q % 2
            n = NCH - MCH
            fns = []
            for g in range(2):
                o, rows = bank(6 + g)[:, 0:n], slice(PS * g, PS * (g + 1))
                fns.append(mm(o, tab["M"][:, 2 * q + g, :], U[:, i, g, MCH:NCH], True, False))
                fns.append(mm(o, tab["Vr"][rows, q, H:H + P], S[rows, i, 0, 0:n], False, False))
                fns.append(mm(o, tab["Vi"][rows, q, H:H + P], S[rows, i, 1, 0:n], False, True))
            done = pr.pe("y_mm", last_of(fns), S_ok[q], tab["M_ok"], U_ok[q], yb_free[0])
            U_free[i] = S_free[i] = done
            y_ok[q] = yb_free[0] = pr.act("gelu", lambda e: e.activation(
                y[:, i, :, :], env["banks"][3][:, :, 0:n], ACT.Gelu_apprx_tanh),
                done, y_free[i])

        def back(q):
            i = q % 2
            tb = bank(1)
            tr = pr.pe("y_turn", turns(tb, [y[:, i, g, b * P:(b + 1) * P] for g in range(2)
                                            for b in range(2)], ident), y_ok[q], yt_free[0])
            y_free[i] = tr
            src = tb.rearrange("p (g b s h) -> p g b s h", g=2, b=2, s=CH)
            for b in range(2):
                dst = g_tok[:, b, :, 2 * H * q:2 * H * (q + 1)].rearrange("p s (g h) -> p g s h", g=2)
                yt_free[0] = pr.act("y_out", lambda e, b=b, dst=dst: e.activation(
                    dst, src[:, :, b, :, :], ACT.Copy), tr)

        for q in range(NQ + 2):
            if q < NQ:
                enter(q)
                recur(q)
            if 1 <= q <= NQ:
                leave(q - 1)
            if q >= 2:
                back(q - 2)
        with env["nc"].allow_non_contiguous_dma(reason="the meta tokens' 8192 values"):
            pr.emit()


def finish_channels(env, tag, tmpsq, acc, y, hi, lo, first, *waits):
    pr = env["pr"]
    w = list(waits)
    s = split_pair(pr, tag, hi, lo, y, w)
    q = pr.act(f"{tag}_sq", lambda e: e.activation(acc if first else tmpsq, y, ACT.Square), w,
               env.get(f"{tag}_sq_free"))
    out = q
    if not first:
        out = pr.dve(f"{tag}_sum", lambda e: e.tensor_tensor(acc, acc, tmpsq, ALU.add), q,
                     env.get(f"{tag}_sum_ok"))
    env[f"{tag}_sum_ok"] = out
    env[f"{tag}_sq_free"] = out
    return [s, out, q]


def pool_mixer(env, keep, vT, rs):
    pr, sb, t, bank, col = (env[k] for k in ("pr", "sb", "t", "bank", "col"))
    hi = sb(keep, "pool_hi", [P, NWIN, TOK], F32R, "right")
    lo = sb(keep, "pool_lo", [P, NWIN, TOK], F32R, "right")
    L = META + TOK
    with ExitStack() as st:
        a = sb(st, "win_a", [P, L])
        b = sb(st, "win_b", [P, L])
        p = sb(st, "pooled", [P, TOK])
        y = sb(st, "yp", [P, TOK])
        sq = sb(st, "yp_sq", [P, TOK])
        acc = sb(st, "yp_acc", [P, TOK])
        pw = sb(st, "pool_w_sb", [P, NWIN, P])
        ones = sb(st, "ones_col", [P, 1])
        pw_ok = pr.load("pool_w_in", pw[:, :, :], t["pool_w"][0].rearrange("k c d -> c k d"))
        one_ok = pr.pool("ones_col", lambda e: e.memset(ones[:, :], 1.0))
        chain = None
        p_free, y_free = None, None
        bank_free = [None] * 4
        for k in range(NWIN):
            w = 2 << k
            cur, d, bufs = vT[:, k, :], 1, [a[:, :], b[:, :]]
            while d < w:
                nxt = bufs[0]
                bufs.reverse()
                s0 = 2 * d - 1
                chain = pr.dve("window", lambda e, nxt=nxt, cur=cur, s0=s0, d=d: e.tensor_tensor(
                    nxt[:, s0:L], cur[:, s0:L], cur[:, s0 - d:L - d], ALU.add), chain)
                cur, d = nxt, 2 * d
            chain = pr.dve("pooled", lambda e, cur=cur, k=k, w=w: e.scalar_tensor_tensor(
                p[:, :], cur[:, META:L], 1.0 / w, vT[:, k, META:L], ALU.mult, ALU.subtract),
                chain, p_free)
            evs = []
            for n in range(4):
                mmd = pr.pe("pool_mm", mm(bank(n), pw[:, k, :], p[:, n * W5:(n + 1) * W5]),
                            chain, pw_ok, bank_free[n])
                dst = y[:, :].rearrange("d (b s p) -> d b p s", b=2, s=CH)[
                    :, n // 2, 64 * (n % 2):64 * (n % 2) + 64, :]
                bank_free[n] = pr.act("yp_out", lambda e, n=n, dst=dst, k=k: e.activation(
                    dst, bank(n).rearrange("d (p s) -> d p s", s=CH), ACT.Copy,
                    scale=col("pscale", k)), mmd, y_free)
                evs.append(bank_free[n])
            p_free = mmd
            y_free = finish_channels(env, "yp", sq[:, :], acc[:, :], y[:, :], hi[:, k, :],
                                     lo[:, k, :], k == 0, evs)
        token_rstd(env, "pn", acc, ones, rs[:, 1, :], one_ok, env["yp_sum_ok"])
        pr.emit()
    return hi, lo


def token_rstd(env, tag, acc, ones, out, *waits):
    pr, bank = env["pr"], env["bank"]
    done = pr.pe(f"{tag}_sum", last_of([
        mm(bank(4)[:, r:r + 1], acc[:, r * P:(r + 1) * P], ones[:, :]) for r in range(NT)]), *waits)
    c = pr.dve(f"{tag}_ss", lambda e: e.tensor_copy(out, bank(4)[:, 0:NT]), done)
    return rstd_from_sums(pr, tag, out, out, 1.0 / W5, EPS, c)


def ssm_gate(env, keep, g_tok, rs):
    pr, sb, t, bank, ident, col = (env[k] for k in ("pr", "sb", "t", "bank", "ident", "col"))
    hi = sb(keep, "ssm_hi", [P, 4, TOK], F32R, "right")
    lo = sb(keep, "ssm_lo", [P, 4, TOK], F32R, "right")
    with ExitStack() as st:
        gT = sb(st, "gT", [P, 2, W5])
        sg = sb(st, "sg", [P, 2, W5])
        y = sb(st, "ys", [P, 2, W5])
        sq = sb(st, "ys_sq", [P, W5])
        acc = sb(st, "ys_acc", [P, TOK])
        gw = sb(st, "glu_w_sb", [P, 4, P])
        ones = sb(st, "ones_col2", [P, 1])
        gw_ok = pr.load("glu_w_in", gw[:, :, :], t["glu_w"])
        one_ok = pr.pool("ones_col2", lambda e: e.memset(ones[:, :], 1.0))
        turn_free, mm_free, g_free, s_free, y_free = ([None] * 2 for _ in range(5))
        n = 0
        for q in range(4):
            for m in range(4):
                i = n % 2
                n += 1
                rows = [4 * m + j for j in range(4)]
                tr = pr.pe("g_turn", turns(bank(i), [g_tok[:, r // CH, r % CH, q * P:(q + 1) * P]
                                                     for r in rows], ident), turn_free[i])
                turn_free[i] = pr.act("gT_out", lambda e, i=i: e.activation(
                    gT[:, i, :], bank(i), ACT.Copy), tr, g_free[i])
                gate = pr.pe("glu_mm", mm(bank(2 + i), gw[:, q, :], gT[:, i, :]), turn_free[i],
                             gw_ok, mm_free[i])
                mm_free[i] = pr.act("glu_sig", lambda e, i=i, q=q: e.activation(
                    sg[:, i, :], bank(2 + i), ACT.Sigmoid, bias=col("glub", q)), gate, s_free[i])
                yo = pr.dve("ys_out", lambda e, i=i: e.tensor_tensor(
                    y[:, i, :], gT[:, i, :], sg[:, i, :], ALU.mult), mm_free[i], y_free[i])
                g_free[i], s_free[i] = [yo, gate], yo
                cs = slice(m * W5, (m + 1) * W5)
                y_free[i] = finish_channels(env, "ys", sq[:, :], acc[:, cs], y[:, i, :],
                                            hi[:, q, cs], lo[:, q, cs], q == 0, yo)
        token_rstd(env, "sn", acc, ones, rs[:, 0, :], one_ok, env["ys_sum_ok"])
        pr.emit()
    return hi, lo


def w_out_stage(env, rs, ssm_pair, pool_pair):
    pr, sb, t, bank, col = (env[k] for k in ("pr", "sb", "t", "bank", "col"))
    NX = 4
    with ExitStack() as st:
        w_hi = sb(st, "wout_hi", [P, KT, W5], F32R)
        w_lo = sb(st, "wout_lo", [P, KT, W5], F32R)
        w_st = sb(st, "wout_stage", [P, 2, W5])
        xr = sb(st, "x_res", [P, NX, W5])
        xv = t["x"][0].rearrange("(b p s) d -> b s p d", b=2, s=CH)
        hv = env["h1"][:, :].rearrange("(b p s) d -> b s p d", b=2, s=CH)
        w_free, st_free = None, [None, None]
        x_free, b_free = [None] * NX, [None] * 2
        n = 0
        for half in range(2):
            cs = slice(half * W5, (half + 1) * W5)
            ok = []
            for k in range(KT):
                i = k % 2
                ld = pr.load(f"wout_in{i}", w_st[:, i, :], t["w_out"][0, k * P:(k + 1) * P, cs],
                             st_free[i])
                h_ = pr.act("wout_hi", lambda e, k=k, i=i: e.activation(
                    w_hi[:, k, :], w_st[:, i, :], ACT.Copy, scale=col("mixg", k)), ld, w_free)
                st_free[i] = pr.dve("wout_lo", lambda e, k=k, i=i: e.scalar_tensor_tensor(
                    w_lo[:, k, :], w_st[:, i, :], col("mixg", k), w_hi[:, k, :].bitcast(F32),
                    ALU.mult, ALU.subtract), h_, w_free)
                ok.append(st_free[i])
            for r in range(NT):
                i, x = n % 2, n % NX
                n += 1
                ts_ = slice(r * P, (r + 1) * P)
                ld = pr.load(f"x_res_in{x}", xr[:, x, :], xv[r // CH, r % CH][:, cs], x_free[x])
                outs = [bank(2 * i), bank(2 * i + 1)]
                done = []
                for part, (mh, ml) in enumerate((ssm_pair, pool_pair)):
                    done.append(pr.pe("wout_mm", contraction(
                        outs[part], [(mh[:, k, ts_], ml[:, k, ts_]) for k in range(4)],
                        [(w_hi[:, 4 * part + k, :], w_lo[:, 4 * part + k, :]) for k in range(4)]),
                        ok, b_free[i]))
                a = pr.dve("h1_ssm", lambda e, x=x, o=outs[0], r=r: e.scalar_tensor_tensor(
                    xr[:, x, :], o, rs[:, 0, r:r + 1], xr[:, x, :], ALU.mult, ALU.add), done[0], ld)
                b = pr.dve("h1_pool", lambda e, x=x, o=outs[1], r=r: e.scalar_tensor_tensor(
                    xr[:, x, :], o, rs[:, 1, r:r + 1], xr[:, x, :], ALU.mult, ALU.add), done[1], a)
                b_free[i] = b
                x_free[x] = pr.load(f"h1_st{x}", hv[r // CH, r % CH][:, cs], xr[:, x, :], b, q="act")
            w_free = done[1]
        pr.hold("sp", x_free)
        pr.emit()



def row_in(env, stack, name, width=D):
    buf = env["sb"](stack, f"row_{name}", [P, width])
    rows = env["t"]["rows"]
    src = bass.AP(tensor=rows.tensor, offset=rows.offset + ROWS[name], ap=[[0, P], [1, width]])
    return buf, env["pr"].load(f"row_{name}", buf[:, :], src)


def transposed_halves(env, tag, i, z, hi, lo, turned, banks2, *waits):
    pr, bank, ident = env["pr"], env["bank"], env["ident"]
    oks = []
    for g in range(2):
        b = banks2[g]
        tr = pr.pe(f"{tag}_turn", turns(bank(b), [z[:, k * P:(k + 1) * P]
                                                  for k in range(4 * g, 4 * g + 4)], ident),
                   turned.get(b), *waits)
        turned[b] = split_pair(pr, tag, hi[:, 4 * g:4 * g + 4, i * P:(i + 1) * P],
                               lo[:, 4 * g:4 * g + 4, i * P:(i + 1) * P],
                               bank(b).rearrange("p (j c) -> p j c", j=4), tr)
        oks.append(turned[b])
    return oks, tr


def feed_forward(env):
    pr, sb, t, bank, banks = (env[k] for k in ("pr", "sb", "t", "bank", "banks"))
    for half in range(2):
        with ExitStack() as st:
            acc = sb(st, f"ff_acc{half}", [P, HT, D])
            rows = slice(half * HALF, (half + 1) * HALF)
            h1v = env["h1"][rows, :].rearrange("(i p) d -> i p d", p=P)
            h2v = env["h2"][rows, :].rearrange("(i p) d -> i p d", p=P)
            with ExitStack() as st2:
                n_hi = sb(st2, f"n2_hi{half}", [P, KT, HALF], F32R)
                n_lo = sb(st2, f"n2_lo{half}", [P, KT, HALF], F32R)
                norm2(env, half, acc, h1v, n_hi, n_lo)
                ff_products(env, half, acc, n_hi, n_lo)
            leave_block1(env, half, acc, h2v)


def norm2(env, half, acc, h1v, n_hi, n_lo):
    pr, sb = env["pr"], env["sb"]
    with ExitStack() as st:
        g2, g2_ok = row_in(env, st, "g2")
        z = sb(st, "z2", [P, 2, D])
        ss = sb(st, "ss2", [P, HT])
        ld = [pr.load(f"h1_in{i}", acc[:, i, :], h1v[i]) for i in range(HT)]
        sq = None
        for i in range(HT):
            sq = pr.act("h1_sq", lambda e, i=i: e.activation(
                z[:, 1, :], acc[:, i, :], ACT.Square, accum_out=ss[:, i:i + 1]), ld[i], sq)
        r_ok = rstd_from_sums(pr, "n2", ss[:, :], ss[:, :], 1.0 / D, EPS, sq)
        turned, z_free = {}, [None, None]
        for i in range(HT):
            zi = z[:, i % 2, :]
            zo = pr.dve("z2", lambda e, i=i, zi=zi: e.scalar_tensor_tensor(
                zi, acc[:, i, :], ss[:, i:i + 1], g2[:, :], ALU.mult, ALU.mult),
                r_ok, g2_ok, z_free[i % 2])
            _, z_free[i % 2] = transposed_halves(env, "n2T", i, zi, n_hi, n_lo, turned,
                                                 (2 * (i % 2), 2 * (i % 2) + 1), zo)
        pr.emit()


def ff_products(env, half, acc, n_hi, n_lo):
    pr, sb, t, bank, banks = (env[k] for k in ("pr", "sb", "t", "bank", "banks"))
    with ExitStack() as st:
        wst = sb(st, "ff_stage", [P, 2, 3, D])
        w_hi = sb(st, "ffw_hi", [P, 2, 3, D], F32R)
        w_lo = sb(st, "ffw_lo", [P, 2, 3, D], F32R)
        f_hi = sb(st, "ff_hi", [P, 2, HALF], F32R)
        f_lo = sb(st, "ff_lo", [P, 2, HALF], F32R)
        sil = sb(st, "silu", [P, 2, W5])
        ff = sb(st, "ff", [P, 2, W5])
        gate = t["w_gate"][0].rearrange("(k p) f -> p k f", p=P)
        up = t["w_up"][0].rearrange("(k p) f -> p k f", p=P)
        w_ok, w_free, st_free = {}, [None, None], [None, None]
        f_ok, f_free = {}, [None, None]
        gu_free, sil_free, ff_free, d_free = [None] * 4, [None] * 2, [None] * 2, [None] * 2

        def weights(j):
            i = j % 2
            js = slice(j * P, (j + 1) * P)
            ld = [pr.load(f"ffw_in{i}", wst[:, i, m, :].rearrange("p (k f) -> p k f", f=P),
                          w[:, :, js], st_free[i]) for m, w in enumerate((gate, up))]
            ld.append(pr.load(f"ffw_in{i}", wst[:, i, 2, :], t["w_down"][0, js, :], st_free[i]))
            w_ok[j] = st_free[i] = split_pair(pr, "ffw", w_hi[:, i], w_lo[:, i], wst[:, i], ld,
                                              w_free[i])

        def gate_up(j):
            i = j % 2
            f_ok[j] = []
            for nh in range(2):
                cs = slice(nh * W5, (nh + 1) * W5)
                done = []
                for m in range(2):
                    done.append(pr.pe("gate_up_mm", contraction(
                        bank(2 * m + nh),
                        [(w_hi[:, i, m, k * P:(k + 1) * P], w_lo[:, i, m, k * P:(k + 1) * P])
                         for k in range(KT)],
                        [(n_hi[:, k, cs], n_lo[:, k, cs]) for k in range(KT)]),
                        w_ok[j], gu_free[2 * m + nh]))
                s = pr.act("silu", lambda e, nh=nh: e.activation(
                    sil[:, nh, :], bank(nh), ACT.Silu), done[0], sil_free[nh])
                gu_free[nh] = s
                f = pr.dve("ff", lambda e, nh=nh: e.tensor_tensor(
                    ff[:, nh, :], sil[:, nh, :], bank(2 + nh), ALU.mult), s, done[1], ff_free[nh])
                gu_free[2 + nh] = sil_free[nh] = f
                ff_free[nh] = split_pair(pr, "ff", f_hi[:, i, cs], f_lo[:, i, cs], ff[:, nh, :], f,
                                         f_free[i])
                f_ok[j].append(ff_free[nh])

        def down(j):
            i = j % 2
            for m in range(HT):
                d = m % 2
                rows = slice(m * P, (m + 1) * P)
                fns = [contraction(
                    bank(4 + 2 * d + nh), [(f_hi[:, i, rows], f_lo[:, i, rows])],
                    [(w_hi[:, i, 2, nh * W5:(nh + 1) * W5], w_lo[:, i, 2, nh * W5:(nh + 1) * W5])])
                    for nh in range(2)]
                done = pr.pe("down_mm", last_of(fns), f_ok[j], d_free[d])
                d_free[d] = pr.dve("ff_acc", lambda e, m=m, d=d: e.tensor_tensor(
                    acc[:, m, :].rearrange("p (a b) -> p a b", a=2),
                    acc[:, m, :].rearrange("p (a b) -> p a b", a=2), banks[2 + d][:, :, :],
                    ALU.add), done)
            w_free[i] = f_free[i] = done

        weights(0)
        weights(1)
        for j in range(NJ + 1):
            if j < NJ:
                gate_up(j)
            if j >= 1:
                down(j - 1)
                if j + 1 < NJ:
                    weights(j + 1)
        pr.emit()


def layer_norm_stats(pr, tag, x, st6, mv, *waits):
    for h in range(2):
        s = pr.dve(f"{tag}_st", lambda e, h=h: e.bn_stats(st6[:, 6 * h:6 * h + 6],
                                                         x[:, h * W5:(h + 1) * W5]), *waits)
    return pr.dve(f"{tag}_mv", lambda e: e.bn_aggr(mv, st6), s)


def leave_block1(env, half, acc, h2v):
    pr, sb = env["pr"], env["sb"]
    with ExitStack() as st:
        gf, gf_ok = row_in(env, st, "gf")
        lg, lg_ok = row_in(env, st, "lin_g")
        lb, lb_ok = row_in(env, st, "lin_b")
        junk = sb(st, "h_junk", [P, D])
        ss = sb(st, "ssf", [P, HT])
        st6 = sb(st, "st6", [P, HT, 12])
        mv = sb(st, "mv", [P, HT, 2])
        rl = sb(st, "rl", [P, HT])
        sq = None
        for i in range(HT):
            sq = pr.act("h_sq", lambda e, i=i: e.activation(
                junk[:, :], acc[:, i, :], ACT.Square, accum_out=ss[:, i:i + 1]), sq)
        r_ok = rstd_from_sums(pr, "nf", ss[:, :], ss[:, :], 1.0 / D, EPS, sq)
        for i in range(HT):
            a = pr.dve("x2", lambda e, i=i: e.scalar_tensor_tensor(
                acc[:, i, :], acc[:, i, :], ss[:, i:i + 1], gf[:, :], ALU.mult, ALU.mult),
                r_ok, gf_ok)
            mv_ok = layer_norm_stats(pr, "li", acc[:, i, :], st6[:, i, :], mv[:, i, :], a)
        l_ok = rstd_from_sums(pr, "lir", rl[:, :], mv[:, :, 1], 1.0, LN_EPS, mv_ok)
        for i in range(HT):
            a = pr.dve("h2_n", lambda e, i=i: e.tensor_scalar(
                acc[:, i, :], acc[:, i, :], mv[:, i, 0:1], rl[:, i:i + 1], ALU.subtract, ALU.mult),
                l_ok)
            g = pr.pool("h2_g", lambda e, i=i: e.tensor_tensor(
                acc[:, i, :], acc[:, i, :], lg[:, :], ALU.mult), a, lg_ok)
            b = pr.dve("h2_b", lambda e, i=i: e.tensor_tensor(
                acc[:, i, :], acc[:, i, :], lb[:, :], ALU.add), g, lb_ok)
            s = pr.load("h2_st", h2v[i], acc[:, i, :], b)
        pr.hold("sp", s)
        pr.emit()


BLOCKS = (("q", 0, W5, "T"), ("k", 512, W5, "T"), ("v", 1024, W5, "tok"), ("ag", 1536, W5, "tok"),
          ("gqk", 2048, W5, "T"), ("gv", 2560, W5, "tok"), ("gg", 3072, W5, "tok"),
          ("glr", 3584, 16, "T"))


def project(env):
    pr, sb, t, bank = (env[k] for k in ("pr", "sb", "t", "bank"))
    for name, _, w, kind in BLOCKS:
        env["p_" + name] = env["scratch"]("p_" + name, [w, TOK] if kind == "T" else [TOK, w])
    for half in range(2):
        with ExitStack() as st:
            hT_hi = sb(st, f"hT_hi{half}", [P, KT, HALF], F32R)
            hT_lo = sb(st, f"hT_lo{half}", [P, KT, HALF], F32R)
            hr = sb(st, "h2_ring", [P, 3, D])
            wst = sb(st, "pw_stage", [P, KT, W5])
            w_hi = sb(st, "pw_hi", [P, 2, KT, W5], F32R)
            w_lo = sb(st, "pw_lo", [P, 2, KT, W5], F32R)
            o_sb = sb(st, "p_ring", [P, 4, W5])
            wv = t["w_in_2"][0].rearrange("(k p) c -> p k c", p=P)
            turned, h_free, h_ok = {}, {}, []
            w_ok, w_free, st_free = {}, [None, None], [None]
            bank_free, o_free, cnt = {b: None for b in range(8)}, [None] * 4, [0]

            def weights(b):
                _, c0, w, _ = BLOCKS[b]
                i = b % 2
                oks = []
                for k in range(0, KT, 4):
                    ks = slice(k, k + 4)
                    ld = pr.load(f"pw_in{k}", wst[:, ks, 0:w], wv[:, ks, c0:c0 + w], st_free[0])
                    oks.append(split_pair(pr, "pw", w_hi[:, i, ks, 0:w], w_lo[:, i, ks, 0:w],
                                          wst[:, ks, 0:w], ld, w_free[i]))
                w_ok[b], st_free[0] = oks, oks

            def product(b, lhs, rhs, scale, func, dst, rows=P):
                n = cnt[0]
                cnt[0] += 1
                bk, o = n % 8, n % 4
                done = pr.pe("proj_mm", contraction(bank(bk), lhs, rhs), w_ok[b], h_ok, turned.get(bk),
                             bank_free[bk])
                ev = pr.act("proj_out", lambda e: e.activation(
                    o_sb[0:rows, o, :], bank(bk)[0:rows, :], func, scale=scale), done, o_free[o])
                bank_free[bk] = ev
                o_free[o] = pr.load(f"proj_st{o}", dst, o_sb[0:rows, o, :], ev, q="pool")
                return done

            def block(b):
                name, _, w, kind = BLOCKS[b]
                i, dst = b % 2, env["p_" + name]
                if kind == "T":
                    for c in range(max(1, w // P)):
                        cs = slice(c * P, (c + 1) * P)
                        scale = 0.125 if name == "q" or (name == "gqk" and c < 2) else 1.0
                        for nh in range(2):
                            ts_ = slice(nh * W5, (nh + 1) * W5)
                            n = min(w, P)
                            to = dst[c * P:c * P + n, half * HALF + nh * W5:half * HALF + (nh + 1) * W5]
                            done = product(
                                b, [(w_hi[:, i, k, cs], w_lo[:, i, k, cs]) for k in range(KT)],
                                [(hT_hi[:, k, ts_], hT_lo[:, k, ts_]) for k in range(KT)],
                                scale, ACT.Copy, to, n)
                else:
                    func = ACT.Silu if name in ("ag", "gg") else ACT.Copy
                    for m in range(HT):
                        ms = slice(m * P, (m + 1) * P)
                        to = dst[half * HALF + m * P:half * HALF + (m + 1) * P, :]
                        done = product(
                            b, [(hT_hi[:, k, ms], hT_lo[:, k, ms]) for k in range(KT)],
                            [(w_hi[:, i, k, :], w_lo[:, i, k, :]) for k in range(KT)],
                            1.0, func, to)
                w_free[i] = done

            for i in range(HT):
                x = i % 3
                r0 = half * HALF + i * P
                ld = pr.load(f"h2_in{x}", hr[:, x, :], env["h2"][r0:r0 + P, :], h_free.get(x))
                oks, h_free[x] = transposed_halves(env, "hT", i, hr[:, x, :], hT_hi, hT_lo, turned,
                                                   (2 * (i % 2), 2 * (i % 2) + 1), ld)
                h_ok += oks
                if i == 1:
                    weights(0)
            for b in range(len(BLOCKS)):
                if b + 1 < len(BLOCKS):
                    weights(b + 1)
                block(b)
            pr.hold("sp", o_free)
            pr.emit()


def band_attention(env):
    pr, sb, t, bank, banks, ident = (env[k] for k in ("pr", "sb", "t", "bank", "banks", "ident"))
    env["mix"] = mix = env["scratch"]("mix", [TOK, D])
    ext_d = env["scratch"]("ext", [NHEAD, EXT])
    skew = env["scratch"]("skew", [NHEAD, P, EXT])
    n_rel = 2 * CLIP + 1
    with ExitStack() as st:
        bias = sb(st, "bias", [P, NHEAD, BAND_W])
        rel = sb(st, "rel", [NHEAD, n_rel])
        ext = sb(st, "ext_sb", [NHEAD, EXT])
        qT = sb(st, "qT", [P, 2, TOK])
        kT = sb(st, "kT", [P, 2, TOK])
        v = sb(st, "v_sb", [P, 2, NT, P])
        ag = sb(st, "ag_sb", [P, 2, NT, P])
        S = sb(st, "S_sb", [P, 3, BAND_W])
        E = sb(st, "E_sb", [P, 3, BAND_W])
        ET = sb(st, "ET_sb", [P, 2, BAND_W])
        o = sb(st, "att_sb", [P, 2, NT, P])
        mx = sb(st, "mx", [P, 4, 4])

        r_ok = pr.load("rel_in", rel[:, :], t["rel_bias_2"][0])
        flat_n = EXT - n_rel
        a_ = rel[:, :]
        e1 = pr.dve("ext", lambda e: e.tensor_copy(ext[:, 0:flat_n], bass.AP(
            tensor=a_.tensor, offset=a_.offset + n_rel - 1, ap=[list(a_.ap[0]), [0, flat_n]])), r_ok)
        e2 = pr.dve("ext", lambda e: e.tensor_copy(ext[:, flat_n:EXT], bass.AP(
            tensor=a_.tensor, offset=a_.offset + n_rel - 1, ap=[list(a_.ap[0]), [-1, n_rel]])), e1)
        s1 = pr.load("ext_st", ext_d[:, :], ext[:, :], e2)
        s2 = pr.load("skew_st", skew[:, :, :], bass.AP(
            tensor=ext_d[:, :].tensor, offset=0, ap=[[EXT, NHEAD], [0, P], [1, EXT]]), s1)
        b_in = pr.load("bias_in", bias[:, :, :], bass.AP(
            tensor=skew[:, :, :].tensor, offset=P - 1,
            ap=[[EXT - 1, P], [P * EXT, NHEAD], [1, BAND_W]]), s2)
        b1 = pr.dve("bias_end", lambda e: e.memset(bias[0:64, :, BAND_W - 64:BAND_W], NEG), b_in)
        bias_ok = pr.dve("bias_end", lambda e: e.memset(bias[64:P, :, 0:64], NEG), b1)

        pair_ok, pair_free, o_free = {}, [None] * 2, [None] * 2
        s_ok, s_free, e_ok, S_free, E_free = {}, [None] * 2, {}, [None] * 3, [None] * 3
        et_free, ETs_free, et_ok, pv_free = [None], [None] * 2, {}, [None] * 2
        r_done = {}
        units = [(hp, qt, hh) for hp in range(NHEAD // 2) for qt in range(NT) for hh in range(2)]

        def load_pair(hp):
            i = hp % 2
            cs = slice(hp * P, (hp + 1) * P)
            w = pair_free[i]
            n = f"{i}"
            pair_ok[hp] = [
                pr.load("qT_in" + n, qT[:, i, :], env["p_q"][cs, :], w),
                pr.load("kT_in" + n, kT[:, i, :], env["p_k"][cs, :], w),
                pr.load("v_in" + n, v[:, i, :, :],
                        env["p_v"][:, cs].rearrange("(m p) c -> p m c", p=P), w),
                pr.load("ag_in" + n, ag[:, i, :, :],
                        env["p_ag"][:, cs].rearrange("(m p) c -> p m c", p=P), w)]

        def geometry(u):
            hp, qt, hh = units[u]
            nk = min(qt + 1, BAND_T)
            return hp, qt, hh, nk, qt + 1 - nk, slice(64 * hh, 64 * hh + 64)

        def scores(u):
            hp, qt, hh, nk, k0, rows = geometry(u)
            i, W = hp % 2, nk * P
            pb = banks[u % 2]
            fns = [mm(pb[:, c // W5, 0:min(W - c, W5)], qT[rows, i, qt * P:(qt + 1) * P],
                      kT[rows, i, k0 * P + c:k0 * P + min(c + W5, W)]) for c in range(0, W, W5)]
            done = pr.pe("score_mm", last_of(fns), pair_ok[hp], s_free[u % 2])
            x = u % 3
            flatp = pb[:, :, :].rearrange("p a b -> p (a b)")[:, 0:W]
            a = pr.dve("score_max", lambda e: e.tensor_tensor_reduce(
                S[:, x, 0:W], flatp, bias[:, 2 * hp + hh, BAND_W - W:BAND_W], 1.0, -3e38,
                ALU.add, ALU.max, mx[:, u % 4, 0:1]), done, bias_ok, S_free[x], E_free[x])
            s_free[u % 2] = a
            b = pr.dve("neg_max", lambda e: e.tensor_scalar(
                mx[:, u % 4, 1:2], mx[:, u % 4, 0:1], -1.0, None, ALU.mult), a)
            e_ok[u] = S_free[x] = pr.act("exp", lambda e: e.activation(
                E[:, x, 0:W], S[:, x, 0:W], ACT.Exp, bias=mx[:, u % 4, 1:2],
                accum_out=mx[:, u % 4, 2:3]), a, b, E_free[x])
            r_done[u] = pr.dve("sum_recip", lambda e: e.reciprocal(mx[:, u % 4, 3:4], mx[:, u % 4, 2:3]),
                               e_ok[u])

        def turn_e(u):
            hp, qt, hh, nk, k0, rows = geometry(u)
            x, y, W = u % 3, u % 2, nk * P
            pb = banks[2]
            tr = pr.pe("E_turn2", last_of([
                (lambda e, j=j: e.transpose(pb[:, j // 4, (j % 4) * P:(j % 4 + 1) * P],
                                            E[:, x, j * P:(j + 1) * P], ident[:, :]))
                for j in range(nk)]), e_ok[u], et_free[0])
            src = pb[:, :, :].rearrange("p a b -> p (a b)")[:, 0:W]
            if u % 3:
                et_ok[u] = pr.act("ET_act", lambda e: e.activation(ET[:, y, 0:W], src, ACT.Copy),
                                  tr, ETs_free[y])
            else:
                et_ok[u] = pr.dve("ET_dve", lambda e: e.tensor_copy(ET[:, y, 0:W], src),
                                  tr, ETs_free[y])
            et_free[0] = et_ok[u]
            E_free[x] = tr

        def values(u):
            hp, qt, hh, nk, k0, rows = geometry(u)
            i, x, y = hp % 2, u % 3, u % 2
            pb = bank(6 + y)
            done = pr.pe("pv_mm", last_of([
                mm(pb[:, 0:64], ET[:, y, j * P:(j + 1) * P], v[:, i, k0 + j, rows], j == 0,
                   j == nk - 1) for j in range(nk)]), et_ok[u], pv_free[y])
            ETs_free[y] = done
            f = pr.dve("att_out", lambda e: e.scalar_tensor_tensor(
                o[:, i, qt, rows], pb[:, 0:64], mx[:, u % 4, 3:4], ag[:, i, qt, rows],
                ALU.mult, ALU.mult), done, r_done[u], o_free[i])
            pv_free[y] = f
            if qt == NT - 1 and hh == 1:
                pair_free[i] = [done, f]
                o_free[i] = pr.load(f"att_st{i}", mix[:, hp * P:(hp + 1) * P].rearrange(
                    "(m p) c -> p m c", p=P), o[:, i, :, :], f)
                if hp + 2 < NHEAD // 2:
                    load_pair(hp + 2)

        load_pair(0)
        load_pair(1)
        n = len(units)
        for u in range(n + 3):
            if u < n:
                scores(u)
            if 2 <= u < n + 2:
                turn_e(u - 2)
            if u >= 3:
                values(u - 3)
        pr.hold("sp", o_free)
        pr.emit()


def gated_linear_attention(env):
    pr, sb, t, bank, banks, ident, col = (env[k] for k in (
        "pr", "sb", "t", "bank", "banks", "ident", "col"))
    C = 64
    NC = TOK // C
    mix = env["mix"]
    for hp in range(2):
        with ExitStack() as st:
            q = sb(st, "gq", [P, TOK])
            k = sb(st, "gk", [P, TOK])
            L = sb(st, "gL", [P, TOK])
            eL = sb(st, "eL", [P, TOK])
            eN = sb(st, "eN", [P, TOK])
            qf = sb(st, "q_fwd", [P, TOK])
            tmp = sb(st, "g_tmp", [P, TOK])
            reset = sb(st, "reset", [P, TOK])
            lend = sb(st, "lend", [P, NC])
            dec = sb(st, "dec", [P, NC])
            v = sb(st, "gv_sb", [P, NT, 2 * P])
            gate = sb(st, "gg_sb", [P, NT, 2 * P])
            raw = sb(st, "o_raw", [P, NT, 2 * P])
            lr_ = sb(st, "glr_sb", [16, TOK])
            gw = sb(st, "w_gg", [16, P])
            mask = sb(st, "tri", [P, C])
            att = sb(st, "g_att", [P, 2, 2, C])
            kdT = sb(st, "kdT", [P, 2, P])
            state = sb(st, "g_state", [P, 4, P])
            ssq = sb(st, "g_ss", [P, NT, 2])
            junk = sb(st, "g_junk", [P, 2, P])
            gn = sb(st, "g_gain", [P, 2 * P])
            cs = slice(hp * P, (hp + 1) * P)
            vs = slice(hp * 2 * P, (hp + 1) * 2 * P)
            q_in = pr.load("gq_in", q[:, :], env["p_gqk"][cs, :])
            k_in = pr.load("gk_in", k[:, :], env["p_gqk"][2 * P + hp * P:2 * P + (hp + 1) * P, :])
            l_in = [pr.load("glr_in", lr_[:, :], env["p_glr"][:, :]),
                    pr.load("wgg_in", gw[:, :], t["w_gla_gate_2"][0][:, cs])]
            v_in = pr.load("gv_in", v[:, :, :], env["p_gv"][:, vs].rearrange("(m p) c -> p m c", p=P))
            g_in = pr.load("gg_in", gate[:, :, :],
                           env["p_gg"][:, vs].rearrange("(m p) c -> p m c", p=P))
            rows = t["rows"]
            n_in = pr.load("ggain_in", gn[:, :], bass.AP(
                tensor=rows.tensor, offset=rows.offset + ROWS["gla_g"] + hp * 2 * P,
                ap=[[0, P], [1, 2 * P]]))
            m1 = pr.pool("g_const", lambda e: e.memset(reset[:, :], 1.0))
            m2 = pr.pool("g_const", lambda e: e.memset(reset[:, 0:TOK:C], 0.0), m1)
            m3 = pr.pool("g_const", lambda e: e.memset(mask[:, :], 1.0), m2)
            for c in range(2):
                m3 = pr.pool("g_const", lambda e, c=c: e.affine_select(
                    out=mask[C * c:C * (c + 1), :], in_=mask[C * c:C * (c + 1), :],
                    compare_op=ALU.is_ge, fill=0.0, base=0, pattern=[[1, C]],
                    channel_multiplier=-1), m3)
            const_ok = m3
            lg = []
            for n in range(4):
                ns = slice(n * W5, (n + 1) * W5)
                d = pr.pe("glogit_mm", mm(bank(n), gw[:, :], lr_[:, ns]), l_in)
                lg.append(pr.act("glogit", lambda e, n=n, ns=ns: e.activation(
                    L[:, ns], bank(n), ACT.Identity, bias=col("bgate", hp)), d))
            a = pr.act("g_abs", lambda e: e.activation(tmp[:, :], L[:, :], ACT.Abs), lg)
            a = pr.act("g_exp", lambda e: e.activation(tmp[:, :], tmp[:, :], ACT.Exp, scale=-1.0), a)
            a = pr.act("g_ln", lambda e: e.activation(tmp[:, :], tmp[:, :], ACT.Ln, bias=1.0), a)
            b = pr.dve("g_logsig", lambda e: e.scalar_tensor_tensor(
                tmp[:, :], L[:, :], 0.0, tmp[:, :], ALU.min, ALU.subtract), a, lg)
            b = pr.dve("g_cumsum", lambda e: e.tensor_tensor_scan(
                L[:, :], reset[:, :], tmp[:, :], 0.0, ALU.mult, ALU.add), b, const_ok)
            sc = 1.0 / 16.0
            x1 = pr.act("g_eL", lambda e: e.activation(eL[:, :], L[:, :], ACT.Exp, scale=sc), b)
            x2 = pr.act("g_eN", lambda e: e.activation(eN[:, :], L[:, :], ACT.Exp, scale=-sc), b)
            b = pr.dve("g_lend", lambda e: e.tensor_copy(lend[:, :], L[:, C - 1:TOK:C]), b)
            x3 = pr.act("g_dec", lambda e: e.activation(dec[:, :], lend[:, :], ACT.Exp, scale=sc), b)
            b = pr.dve("g_left", lambda e: e.tensor_tensor(
                tmp[:, :].rearrange("p (n c) -> p n c", c=C), spread(lend[:, :], C),
                L[:, :].rearrange("p (n c) -> p n c", c=C), ALU.subtract), b)
            x4 = pr.act("g_kdecay", lambda e: e.activation(tmp[:, :], tmp[:, :], ACT.Exp, scale=sc), b)

            def mul(o, x, y, *w):
                return pr.dve("g_mul", lambda e: e.tensor_tensor(o, x, y, ALU.mult), *w)

            kd_ok = mul(tmp[:, :], tmp[:, :], k[:, :], x4, k_in)
            qf_ok = mul(qf[:, :], q[:, :], eL[:, :], x1, q_in)
            ka = mul(eL[:, :], k[:, :], eL[:, :], x1, k_in, qf_ok)
            qn = mul(q[:, :], q[:, :], eN[:, :], x2, qf_ok)
            kn = mul(eN[:, :], k[:, :], eN[:, :], x2, qn)
            gg = const_ok
            for hh in range(2):
                s_ = slice(hh * P, (hh + 1) * P)
                g_ = bass.AP(tensor=gn[:, :].tensor, offset=gn[:, s_].offset,
                             ap=[list(gn[:, s_].ap[0]), [0, NT], [1, P]])
                gg = pr.pool("g_gate", lambda e, s_=s_, g_=g_: e.tensor_tensor(
                    gate[:, :, s_], gate[:, :, s_], g_, ALU.mult), g_in, n_in, gg)
            s0 = pr.dve("g_state", lambda e: e.memset(state[:, 0, :], 0.0))

            att_ok, att_free, kd_free, kdT_ok = {}, [None] * 2, [None] * 2, {}
            a_free, kv_free, o_free, kt_free = [None], [None] * 2, [None] * 2, [None]
            state_ok, state_free = {0: s0}, [None] * 4
            kd_ = tmp
            sq_last = [None, None]

            def inner(m):
                y = m % 2
                done = []
                for hh in range(2):
                    r = slice(C * hh, C * (hh + 1))
                    fns = []
                    for c in range(2):
                        ts_ = slice(m * P + C * c, m * P + C * (c + 1))
                        for w, (l_, r_) in enumerate(((eN, qf), (eL, q))):
                            fns.append(mm(bank(hh)[C * c:C * (c + 1), w * C:(w + 1) * C],
                                          l_[r, ts_], r_[r, ts_]))
                    done.append(pr.pe("g_att_mm", last_of(fns), kn, a_free[0]))
                oks = []
                for hh in range(2):
                    a1 = pr.act("g_anti", lambda e, hh=hh: e.activation(
                        att[:, y, hh, :], bank(hh)[:, C:2 * C], ACT.Copy), done[hh], att_free[y])
                    oks.append(pr.dve("g_causal", lambda e, hh=hh: e.copy_predicated(
                        att[:, y, hh, :], mask[:, :].bitcast(U32), bank(hh)[:, 0:C]),
                        a1, done[hh], const_ok))
                a_free[0] = oks
                att_ok[m] = oks
                tr = pr.pe("kd_turn", turns(bank(2), [kd_[:, m * P:(m + 1) * P]], ident), kd_ok,
                           kt_free[0])
                kdT_ok[m] = kt_free[0] = pr.act("kdT_out", lambda e: e.activation(
                    kdT[:, y, :], bank(2)[:, 0:P], ACT.Copy), tr, kd_free[y])

            def carry(m):
                y = m % 2
                for c in range(2):
                    n = 2 * m + c
                    if n == NC - 1:
                        continue
                    r = slice(C * c, C * (c + 1))
                    kb = bank(3 + c)
                    done = pr.pe("kv_mm", last_of([
                        mm(kb[C * hh:C * (hh + 1), 0:P], kdT[r, y, C * hh:C * (hh + 1)],
                           v[r, m, hh * P:(hh + 1) * P]) for hh in range(2)]),
                        kdT_ok[m], v_in, kv_free[c])
                    kd_free[y] = done
                    state_ok[n + 1] = kv_free[c] = pr.dve("g_state", lambda e, n=n, kb=kb:
                        e.scalar_tensor_tensor(
                            state[:, (n + 1) % 4, :], state[:, n % 4, :], dec[:, n:n + 1],
                            kb[:, 0:P], ALU.mult, ALU.add),
                        done, x3, state_ok[n], state_free[(n + 1) % 4])

            def outer(m):
                y = m % 2
                for hh in range(2):
                    r = slice(C * hh, C * (hh + 1))
                    for c in range(2):
                        n = 2 * m + c
                        rc = slice(C * c, C * (c + 1))
                        ts_ = slice(m * P + C * c, m * P + C * (c + 1))
                        ob = bank(6 + c)[rc, hh * P:(hh + 1) * P]
                        a1 = pr.pe("g_o_mm", mm(ob, att[rc, y, hh, :], v[rc, m, hh * P:(hh + 1) * P],
                                                True, False), att_ok[m], v_in, o_free[0])
                        o_done = pr.pe("g_o_mm", mm(ob, qf[r, ts_], state[r, n % 4, :], False, True),
                                       a1, state_ok[n], qf_ok)
                        state_free[n % 4] = o_done
                att_free[y] = o_done
                ev = []
                for c in range(2):
                    rc = slice(C * c, C * (c + 1))
                    ev.append(pr.dve("g_raw", lambda e, c=c, rc=rc: e.tensor_copy(
                        raw[rc, m, :], bank(6 + c)[rc, 0:2 * P]), o_done))
                for hh in range(2):
                    sq = pr.act("g_sq", lambda e, hh=hh: e.activation(
                        junk[:, hh, :], raw[:, m, hh * P:(hh + 1) * P], ACT.Square,
                        accum_out=ssq[:, m, hh:hh + 1]), ev, sq_last[hh])
                    sq_last[hh] = sq
                o_free[0] = ev
                return sq

            for m in range(NT + 1):
                if m < NT:
                    inner(m)
                if m >= 1:
                    carry(m - 1)
                    sq = outer(m - 1)
            r_ok = rstd_from_sums(pr, "g_n", ssq[:, :, :], ssq[:, :, :], 1.0 / P, EPS, sq)
            for m in range(NT):
                for hh in range(2):
                    s_ = slice(hh * P, (hh + 1) * P)
                    f = pr.dve("g_final", lambda e, m=m, hh=hh, s_=s_: e.scalar_tensor_tensor(
                        raw[:, m, s_], raw[:, m, s_], ssq[:, m, hh:hh + 1], gate[:, m, s_],
                        ALU.mult, ALU.mult), r_ok, gg)
            stt_ = pr.load("gla_st", mix[:, W5 + hp * 2 * P:W5 + (hp + 1) * 2 * P].rearrange(
                "(m p) c -> p m c", p=P), raw[:, :, :], f)
            pr.hold("sp", stt_)
            pr.emit()


def output_block(env):
    for half in range(2):
        output_half(env, half)


def weight_columns(env, tag, w_dram, n_k, w_st, w_hi, w_lo, n, st_free, w_free):
    pr = env["pr"]
    oks = []
    for k in range(0, n_k, 2):
        i = (k // 2) % 2
        ld = pr.load(f"{tag}_in{i}", w_st[:, i, :, :],
                     w_dram.rearrange("(k p) c -> p k c", p=P)[:, k:k + 2, n * W5:(n + 1) * W5],
                     st_free[i])
        st_free[i] = split_pair(pr, tag, w_hi[:, k:k + 2, :], w_lo[:, k:k + 2, :], w_st[:, i, :, :],
                                ld, w_free)
        oks.append(st_free[i])
    return oks


def output_half(env, half):
    pr, sb, t, bank, banks = (env[k] for k in ("pr", "sb", "t", "bank", "banks"))
    KP = 2
    t0 = half * HALF
    with ExitStack() as st:
        r = sb(st, "r", [P, HT, D])
        x_hi = sb(st, "mT_hi", [P, KT, HALF], F32R)
        x_lo = sb(st, "mT_lo", [P, KT, HALF], F32R)
        p_hi = sb(st, "pT_hi", [P, KP, HALF], F32R)
        p_lo = sb(st, "pT_lo", [P, KP, HALF], F32R)
        w_hi = sb(st, "ow_hi", [P, KT, W5], F32R)
        w_lo = sb(st, "ow_lo", [P, KT, W5], F32R)
        pw_hi = sb(st, "oq_hi", [P, KP, W5], F32R)
        pw_lo = sb(st, "oq_lo", [P, KP, W5], F32R)
        w_st = sb(st, "ow_stage", [P, 2, 2, W5])
        ring = sb(st, "o_ring", [P, 2, D])
        bp, bp_ok = row_in(env, st, "b_ple")
        g = sb(st, "ple_g", [P, 2, W5])
        st6 = sb(st, "st6o", [P, HT, 12])
        mv = sb(st, "mvo", [P, HT, 2])
        rl = sb(st, "rlo", [P, HT])
        turned, free = {}, [None, None]
        m_ok = []
        r_ld = pr.load("r_in", r[:, :, :], env["h2"][t0:t0 + HALF, :].rearrange("(m p) d -> p m d", p=P))
        for i in range(HT):
            x = i % 2
            ld = pr.load(f"mix_in{x}", ring[:, x, :], env["mix"][t0 + i * P:t0 + (i + 1) * P, :], free[x])
            oks, free[x] = transposed_halves(env, "mT", i, ring[:, x, :], x_hi, x_lo, turned,
                                             (2 * x, 2 * x + 1), ld, env["ident_ok"])
            m_ok += oks
        p_ok = []
        for i in range(HT):
            x = i % 2
            ld = pr.load(f"mix_in{x}", ring[:, x, 0:2 * P], t["p_2"][0, 0, t0 + i * P:t0 + (i + 1) * P, :],
                         free[x])
            b = 4 + x
            tr = pr.pe("pT_turn", turns(bank(b), [ring[:, x, k * P:(k + 1) * P] for k in range(KP)],
                                        env["ident"]), ld, turned.get(b))
            free[x] = tr
            turned[b] = split_pair(pr, "pT", p_hi[:, :, i * P:(i + 1) * P], p_lo[:, :, i * P:(i + 1) * P],
                                   bank(b)[:, 0:KP * P].rearrange("p (j c) -> p j c", j=KP), tr)
            p_ok.append(turned[b])
        st_free, w_free = [None, None], None
        b_free = {b: turned.get(b) for b in range(8)}
        r_ok = {}
        n_b = 0
        for n in range(2):
            cs = slice(n * W5, (n + 1) * W5)
            w_ok = weight_columns(env, "ow", t["w_out_2"][0], KT, w_st, w_hi, w_lo, n, st_free, w_free)
            for m in range(HT):
                ms = slice(m * P, (m + 1) * P)
                b = 6 + n_b % 2
                n_b += 1
                w_free = done = pr.pe("wo2_mm", contraction(
                    bank(b), [(x_hi[:, k, ms], x_lo[:, k, ms]) for k in range(KT)],
                    [(w_hi[:, k, :], w_lo[:, k, :]) for k in range(KT)]), w_ok, m_ok, b_free[b])
                b_free[b] = r_ok[(m, n)] = pr.dve("r_mix", lambda e, m=m, cs=cs, b=b:
                    e.scalar_tensor_tensor(r[:, m, cs], r[:, m, cs], ALPHA, bank(b), ALU.mult,
                                           ALU.add), done, r_ld)
        rt_ok = []
        for i in range(HT):
            x = i % 2
            oks, _ = transposed_halves(env, "rT", i, r[:, i, :], x_hi, x_lo, turned,
                                       (2 * x, 2 * x + 1), r_ok[(i, 0)], r_ok[(i, 1)], w_free)
            rt_ok += oks
        pw_free, g_free = None, [None, None]
        fin = {}
        for n in range(2):
            cs = slice(n * W5, (n + 1) * W5)
            q_ok = weight_columns(env, "oq", t["w_ple_2"][0], KP, w_st, pw_hi, pw_lo, n, st_free, pw_free)
            w_ok = weight_columns(env, "ow", t["w_ple_gate_2"][0], KT, w_st, w_hi, w_lo, n, st_free,
                                  w_free)
            for m in range(HT):
                x = m % 2
                ms = slice(m * P, (m + 1) * P)
                b1, b2 = 4 + x, 6 + x
                pd = pr.pe("ple_mm", contraction(
                    bank(b2), [(p_hi[:, k, ms], p_lo[:, k, ms]) for k in range(KP)],
                    [(pw_hi[:, k, :], pw_lo[:, k, :]) for k in range(KP)]), q_ok, p_ok, b_free[b2])
                gd = pr.pe("gate_mm", contraction(
                    bank(b1), [(x_hi[:, k, ms], x_lo[:, k, ms]) for k in range(KT)],
                    [(w_hi[:, k, :], w_lo[:, k, :]) for k in range(KT)]), w_ok, rt_ok, b_free[b1],
                    turned.get(b1))
                w_free, pw_free = gd, pd
                a = pr.dve("gate_b", lambda e, x=x, b1=b1, cs=cs: e.tensor_tensor(
                    g[:, x, :], bank(b1), bp[:, cs], ALU.add), gd, bp_ok, g_free[x])
                b_free[b1] = a
                s = pr.act("gate_sig", lambda e, x=x: e.activation(g[:, x, :], g[:, x, :],
                                                                   ACT.Sigmoid), a)
                c = pr.dve("gate_p", lambda e, x=x, b2=b2: e.tensor_tensor(
                    g[:, x, :], g[:, x, :], bank(b2), ALU.mult), s, pd)
                b_free[b2] = c
                fin[(m, n)] = g_free[x] = pr.dve("r_gate", lambda e, x=x, m=m, cs=cs: e.tensor_tensor(
                    r[:, m, cs], r[:, m, cs], g[:, x, :], ALU.add), c, rt_ok)
        rows = t["rows"]
        gl, bl = ring[:, 0, :], ring[:, 1, :]
        gb = [pr.load("ln_rows", dst, bass.AP(tensor=rows.tensor, offset=rows.offset + ROWS[nm],
                                              ap=[[0, P], [1, D]]), free)
              for nm, dst in (("ln_g", gl), ("ln_b", bl))]
        for m in range(HT):
            mv_ok = layer_norm_stats(pr, "lo", r[:, m, :], st6[:, m, :], mv[:, m, :], fin[(m, 0)],
                                     fin[(m, 1)])
        l_ok = rstd_from_sums(pr, "lor", rl[:, :], mv[:, :, 1], 1.0, LN_EPS, mv_ok)
        for m in range(HT):
            a = pr.dve("o_n", lambda e, m=m: e.tensor_scalar(
                r[:, m, :], r[:, m, :], mv[:, m, 0:1], rl[:, m:m + 1], ALU.subtract, ALU.mult), l_ok)
            c = pr.pool("o_g", lambda e, m=m: e.tensor_tensor(r[:, m, :], r[:, m, :], gl, ALU.mult),
                        a, gb)
            d = pr.dve("o_b", lambda e, m=m: e.tensor_tensor(r[:, m, :], r[:, m, :], bl, ALU.add), c)
            s = pr.load("out_st", t["out"][0, t0 + m * P:t0 + (m + 1) * P, :], r[:, m, :], d)
        pr.hold("sp", s)
        pr.emit()


def columns(a):
    return np.ascontiguousarray(a.reshape(-1, P).T)


def laid_out(inp):
    f = {k: np.asarray(v) for k, v in inp.items()}
    pairs = {"g1": f["norm1_g"], "mixg": np.concatenate([f["ssm_norm_g"], f["pool_norm_g"]], -1),
             "pscale": f["pool_scale"], "glub": f["ssm_glu_b"], "bgate": f["b_gla_gate_2"],
             "lr": f["ssm_lambda_re"], "li": f["ssm_lambda_im"],
             "log_step": np.repeat(f["ssm_log_step"], PS)}
    at, parts, n = {}, [], 0
    for name, a in pairs.items():
        c = columns(a)
        at[name] = n
        n += c.shape[1]
        parts.append(c)
    out = {"cols": np.concatenate(parts, 1)}

    def per_pair(a):
        return a.reshape(NQ, P, H).transpose(1, 0, 2)

    out["B_re"], out["B_im"] = per_pair(f["ssm_b_re"][0]), per_pair(f["ssm_b_im"][0])
    out["C_re"] = per_pair(f["ssm_c_re"][0].transpose(0, 2, 1))
    out["C_im"] = per_pair(f["ssm_c_im"][0].transpose(0, 2, 1))
    out["d"] = f["ssm_d"][0].T
    glu = np.zeros((P, 4, P), f["ssm_glu_w"].dtype)
    for g in range(G):
        q, r = g // 8, H * (g % 8)
        glu[r:r + H, q, r:r + H] = f["ssm_glu_w"][0, g]
    out["glu_w"] = glu
    out["rows"] = np.concatenate([f[k].reshape(-1) for k in (
        "norm2_g", "final_norm_g", "ln_in_g_2", "ln_in_b_2", "b_ple_gate_2", "ln_g_2", "ln_b_2",
        "gla_norm_g_2")])
    for k in ("x", "meta_tokens", "w_in", "pool_w", "w_out", "w_gate", "w_up", "w_down", "p_2",
              "w_in_2", "w_gla_gate_2", "rel_bias_2", "w_out_2", "w_ple_2", "w_ple_gate_2"):
        out[k] = f[k]
    return {k: np.ascontiguousarray(v) for k, v in out.items()}, at


ROWS = {n: i * D for i, n in enumerate(("g2", "gf", "lin_g", "lin_b", "b_ple", "ln_g", "ln_b",
                                        "gla_g"))}


def kernel(**inputs):
    import concourse.bacc as bacc
    from concourse.bass_utils import run_bass_kernel_spmd

    nc = bacc.Bacc("TRN2", target_bir_lowering=False, num_devices=1)
    arrays, at = laid_out(inputs)
    t = {"_cols": at, "_show": ()}
    for name, a in arrays.items():
        t[name] = nc.dram_tensor(f"in_{name}", a.shape, F32, kind="ExternalInput").ap()
    t["out"] = nc.dram_tensor("out", (1, TOK, D), F32, kind="ExternalOutput").ap()
    build(nc, t)
    r = run_bass_kernel_spmd(nc, [{f"in_{k}": v for k, v in arrays.items()}], core_ids=[0])
    return r.results[0]["out"]
```

```python
import math
from contextlib import ExitStack

import numpy as np

import concourse.bass as bass
from concourse import mybir

F32 = mybir.dt.float32
F32R = mybir.dt.float32r
U32 = mybir.dt.uint32
ALU = mybir.AluOpType
ACT = mybir.ActivationFunctionType
AX = mybir.AxisListType

P = 128
D = 1024
KT = D // P
TOK = 2048
META = 16
NT = TOK // P
CH = 8
NCH = (TOK + META) // CH
MCH = META // CH
G, H, PS = 32, 16, 64
NQ = G // 2
W5 = 512
DFF = 2816
NJ = DFF // P
HALF = TOK // 2
HT = HALF // P
NWIN = 4
EPS = 1e-6
LN_EPS = 1e-5
BAND_T = 5
BAND_W = BAND_T * P
NHEAD = 8
AD = 64
CLIP = 128
EXT = 768
ALPHA = 2.0 ** 0.25
NEG = -1e30
TWO_PI_HI = 6.28125
TWO_PI_LO = 2 * math.pi - TWO_PI_HI
ROUND = 1.5 * 2.0 ** 23
PI_LOW = 3.1415925


def flat(waits):
    for w in waits:
        if isinstance(w, list):
            yield from flat(w)
        elif w is not None:
            yield w


class Program:

    def __init__(self, nc, ctx):
        self.nc, self.ctx = nc, ctx
        self.sems, self.count, self.waited = [], [], {}
        self.idle = {}
        self.fresh()

    def fresh(self):
        self.queue = {e: [] for e in ("pe", "act", "dve", "pool", "sp")}
        self.at = {}

    def _sem(self, engine, name, by):
        kind = (engine, by)
        if name in self.at:
            assert self.at[name][1] == kind, name
            return self.at[name][0]
        if self.idle.get(kind):
            n = self.idle[kind].pop(0)
        else:
            n = len(self.sems)
            self.sems.append(self.ctx.enter_context(self.nc.semaphore(
                f"{engine}_{'dma' if by == 16 else 'step'}{n}")))
            self.count.append(0)
        self.at[name] = (n, kind)
        return n

    def step(self, engine, name, run, waits, by=1):
        n = self._sem(engine, name, by)
        self.queue[engine].append((self.needed(engine, waits), run, self.sems[n], by))
        self.count[n] += by
        return (n, self.count[n])

    def needed(self, engine, waits):
        top = {}
        for n, value in flat(waits):
            top[n] = max(value, top.get(n, 0))
        need = [(n, v) for n, v in top.items() if v > self.waited.get((engine, n), 0)]
        for n, v in need:
            self.waited[(engine, n)] = v
        return [(self.sems[n], v) for n, v in need]

    def hold(self, engine, *waits):
        self.queue[engine].append((self.needed(engine, waits), None, None, 0))

    def pe(self, name, run, *waits):
        return self.step("pe", name, run, waits)

    def act(self, name, run, *waits):
        return self.step("act", name, run, waits)

    def dve(self, name, run, *waits):
        return self.step("dve", name, run, waits)

    def pool(self, name, run, *waits):
        return self.step("pool", name, run, waits)

    def load(self, name, out, in_, *waits, q="sp"):
        return self.step(q, name, lambda e: e.dma_start(out, in_), waits, 16)

    def emit(self):
        queue = self.queue

        def play(items):
            def body(eng):
                for need, run, sem, by in items:
                    for s, v in need:
                        eng.wait_ge(s, v)
                    if run is not None:
                        run(eng).then_inc(sem, by)
            return body

        with self.nc.Block() as block:
            block.sync(play(queue["sp"]))
            block.gpsimd(play(queue["pool"]))
            block.scalar(play(queue["act"]))
            block.vector(play(queue["dve"]))
            block.tensor(play(queue["pe"]))
        for n, kind in self.at.values():
            self.idle.setdefault(kind, []).append(n)
        self.fresh()


def products(e, out, lhs, rhs, first, last):
    e.matmul(out, lhs[1], rhs[0], start=first, stop=False)
    e.matmul(out, lhs[0], rhs[1], start=False, stop=False)
    return e.matmul(out, lhs[0], rhs[0], start=False, stop=last)


def contraction(out, lhs, rhs):
    def run(e):
        n = len(lhs)
        for k in range(n):
            ins = products(e, out, lhs[k], rhs[k], k == 0, k == n - 1)
        return ins
    return run


def turns(out, tiles, ident):
    def run(e):
        for j, tile in enumerate(tiles):
            ins = e.transpose(out[:, j * P:(j + 1) * P], tile, ident[:, :])
        return ins
    return run


def split_pair(pr, tag, hi, lo, src, *waits):
    a = pr.act(f"{tag}_hi", lambda e: e.activation(hi, src, ACT.Copy), *waits)
    return pr.dve(f"{tag}_lo", lambda e: e.tensor_tensor(lo, src, hi.bitcast(F32), ALU.subtract),
                  a, *waits)


def spread(ap, n):
    return bass.AP(tensor=ap.tensor, offset=ap.offset, ap=[list(x) for x in ap.ap] + [[0, n]])


def last_of(fns):
    def run(e):
        for f in fns:
            ins = f(e)
        return ins
    return run


def mm(out, l, r, first=True, last=True):
    return lambda e: e.matmul(out, l, r, start=first, stop=last)


def over_partitions(ap, width):
    return bass.AP(tensor=ap.tensor, offset=ap.offset, ap=[[0, P], [1, width]])


def build(nc, t, upto=99):
    ctx = ExitStack()
    with ctx:
        pr = Program(nc, ctx)
        dram = {}

        def scratch(name, shape):
            dram[name] = nc.dram_tensor(name, shape, F32, kind=("ExternalOutput" if name in t.get("_show", ()) else "Internal"))
            return dram[name]

        uses = {}

        def sb(stack, name, shape, dt=F32, side=None):
            uses[name] = uses.get(name, 0) + 1
            n = name if uses[name] == 1 else f"{name}_{uses[name]}"
            return stack.enter_context(nc.sbuf_tensor(n, shape, dt, side=side))

        rs2 = sb(ctx, "rs2", [P, NT])
        h1 = scratch("h1", [TOK, D])
        h2 = scratch("h2", [TOK, D])
        u_meta = scratch("u_meta", [META, W5])
        banks = [ctx.enter_context(nc.psum_tensor(f"bank{i}", [P, 2, W5], F32)) for i in range(4)]

        def bank(i):
            return banks[i // 2][:, i % 2, :]

        ident = sb(ctx, "ident", [P, P])
        cols = sb(ctx, "cols", [P, t["cols"].shape[1]])
        c_at = t["_cols"]

        def col(name, i=0, n=1):
            return cols[:, c_at[name] + i:c_at[name] + i + n]

        z0 = pr.pool("ident_zero", lambda e: e.memset(ident[:, :], 0.0))
        ident_ok = pr.pool("ident", lambda e: e.affine_select(
            out=ident[:, :], in_=ident[:, :], compare_op=ALU.not_equal, fill=1.0, base=0,
            pattern=[[-1, P]], channel_multiplier=1), z0)
        cols_ok = pr.load("cols_in", cols[:, :], t["cols"])
        env = dict(pr=pr, sb=sb, scratch=scratch, dram=dram, bank=bank, banks=banks, ident=ident,
                   col=col, t=t, ident_ok=ident_ok, cols_ok=cols_ok, h1=h1, h2=h2, u_meta=u_meta,
                   nc=nc, ctx=ctx, rs2=rs2)
        block1_mixers(env, upto)
        if upto >= 4:
            feed_forward(env)
        if upto >= 6:
            band_attention(env)
        out_w = [sb(ctx, f"ow_{n}", [P, KT, D], F32R, "right") for n in ("hi", "lo")]
        gated_linear_attention(env, out_w)
        output_block(env, out_w)


def rstd_from_sums(pr, tag, out, tmp, scale, eps, *waits):
    a = pr.dve(f"{tag}_ms", lambda e: e.tensor_scalar(tmp, tmp, scale, eps, ALU.mult, ALU.add), *waits)
    b = pr.act(f"{tag}_root", lambda e: e.activation(tmp, tmp, ACT.Sqrt), a)
    return pr.dve(f"{tag}_rstd", lambda e: e.reciprocal(out, tmp), b)


def block1_mixers(env, upto):
    sb, nc = env["sb"], env["nc"]
    with ExitStack() as right:
        with ExitStack() as left:
            rs = sb(left, "rs_mix", [P, 2, NT])
            with ExitStack() as keep_v:
                vT = sb(keep_v, "vT", [P, NWIN, META + TOK])
                with ExitStack() as keep_u:
                    u_grp = sb(keep_u, "u_grp", [P, 2, G, CH, H])
                    input_projection(env, u_grp, vT)
                    if upto < 2:
                        return
                    g_tok = ssm(env, right, u_grp)
                    if upto < 3:
                        return
                pool_pair = pool_mixer(env, right, vT, rs)
            ssm_pair = ssm_gate(env, right, g_tok, rs)
            w_out_stage(env, rs, ssm_pair, pool_pair)


def input_projection(env, u_grp, vT):
    pr, sb, t, bank, ident, col = (env[k] for k in ("pr", "sb", "t", "bank", "ident", "col"))
    ident_ok, cols_ok = env["ident_ok"], env["cols_ok"]
    NX = 3
    with ExitStack() as st:
        w_hi = sb(st, "win_hi", [P, KT, D], F32R)
        w_lo = sb(st, "win_lo", [P, KT, D], F32R)
        w_st = sb(st, "win_stage", [P, 2, D])
        xr = sb(st, "x_ring", [P, NX, D])
        xT_hi = sb(st, "xT_hi", [P, 2, KT, P], F32R)
        xT_lo = sb(st, "xT_lo", [P, 2, KT, P], F32R)
        v_tok = sb(st, "v_tok", [P, 2, W5])
        um = sb(st, "um", [P, W5])
        junk = sb(st, "sq_junk", [P, D])
        ss = sb(st, "ss", [P, NT + 1])
        rs = sb(st, "rs", [P, NT + 1])

        xv = t["x"][0].rearrange("(b p s) d -> b s p d", b=2, s=CH)
        meta_zero = pr.dve("meta_zero", lambda e: e.memset(xr[:, 0, :], 0.0))
        split = []

        def split_w(k):
            i = k % 2
            ld = pr.load(f"win_in{i}", w_st[:, i, :], t["w_in"][0, k * P:(k + 1) * P, :],
                         split[k - 2] if k >= 2 else None)
            hi = pr.act("win_hi", lambda e: e.activation(
                w_hi[:, k, :], w_st[:, i, :], ACT.Copy, scale=col("g1", k)), ld, cols_ok)
            split.append(pr.dve("win_lo", lambda e: e.scalar_tensor_tensor(
                w_lo[:, k, :], w_st[:, i, :], col("g1", k), w_hi[:, k, :].bitcast(F32),
                ALU.mult, ALU.subtract), hi, ld, cols_ok))

        tiles = [-1] + list(range(NT))
        loaded, slot_free, rs_ok = {}, {}, {}
        turned, xT_free, xT_ok = [None, None], [None, None], {}
        uv_free, v_ok, v_free, vt_free = [None, None], {}, [None, None], [None, None]

        def fetch(n):
            i, r = n % NX, tiles[n]
            if r < 0:
                loaded[n] = pr.load(f"x_in{i}", xr[0:META, i, :], t["meta_tokens"], meta_zero)
            else:
                loaded[n] = pr.load(f"x_in{i}", xr[:, i, :], xv[r // CH, r % CH], slot_free.get(i))

        def turn(n):
            i, x2 = n % NX, n % 2
            ready = [loaded[n], meta_zero]
            sq = pr.act("x_sq", lambda e: e.activation(
                junk[:, :], xr[:, i, :], ACT.Square, accum_out=ss[:, n:n + 1]), ready)
            oks = []
            for g in range(2):
                tr = pr.pe("x_turn", turns(bank(g), [xr[:, i, k * P:(k + 1) * P]
                                                     for k in range(4 * g, 4 * g + 4)], ident),
                           ready, ident_ok, turned[g])
                src = bank(g).rearrange("p (j c) -> p j c", j=4)
                turned[g] = split_pair(pr, "xT", xT_hi[:, x2, 4 * g:4 * g + 4, :],
                                       xT_lo[:, x2, 4 * g:4 * g + 4, :], src, tr, xT_free[x2])
                oks.append(turned[g])
            slot_free[i] = [sq, tr]
            xT_ok[n] = oks
            rs_ok[n] = sq

        def roots(ns):
            a, b = ns[0], ns[-1] + 1
            ok = rstd_from_sums(pr, "n1", rs[:, a:b], ss[:, a:b], 1.0 / D, EPS, rs_ok[ns[-1]])
            for n in ns:
                rs_ok[n] = ok

        def multiply(n):
            x2, r = n % 2, tiles[n]
            outs = [bank(2 + 2 * x2), bank(3 + 2 * x2)]
            done = []
            for part in range(2):
                cs = slice(part * W5, (part + 1) * W5)
                done.append(pr.pe("win_mm", contraction(
                    outs[part], [(xT_hi[:, x2, k, :], xT_lo[:, x2, k, :]) for k in range(KT)],
                    [(w_hi[:, k, cs], w_lo[:, k, cs]) for k in range(KT)]),
                    xT_ok[n], split, uv_free[x2]))
            xT_free[x2] = done[1]
            scale = rs[:, n:n + 1]
            dst, src = um[:, :], outs[0]
            if r >= 0:
                dst = u_grp[:, r // CH, :, r % CH, :]
                src = src.rearrange("p (g h) -> p g h", h=H)
            u = pr.act("u_out", lambda e: e.activation(dst, src, ACT.Copy, scale=scale),
                       done[0], rs_ok[n])
            if r < 0:
                env["u_meta_ok"] = pr.load("u_meta_st", env["u_meta"][:, :], um[0:META, :], u,
                                           q="pool")
            v_ok[n] = pr.dve("v_out", lambda e: e.tensor_scalar(
                v_tok[:, x2, :], outs[1], scale, None, ALU.mult), done[1], rs_ok[n], v_free[x2])
            uv_free[x2] = [u, v_ok[n]]

        def turn_v(n):
            x2, r = n % 2, tiles[n]
            tb = bank(6 + x2)
            vt = pr.pe("v_turn", turns(tb, [v_tok[:, x2, j * P:(j + 1) * P] for j in range(NWIN)],
                                       ident), v_ok[n], vt_free[x2])
            src = tb.rearrange("p (j c) -> p j c", j=NWIN)
            if r < 0:
                dst, src = vT[:, :, 0:META], src[:, :, 0:META]
            else:
                lo = META + (r // CH) * HALF + r % CH
                dst = vT[:, :, lo:lo + CH * (P - 1) + 1:CH]
            v_free[x2] = vt
            vt_free[x2] = pr.dve("vT_out", lambda e: e.tensor_copy(dst, src), vt)

        n_all = len(tiles)
        fetch(0)
        fetch(1)
        for k in range(KT):
            split_w(k)
            if k == 2:
                turn(0)
                fetch(2)
        for n in range(1, n_all + 2):
            if n < n_all:
                turn(n)
                if n + 2 < n_all:
                    fetch(n + 2)
            if n == 1:
                roots([0, 1])
            elif n < n_all:
                roots([n])
            if 1 <= n <= n_all:
                multiply(n - 1)
            if n >= 2:
                turn_v(n - 2)
        pr.hold("sp", env["u_meta_ok"])
        pr.emit()


def ssm(env, right, u_grp):
    with ExitStack() as st:
        pr, sb = env["pr"], env["sb"]
        tab = dict(
            Vr=sb(st, "Vr", [P, NQ, (CH + 1) * H]), Vi=sb(st, "Vi", [P, NQ, (CH + 1) * H]),
            Er=sb(st, "Er", [P, NQ, P]), Ei=sb(st, "Ei", [P, NQ, P]),
            M=sb(st, "M_intra", [P, G, P]),
            Tc=sb(st, "Tc", [P, NQ, NCH]), Ts=sb(st, "Ts", [P, NQ, NCH]),
            rho=sb(st, "rho", [P, NQ]))
        ssm_tables(env, tab)
        g_tok = sb(right, "g_tok", [P, 2, CH, W5], F32, "right")
        ssm_run(env, tab, u_grp, g_tok)
    return g_tok


def ssm_tables(env, tab):
    pr, sb, t, bank, ident, col = (env[k] for k in ("pr", "sb", "t", "bank", "ident", "col"))
    with ExitStack() as st:
        W = [sb(st, f"W{c}", [P, NQ, CH, H]) for c in "ri"]
        tmp = sb(st, "tab_tmp", [P, 4, NQ * P])
        B = [sb(st, f"B{c}", [P, NQ, H]) for c in "ri"]
        bb = [sb(st, f"Bbar{c}", [P, NQ, H]) for c in "ri"]
        sm = sb(st, "tab_small", [P, 24, NQ])
        d_sb = sb(st, "d_sb", [H, G])
        dd = sb(st, "d_diag", [H, G, H])
        s_ = [sm[:, i, :] for i in range(24)]
        (step, mag, ang, c1, sn, ar, ai, nai, nr, den, cr, ci, t1, t2, t3, t4, rd, r1, r2, kq, lr,
         wr, wi, _) = s_
        Vr, Vi = (tab[k][:, :, :].rearrange("p q (j h) -> p q j h", h=H) for k in ("Vr", "Vi"))
        in_ok = [pr.load("B_in", B[0][:, :, :], t["B_re"]), pr.load("B_in", B[1][:, :, :], t["B_im"]),
                 pr.load("B_in", Vr[:, :, 0, :], t["C_re"]), pr.load("B_in", Vi[:, :, 0, :], t["C_im"]),
                 pr.load("B_in", d_sb[:, :], t["d"])]
        chain = [None]

        def v(fn, *waits):
            chain[0] = pr.dve("tables", fn, chain[0], *waits)

        def a(fn, *waits):
            chain[0] = pr.act("tables_act", fn, chain[0], *waits)

        def tt(o, x, y, op, *waits):
            v(lambda e: e.tensor_tensor(o, x, y, op), *waits)

        def ts(o, x, k1, k2, op1, op2, *waits):
            v(lambda e: e.tensor_scalar(o, x, k1, k2, op1, op2), *waits)

        def stt(o, x, k, y, op1, op2):
            v(lambda e: e.scalar_tensor_tensor(o, x, k, y, op1, op2))

        def complex_product(outr, outi, xr, xi, yr, yi, tmps):
            p1, p2, p3, p4 = tmps
            tt(p1, xr, yr, ALU.mult)
            tt(p2, xi, yi, ALU.mult)
            tt(p3, xr, yi, ALU.mult)
            tt(p4, xi, yr, ALU.mult)
            tt(outr, p1, p2, ALU.subtract)
            tt(outi, p3, p4, ALU.add)

        def reduced_sin(out, shift):
            ts(kq, ang, shift, 1 / (2 * math.pi), ALU.add, ALU.mult)
            ts(kq, kq, ROUND, None, ALU.add, ALU.bypass)
            ts(kq, kq, ROUND, None, ALU.subtract, ALU.bypass)
            stt(r1, kq, -TWO_PI_HI, ang, ALU.mult, ALU.add)
            stt(r1, kq, -TWO_PI_LO, r1, ALU.mult, ALU.add)
            ts(r1, r1, shift, None, ALU.add, ALU.bypass)
            ts(r1, r1, PI_LOW, -PI_LOW, ALU.min, ALU.max)
            a(lambda e: e.activation(out, r1, ACT.Sin))

        ts(lr, col("lr", 0, NQ), -1e-4, None, ALU.min, ALU.bypass, env["cols_ok"])
        li = col("li", 0, NQ)
        a(lambda e: e.activation(step, col("log_step", 0, NQ), ACT.Exp))
        tt(t1, lr, step, ALU.mult)
        a(lambda e: e.activation(mag, t1, ACT.Exp))
        a(lambda e: e.activation(tab["rho"][:, :], t1, ACT.Exp, scale=float(CH)))
        tt(ang, li, step, ALU.mult)
        reduced_sin(sn, 0.0)
        reduced_sin(c1, math.pi / 2)
        tt(ar, mag, c1, ALU.mult)
        tt(ai, mag, sn, ALU.mult)
        ts(nai, ai, -1.0, None, ALU.mult, ALU.bypass)
        ts(nr, ar, -1.0, None, ALU.add, ALU.bypass)
        tt(den, lr, lr, ALU.mult)
        tt(t1, li, li, ALU.mult)
        tt(den, den, t1, ALU.add)
        v(lambda e: e.reciprocal(rd, den))
        tt(t1, nr, lr, ALU.mult)
        tt(t2, ai, li, ALU.mult)
        tt(t1, t1, t2, ALU.add)
        tt(cr, t1, rd, ALU.mult)
        tt(t1, ai, lr, ALU.mult)
        tt(t2, nr, li, ALU.mult)
        tt(t1, t1, t2, ALU.subtract)
        tt(ci, t1, rd, ALU.mult)

        def over(x, n):
            return spread(x, n)

        def tmps(n, k):
            return [tmp[:, i, 0:NQ * n].rearrange("p (q n) -> p q n", q=NQ) for i in range(4)]

        t16 = tmps(H, 4)
        pr_wait = in_ok
        tt(bb[0][:, :, :], B[0][:, :, :], over(cr, H), ALU.mult, pr_wait)
        complex_product(bb[0][:, :, :], bb[1][:, :, :], over(cr, H), over(ci, H),
                        B[0][:, :, :], B[1][:, :, :], t16)
        for c in range(2):
            v(lambda e, c=c: e.tensor_copy(W[c][:, :, CH - 1, :], bb[c][:, :, :]))
        for s in range(CH - 1, 0, -1):
            complex_product(W[0][:, :, s - 1, :], W[1][:, :, s - 1, :], over(ar, H), over(ai, H),
                            W[0][:, :, s, :], W[1][:, :, s, :], t16)
        w_ok = chain[0]
        ts(Vi[:, :, 0, :], Vi[:, :, 0, :], -1.0, None, ALU.mult, ALU.bypass)
        for j in range(CH):
            complex_product(Vr[:, :, j + 1, :], Vi[:, :, j + 1, :], over(ar, H), over(nai, H),
                            Vr[:, :, j, :], Vi[:, :, j, :], t16)
        v_ok = chain[0]
        free = [None] * 4
        n = 0
        e_ok = []
        for c, E in ((0, tab["Er"]), (1, tab["Ei"])):
            for q0 in range(0, NQ, 4):
                b = n % 4
                tr = pr.pe("E_turn", turns(bank(b), [W[c][:, q, :, :] for q in range(q0, q0 + 4)],
                                           ident), w_ok, env["ident_ok"], free[b])
                free[b] = pr.act("E_out", lambda e, E=E, q0=q0, b=b: e.activation(
                    E[:, q0:q0 + 4, :], bank(b).rearrange("p (j c) -> p j c", j=4), ACT.Copy), tr)
                n += 1
        e_ok = free[(n - 1) % 4]
        complex_product(wr, wi, c1, sn, c1, sn, (t1, t2, t3, t4))
        complex_product(wr, wi, wr, wi, wr, wi, (t1, t2, t3, t4))
        complex_product(wr, wi, wr, wi, wr, wi, (t1, t2, t3, t4))
        Tc, Ts = tab["Tc"], tab["Ts"]
        v(lambda e: e.memset(Tc[:, :, 0], 1.0))
        v(lambda e: e.memset(Ts[:, :, 0], 0.0))
        v(lambda e: e.tensor_copy(Tc[:, :, 1], wr))
        v(lambda e: e.tensor_copy(Ts[:, :, 1], wi))
        n = 2
        while n < NCH:
            h = n // 2
            complex_product(Tc[:, :, n], Ts[:, :, n], Tc[:, :, h], Ts[:, :, h], Tc[:, :, h],
                            Ts[:, :, h], (t1, t2, t3, t4))
            m = min(n, NCH - n)
            complex_product(Tc[:, :, n + 1:n + m], Ts[:, :, n + 1:n + m], Tc[:, :, 1:m],
                            Ts[:, :, 1:m], over(Tc[:, :, n], m - 1), over(Ts[:, :, n], m - 1),
                            tmps(m - 1, 4))
            n *= 2
        K = tmp[:, 0:2, :].rearrange("p a (g n) -> p (a g) n", n=P)
        t_ok = chain[0]
        k_ok = []
        kfree = [None, None]
        for g0 in range(0, G, 8):
            b = 4 + 2 * ((g0 // 8) % 2)
            for side in range(2):
                fns = []
                rows = slice(PS * side, PS * (side + 1))
                for j in range(4):
                    o, q = bank(b + side)[0:H, j * P:(j + 1) * P], g0 // 2 + j
                    for c, V in ((0, tab["Vr"]), (1, tab["Vi"])):
                        fns.append(mm(o, bb[c][rows, q, :], V[rows, q, 0:P], c == 0, c == 1))
                done = pr.pe("K_mm", last_of(fns), v_ok, kfree[(g0 // 8) % 2])
                k_ok.append(pr.act("K_out", lambda e, b=b, g0=g0, side=side: e.activation(
                    K[0:H, g0 + side:g0 + 8:2, :],
                    bank(b + side)[0:H, :].rearrange("p (j c) -> p j c", j=4), ACT.Copy),
                    done, t_ok))
            kfree[(g0 // 8) % 2] = k_ok[-2:]
        k_all = list(k_ok)
        tt(dd[:, :, :], over(d_sb[:, :], H), bass.AP(
            tensor=ident[:, :].tensor, offset=ident[:, :].offset,
            ap=[list(ident[0:H, :].ap[0]), [0, G], [1, H]]), ALU.mult)
        tt(K[0:H, :, 0:H], K[0:H, :, 0:H], dd[:, :, :], ALU.add, k_all)
        k_ok = chain[0]
        m_zero = pr.pool("M_zero", lambda e: e.memset(tab["M"][:, :, :], 0.0))
        for s in range(CH):
            tab["M_ok"] = pr.load("M_in", tab["M"][H * s:H * (s + 1), :, H * s:P],
                                  K[0:H, :, 0:P - H * s], k_ok, m_zero, k_all)
        tab.update(ok=chain[0], e_ok=e_ok)
        pr.hold("sp", tab["M_ok"])
        pr.emit()


def ssm_run(env, tab, u_grp, g_tok):
    pr, sb, t, bank, ident = (env[k] for k in ("pr", "sb", "t", "bank", "ident"))
    with ExitStack() as st:
        um8 = sb(st, "um8", [P, MCH, G])
        U = sb(st, "U_ring", [P, 2, 2, NCH])
        z = sb(st, "z", [P, 4, NCH])
        R = sb(st, "R_ring", [P, 2, 2, NCH])
        S = sb(st, "S_ring", [P, 2, 2, NCH])
        zz = sb(st, "S_tmp", [P, 4, NCH])
        y = sb(st, "y_ring", [P, 2, 2, 2 * P])
        um = env["u_meta"]
        for c in range(MCH):
            for s in range(CH):
                um_ok = pr.load("um8_in", um8[H * s:H * (s + 1), c, :], bass.AP(
                    tensor=um[:, :].tensor, offset=(c * CH + s) * W5, ap=[[1, H], [H, G]]))
        NX1 = NCH - 1
        Ur, X_ok, U_ok, S_ok, y_ok, z_ok = {}, {}, {}, {}, {}, {}
        U_free, x_free, R_free, S_free = [None] * 2, [None] * 2, [None] * 2, [None] * 2
        y_free, ut_free, yb_free, yt_free = [None] * 2, [None] * 2, [None], [None]
        last = [None]

        def enter(q):
            i = q % 2
            ub = bank(0)
            tiles = [u_grp[:, b, g, :, :] for g in (2 * q, 2 * q + 1) for b in range(2)]
            tr = pr.pe("U_turn", turns(ub, tiles, ident), ut_free[0])
            c = pr.act("U_out", lambda e: e.activation(
                U[:, i, :, MCH:NCH], ub.rearrange("p (g c) -> p g c", g=2), ACT.Copy),
                tr, U_free[i])
            m = pr.dve("U_meta", lambda e: e.tensor_copy(
                U[:, i, :, 0:MCH], um8[:, :, 2 * q:2 * q + 2].rearrange("p c g -> p g c")), um_ok, U_free[i])
            ut_free[0] = c
            U_ok[q] = [c, m]
            Ur[q] = tr
            fns = []
            for r, E in ((0, tab["Er"]), (1, tab["Ei"])):
                for g in range(2):
                    fns.append(mm(bank(2 + 2 * i + r)[PS * g:PS * (g + 1), 0:NX1],
                                  E[:, q, PS * g:PS * (g + 1)], U[:, i, g, 0:NX1]))
            X_ok[q] = pr.pe("X_mm", last_of(fns), U_ok[q], x_free[i])

        def recur(q):
            i = q % 2
            xr, xi = bank(2 + 2 * i)[:, 0:NX1], bank(3 + 2 * i)[:, 0:NX1]
            c, s = tab["Tc"][:, q, 1:NCH], tab["Ts"][:, q, 1:NCH]
            z_ = [z[:, k, 0:NX1] for k in range(4)]

            def tt(o, a, b, op, *w):
                return pr.dve("turn_in", lambda e: e.tensor_tensor(o, a, b, op), *w)

            tt(z_[0], xr, c, ALU.mult, X_ok[q], tab["ok"])
            a2 = tt(z_[1], xi, s, ALU.mult)
            tt(z_[2], xi, c, ALU.mult)
            x_free[i] = a4 = tt(z_[3], xr, s, ALU.mult)
            tt(z_[0], z_[0], z_[1], ALU.add, a2)
            a6 = tt(z_[2], z_[2], z_[3], ALU.subtract, a4)
            rho = bass.AP(tensor=tab["rho"][:, :].tensor, offset=tab["rho"][:, q:q + 1].offset,
                          ap=[list(tab["rho"][:, q:q + 1].ap[0]), [0, NX1]])
            for k in range(2):
                r_ok = pr.dve("scan", lambda e, k=k: e.tensor_tensor_scan(
                    R[:, i, k, 0:NX1], rho, z_[2 * k], 0.0, ALU.mult, ALU.add), a6, R_free[i])
            c2, s2 = tab["Tc"][:, q, MCH:NCH], tab["Ts"][:, q, MCH:NCH]
            Rr, Ri = R[:, i, 0, 1:NX1], R[:, i, 1, 1:NX1]
            w = [zz[:, k, 0:NCH - MCH] for k in range(4)]

            def gt(o, a, b, op, *ws):
                last[0] = pr.pool("turn_back", lambda e: e.tensor_tensor(o, a, b, op), last[0], *ws)
                return last[0]

            gt(w[0], Rr, c2, ALU.mult, r_ok)
            g2 = gt(w[1], Ri, s2, ALU.mult)
            gt(w[2], Rr, s2, ALU.mult)
            R_free[i] = g4 = gt(w[3], Ri, c2, ALU.mult)
            gt(S[:, i, 0, 0:NCH - MCH], w[0], w[1], ALU.subtract, g2, S_free[i])
            S_ok[q] = gt(S[:, i, 1, 0:NCH - MCH], w[2], w[3], ALU.add, g4)

        def leave(q):
            i = q % 2
            n = NCH - MCH
            fns = []
            for g in range(2):
                o, rows = bank(6 + g)[:, 0:n], slice(PS * g, PS * (g + 1))
                fns.append(mm(o, tab["M"][:, 2 * q + g, :], U[:, i, g, MCH:NCH], True, False))
                fns.append(mm(o, tab["Vr"][rows, q, H:H + P], S[rows, i, 0, 0:n], False, False))
                fns.append(mm(o, tab["Vi"][rows, q, H:H + P], S[rows, i, 1, 0:n], False, True))
            done = pr.pe("y_mm", last_of(fns), S_ok[q], tab["M_ok"], U_ok[q], yb_free[0])
            U_free[i] = S_free[i] = done
            y_ok[q] = yb_free[0] = pr.act("gelu", lambda e: e.activation(
                y[:, i, :, :], env["banks"][3][:, :, 0:n], ACT.Gelu_apprx_tanh),
                done, y_free[i])

        def back(q):
            i = q % 2
            tb = bank(1)
            tr = pr.pe("y_turn", turns(tb, [y[:, i, g, b * P:(b + 1) * P] for g in range(2)
                                            for b in range(2)], ident), y_ok[q], yt_free[0])
            y_free[i] = tr
            src = tb.rearrange("p (g b s h) -> p g b s h", g=2, b=2, s=CH)
            for b in range(2):
                dst = g_tok[:, b, :, 2 * H * q:2 * H * (q + 1)].rearrange("p s (g h) -> p g s h", g=2)
                yt_free[0] = pr.act("y_out", lambda e, b=b, dst=dst: e.activation(
                    dst, src[:, :, b, :, :], ACT.Copy), tr)

        for q in range(NQ + 2):
            if q < NQ:
                enter(q)
                recur(q)
            if 1 <= q <= NQ:
                leave(q - 1)
            if q >= 2:
                back(q - 2)
        with env["nc"].allow_non_contiguous_dma(reason="the meta tokens' 8192 values"):
            pr.emit()


def finish_channels(env, tag, tmpsq, acc, y, hi, lo, first, *waits):
    pr = env["pr"]
    w = list(waits)
    s = split_pair(pr, tag, hi, lo, y, w)
    q = pr.act(f"{tag}_sq", lambda e: e.activation(acc if first else tmpsq, y, ACT.Square), w,
               env.get(f"{tag}_sq_free"))
    out = q
    if not first:
        out = pr.dve(f"{tag}_sum", lambda e: e.tensor_tensor(acc, acc, tmpsq, ALU.add), q,
                     env.get(f"{tag}_sum_ok"))
    env[f"{tag}_sum_ok"] = out
    env[f"{tag}_sq_free"] = out
    return [s, out, q]


def pool_mixer(env, keep, vT, rs):
    pr, sb, t, bank, col = (env[k] for k in ("pr", "sb", "t", "bank", "col"))
    hi = sb(keep, "pool_hi", [P, NWIN, TOK], F32R, "right")
    lo = sb(keep, "pool_lo", [P, NWIN, TOK], F32R, "right")
    L = META + TOK
    with ExitStack() as st:
        a = sb(st, "win_a", [P, L])
        b = sb(st, "win_b", [P, L])
        p = sb(st, "pooled", [P, TOK])
        y = sb(st, "yp", [P, TOK])
        sq = sb(st, "yp_sq", [P, TOK])
        acc = sb(st, "yp_acc", [P, TOK])
        pw = sb(st, "pool_w_sb", [P, NWIN, P])
        ones = sb(st, "ones_col", [P, 1])
        pw_ok = pr.load("pool_w_in", pw[:, :, :], t["pool_w"][0].rearrange("k c d -> c k d"))
        one_ok = pr.pool("ones_col", lambda e: e.memset(ones[:, :], 1.0))
        chain = None
        p_free, y_free = None, None
        bank_free = [None] * 4
        for k in range(NWIN):
            w = 2 << k
            cur, d, bufs = vT[:, k, :], 1, [a[:, :], b[:, :]]
            while d < w:
                nxt = bufs[0]
                bufs.reverse()
                s0 = 2 * d - 1
                chain = pr.dve("window", lambda e, nxt=nxt, cur=cur, s0=s0, d=d: e.tensor_tensor(
                    nxt[:, s0:L], cur[:, s0:L], cur[:, s0 - d:L - d], ALU.add), chain)
                cur, d = nxt, 2 * d
            chain = pr.dve("pooled", lambda e, cur=cur, k=k, w=w: e.scalar_tensor_tensor(
                p[:, :], cur[:, META:L], 1.0 / w, vT[:, k, META:L], ALU.mult, ALU.subtract),
                chain, p_free)
            evs = []
            for n in range(4):
                mmd = pr.pe("pool_mm", mm(bank(n), pw[:, k, :], p[:, n * W5:(n + 1) * W5]),
                            chain, pw_ok, bank_free[n])
                dst = y[:, :].rearrange("d (b s p) -> d b p s", b=2, s=CH)[
                    :, n // 2, 64 * (n % 2):64 * (n % 2) + 64, :]
                bank_free[n] = pr.act("yp_out", lambda e, n=n, dst=dst, k=k: e.activation(
                    dst, bank(n).rearrange("d (p s) -> d p s", s=CH), ACT.Copy,
                    scale=col("pscale", k)), mmd, y_free)
                evs.append(bank_free[n])
            p_free = mmd
            y_free = finish_channels(env, "yp", sq[:, :], acc[:, :], y[:, :], hi[:, k, :],
                                     lo[:, k, :], k == 0, evs)
        token_rstd(env, "pn", acc, ones, rs[:, 1, :], one_ok, env["yp_sum_ok"])
        pr.emit()
    return hi, lo


def token_rstd(env, tag, acc, ones, out, *waits):
    pr, bank = env["pr"], env["bank"]
    done = pr.pe(f"{tag}_sum", last_of([
        mm(bank(4)[:, r:r + 1], acc[:, r * P:(r + 1) * P], ones[:, :]) for r in range(NT)]), *waits)
    c = pr.dve(f"{tag}_ss", lambda e: e.tensor_copy(out, bank(4)[:, 0:NT]), done)
    return rstd_from_sums(pr, tag, out, out, 1.0 / W5, EPS, c)


def ssm_gate(env, keep, g_tok, rs):
    pr, sb, t, bank, ident, col = (env[k] for k in ("pr", "sb", "t", "bank", "ident", "col"))
    hi = sb(keep, "ssm_hi", [P, 4, TOK], F32R, "right")
    lo = sb(keep, "ssm_lo", [P, 4, TOK], F32R, "right")
    with ExitStack() as st:
        gT = sb(st, "gT", [P, 2, W5])
        sg = sb(st, "sg", [P, 2, W5])
        y = sb(st, "ys", [P, 2, W5])
        sq = sb(st, "ys_sq", [P, W5])
        acc = sb(st, "ys_acc", [P, TOK])
        gw = sb(st, "glu_w_sb", [P, 4, P])
        ones = sb(st, "ones_col2", [P, 1])
        gw_ok = pr.load("glu_w_in", gw[:, :, :], t["glu_w"])
        one_ok = pr.pool("ones_col2", lambda e: e.memset(ones[:, :], 1.0))
        turn_free, mm_free, g_free, s_free, y_free = ([None] * 2 for _ in range(5))
        n = 0
        for q in range(4):
            for m in range(4):
                i = n % 2
                n += 1
                rows = [4 * m + j for j in range(4)]
                tr = pr.pe("g_turn", turns(bank(i), [g_tok[:, r // CH, r % CH, q * P:(q + 1) * P]
                                                     for r in rows], ident), turn_free[i])
                turn_free[i] = pr.act("gT_out", lambda e, i=i: e.activation(
                    gT[:, i, :], bank(i), ACT.Copy), tr, g_free[i])
                gate = pr.pe("glu_mm", mm(bank(2 + i), gw[:, q, :], gT[:, i, :]), turn_free[i],
                             gw_ok, mm_free[i])
                mm_free[i] = pr.act("glu_sig", lambda e, i=i, q=q: e.activation(
                    sg[:, i, :], bank(2 + i), ACT.Sigmoid, bias=col("glub", q)), gate, s_free[i])
                yo = pr.dve("ys_out", lambda e, i=i: e.tensor_tensor(
                    y[:, i, :], gT[:, i, :], sg[:, i, :], ALU.mult), mm_free[i], y_free[i])
                g_free[i], s_free[i] = [yo, gate], yo
                cs = slice(m * W5, (m + 1) * W5)
                y_free[i] = finish_channels(env, "ys", sq[:, :], acc[:, cs], y[:, i, :],
                                            hi[:, q, cs], lo[:, q, cs], q == 0, yo)
        token_rstd(env, "sn", acc, ones, rs[:, 0, :], one_ok, env["ys_sum_ok"])
        pr.emit()
    return hi, lo


def w_out_stage(env, rs, ssm_pair, pool_pair):
    pr, sb, t, bank, col = (env[k] for k in ("pr", "sb", "t", "bank", "col"))
    NX = 4
    with ExitStack() as st:
        w_hi = sb(st, "wout_hi", [P, KT, W5], F32R)
        w_lo = sb(st, "wout_lo", [P, KT, W5], F32R)
        w_st = sb(st, "wout_stage", [P, 2, W5])
        xr = sb(st, "x_res", [P, NX, W5])
        xv = t["x"][0].rearrange("(b p s) d -> b s p d", b=2, s=CH)
        hv = env["h1"][:, :].rearrange("(b p s) d -> b s p d", b=2, s=CH)
        w_free, st_free = None, [None, None]
        x_free, b_free = [None] * NX, [None] * 2
        junk = sb(st, "h1_junk", [P, W5])
        ss = sb(st, "h1_ss", [P, 2, NT])
        n, sq = 0, None
        for half in range(2):
            cs = slice(half * W5, (half + 1) * W5)
            ok = []
            for k in range(KT):
                i = k % 2
                ld = pr.load(f"wout_in{i}", w_st[:, i, :], t["w_out"][0, k * P:(k + 1) * P, cs],
                             st_free[i])
                h_ = pr.act("wout_hi", lambda e, k=k, i=i: e.activation(
                    w_hi[:, k, :], w_st[:, i, :], ACT.Copy, scale=col("mixg", k)), ld, w_free)
                st_free[i] = pr.dve("wout_lo", lambda e, k=k, i=i: e.scalar_tensor_tensor(
                    w_lo[:, k, :], w_st[:, i, :], col("mixg", k), w_hi[:, k, :].bitcast(F32),
                    ALU.mult, ALU.subtract), h_, w_free)
                ok.append(st_free[i])
            for r in range(NT):
                i, x = n % 2, n % NX
                n += 1
                ts_ = slice(r * P, (r + 1) * P)
                ld = pr.load(f"x_res_in{x}", xr[:, x, :], xv[r // CH, r % CH][:, cs], x_free[x])
                outs = [bank(2 * i), bank(2 * i + 1)]
                done = []
                for part, (mh, ml) in enumerate((ssm_pair, pool_pair)):
                    done.append(pr.pe("wout_mm", contraction(
                        outs[part], [(mh[:, k, ts_], ml[:, k, ts_]) for k in range(4)],
                        [(w_hi[:, 4 * part + k, :], w_lo[:, 4 * part + k, :]) for k in range(4)]),
                        ok, b_free[i]))
                a = pr.dve("h1_ssm", lambda e, x=x, o=outs[0], r=r: e.scalar_tensor_tensor(
                    xr[:, x, :], o, rs[:, 0, r:r + 1], xr[:, x, :], ALU.mult, ALU.add), done[0], ld)
                b = pr.dve("h1_pool", lambda e, x=x, o=outs[1], r=r: e.scalar_tensor_tensor(
                    xr[:, x, :], o, rs[:, 1, r:r + 1], xr[:, x, :], ALU.mult, ALU.add), done[1], a)
                b_free[i] = b
                sq = pr.act("h1_sq", lambda e, x=x, half=half, r=r: e.activation(
                    junk[:, :], xr[:, x, :], ACT.Square, accum_out=ss[:, half, r:r + 1]), b, sq)
                x_free[x] = [sq, pr.load(f"h1_st{x}", hv[r // CH, r % CH][:, cs], xr[:, x, :], b)]
            w_free = done[1]
        rs2 = env["rs2"][:, :]
        both = pr.dve("h1_ss", lambda e: e.tensor_tensor(rs2, ss[:, 0, :], ss[:, 1, :], ALU.add), sq)
        rstd_from_sums(pr, "n2", rs2, rs2, 1.0 / D, EPS, both)
        pr.hold("sp", x_free)
        pr.emit()



def row_in(env, stack, name, width=D):
    buf = env["sb"](stack, f"row_{name}", [P, width])
    rows = env["t"]["rows"]
    src = bass.AP(tensor=rows.tensor, offset=rows.offset + ROWS[name], ap=[[0, P], [1, width]])
    return buf, env["pr"].load(f"row_{name}", buf[:, :], src)


def transposed_halves(env, tag, i, z, hi, lo, turned, banks2, *waits):
    pr, bank, ident = env["pr"], env["bank"], env["ident"]
    oks = []
    for g in range(2):
        b = banks2[g]
        tr = pr.pe(f"{tag}_turn", turns(bank(b), [z[:, k * P:(k + 1) * P]
                                                  for k in range(4 * g, 4 * g + 4)], ident),
                   turned.get(b), *waits)
        turned[b] = split_pair(pr, tag, hi[:, 4 * g:4 * g + 4, i * P:(i + 1) * P],
                               lo[:, 4 * g:4 * g + 4, i * P:(i + 1) * P],
                               bank(b).rearrange("p (j c) -> p j c", j=4), tr)
        oks.append(turned[b])
    return oks, tr


def layer_norm_stats(pr, tag, x, st6, mv, *waits):
    for h in range(2):
        s = pr.dve(f"{tag}_st", lambda e, h=h: e.bn_stats(st6[:, 6 * h:6 * h + 6],
                                                         x[:, h * W5:(h + 1) * W5]), *waits)
    return pr.dve(f"{tag}_mv", lambda e: e.bn_aggr(mv, st6), s)


class Leaving:

    def __init__(self, env, stack, acc):
        sb = env["sb"]
        self.env, self.acc = env, acc
        self.gf, self.gf_ok = row_in(env, stack, "gf")
        self.lg, self.lg_ok = row_in(env, stack, "lin_g")
        self.lb, self.lb_ok = row_in(env, stack, "lin_b")
        self.junk = sb(stack, "h_junk", [P, D])
        self.ss = sb(stack, "ssf", [P, HT])
        self.st6 = sb(stack, "st6", [P, HT, 12])
        self.mv = sb(stack, "mv", [P, HT, 2])
        self.rl = sb(stack, "rl", [P, HT])
        self.shift = sb(stack, "shift", [P, HT])
        self.junk_free = None
        self.h2v = env["h2"][:, :].rearrange("(b p s) d -> b s p d", b=2, s=CH)

    def normalise(self, tiles, ready):
        pr, acc = self.env["pr"], self.acc
        ts_ = slice(tiles[0], tiles[-1] + 1)
        for i in tiles:
            sq = self.junk_free = pr.act("h_sq", lambda e, i=i: e.activation(
                self.junk[:, :], acc[:, i, :], ACT.Square, accum_out=self.ss[:, i:i + 1]),
                ready.get(i), self.junk_free)
            y = pr.dve("h_gf", lambda e, i=i: e.tensor_tensor(
                acc[:, i, :], acc[:, i, :], self.gf[:, :], ALU.mult), sq, self.gf_ok)
            mv_ok = layer_norm_stats(pr, "li", acc[:, i, :], self.st6[:, i, :], self.mv[:, i, :], y)
        ss, mean, var = self.ss[:, ts_], self.mv[:, ts_, 0], self.mv[:, ts_, 1]
        a = pr.dve("li_eps", lambda e: e.tensor_scalar(ss, ss, LN_EPS / D, LN_EPS * EPS, ALU.mult,
                                                      ALU.add), sq)
        a = pr.dve("li_var", lambda e: e.tensor_tensor(ss, ss, var, ALU.add), a, mv_ok)
        a = pr.act("li_root", lambda e: e.activation(ss, ss, ACT.Sqrt), a)
        a = pr.dve("li_rstd", lambda e: e.reciprocal(self.rl[:, ts_], ss), a)
        a = pr.dve("li_shift", lambda e: e.scalar_tensor_tensor(
            self.shift[:, ts_], mean, -1.0, self.rl[:, ts_], ALU.mult, ALU.mult), a)
        out, g = {}, None
        for i in tiles:
            n = pr.act("h2_n", lambda e, i=i: e.activation(
                acc[:, i, :], acc[:, i, :], ACT.Identity, scale=self.rl[:, i:i + 1],
                bias=self.shift[:, i:i + 1]), a)
            g = out[i] = pr.pool("h2_g", lambda e, i=i: e.tensor_tensor(
                acc[:, i, :], acc[:, i, :], self.lg[:, :], ALU.mult), n, self.lg_ok, g)
        return out

    def store(self, half, tiles, g):
        pr, acc, out = self.env["pr"], self.acc, {}
        for i in tiles:
            b = pr.dve("h2_b", lambda e, i=i: e.tensor_tensor(
                acc[:, i, :], acc[:, i, :], self.lb[:, :], ALU.add), g[i], self.lb_ok)
            out[i] = pr.load(f"h2_st{i}", self.h2v[half, i], acc[:, i, :], b)
        return out


def feed_forward(env):
    pr, sb, t, bank, banks = (env[k] for k in ("pr", "sb", "t", "bank", "banks"))
    with ExitStack() as keep:
        acc = sb(keep, "ff_acc", [P, HT, D])
        leave = Leaving(env, keep, acc)
        with ExitStack() as st:
            g2, g2_ok = row_in(env, st, "g2")
            n_hi = sb(st, "n2_hi", [P, KT, HALF], F32R)
            n_lo = sb(st, "n2_lo", [P, KT, HALF], F32R)
            z = sb(st, "z2", [P, 3, D])
            wst = sb(st, "ff_stage", [P, 3, D])
            wg_hi = sb(st, "gate_up_hi", [P, 2, 2, D], F32R)
            wg_lo = sb(st, "gate_up_lo", [P, 2, 2, D], F32R)
            wd_hi = sb(st, "down_hi", [P, D], F32R)
            wd_lo = sb(st, "down_lo", [P, D], F32R)
            f_hi = sb(st, "ff_hi", [P, 2, HALF], F32R)
            f_lo = sb(st, "ff_lo", [P, 2, HALF], F32R)
            sil = sb(st, "silu", [P, 2, W5])
            ff = sb(st, "ff", [P, 2, W5])
            gate = t["w_gate"][0].rearrange("(k p) f -> p k f", p=P)
            up = t["w_up"][0].rearrange("(k p) f -> p k f", p=P)
            h1v = env["h1"][:, :].rearrange("(b p s) d -> b s p d", b=2, s=CH)
            gu_in, gu_ok, gu_used, gu_st_free = {}, {}, [None, None], None
            d_in, d_ok, d_used, d_st_free = {}, {}, None, None
            f_ok, f_free = {}, [None, None]
            bank_free, sil_free, ff_free = {b: None for b in range(8)}, [None] * 2, [None] * 2
            n_ok, n_free, z_free, acc_ok, acc_done = [[], []], None, [None] * 3, {}, {}

            def js(J):
                return slice(J % NJ * P, (J % NJ + 1) * P)

            def load_gate_up(J):
                gu_in[J] = [pr.load("gate_up_in", wst[:, m, :].rearrange("p (k f) -> p k f", f=P),
                                    w[:, :, js(J)], gu_st_free) for m, w in enumerate((gate, up))]

            def split_gate_up(J):
                nonlocal gu_st_free
                i = J % 2
                gu_ok[J] = gu_st_free = split_pair(pr, "gate_up", wg_hi[:, i], wg_lo[:, i],
                                                   wst[:, 0:2], gu_in[J], gu_used[i])

            def load_down(J):
                d_in[J] = pr.load("down_in", wst[:, 2, :], t["w_down"][0, js(J), :], d_st_free)

            def split_down(J):
                nonlocal d_st_free
                d_ok[J] = d_st_free = split_pair(pr, "down", wd_hi[:, :], wd_lo[:, :],
                                                 wst[:, 2, :], d_in[J], d_used)

            def norm_tile(half, i):
                x = i % 3
                ld = pr.load(f"h1_in{x}", z[:, x, :], h1v[half, i], z_free[x])
                r = half * HT + i
                zo = pr.dve("z2", lambda e: e.scalar_tensor_tensor(
                    z[:, x, :], z[:, x, :], env["rs2"][:, r:r + 1], g2[:, :], ALU.mult, ALU.mult),
                    ld, g2_ok)
                oks, z_free[x] = transposed_halves(env, "n2T", i, z[:, x, :], n_hi, n_lo, bank_free,
                                                   (2 * (i % 2), 2 * (i % 2) + 1), zo, n_free)
                n_ok[i // 4] = oks if i % 4 == 0 else n_ok[i // 4] + oks

            def load_acc(half, i):
                acc_ok[i] = pr.load(f"acc_in{i}", acc[:, i, :], h1v[half, i], acc_ok.get(i))

            def gate_up(J, nh):
                i, cs = J % 2, slice(nh * W5, (nh + 1) * W5)
                done = []
                for m in range(2):
                    done.append(pr.pe("gate_up_mm", contraction(
                        bank(2 * m + nh),
                        [(wg_hi[:, i, m, k * P:(k + 1) * P], wg_lo[:, i, m, k * P:(k + 1) * P])
                         for k in range(KT)],
                        [(n_hi[:, k, cs], n_lo[:, k, cs]) for k in range(KT)]),
                        gu_ok[J], n_ok[nh], bank_free[2 * m + nh]))
                s = pr.act("silu", lambda e: e.activation(sil[:, nh, :], bank(nh), ACT.Silu),
                           done[0], sil_free[nh])
                bank_free[nh] = s
                f = pr.dve("ff", lambda e: e.tensor_tensor(
                    ff[:, nh, :], sil[:, nh, :], bank(2 + nh), ALU.mult), s, done[1], ff_free[nh])
                bank_free[2 + nh] = sil_free[nh] = f
                ff_free[nh] = split_pair(pr, "ff", f_hi[:, i, cs], f_lo[:, i, cs], ff[:, nh, :], f,
                                         f_free[i])
                f_ok[J, nh] = ff_free[nh]
                gu_used[i] = done[1]
                return done[1]

            def down(J, m):
                i, d = J % 2, m % 2
                rows = slice(m * P, (m + 1) * P)
                done = pr.pe("down_mm", last_of([contraction(
                    bank(4 + 2 * d + nh), [(f_hi[:, i, rows], f_lo[:, i, rows])],
                    [(wd_hi[:, nh * W5:(nh + 1) * W5], wd_lo[:, nh * W5:(nh + 1) * W5])])
                    for nh in range(2)]), d_ok[J], f_ok[J, m // 4], bank_free[4 + 2 * d])
                bank_free[4 + 2 * d] = acc_done[m] = pr.dve("ff_acc", lambda e: e.tensor_tensor(
                    acc[:, m, :].rearrange("p (a b) -> p a b", a=2),
                    acc[:, m, :].rearrange("p (a b) -> p a b", a=2), banks[2 + d][:, :, :],
                    ALU.add), done, acc_ok[m])
                return done

            for i in range(3):
                norm_tile(0, i)
            load_gate_up(0)
            for i in range(3, HT):
                norm_tile(0, i)
                if i == 3:
                    split_gate_up(0)
                    load_gate_up(1)
                    load_down(0)
            for i in range(HT):
                load_acc(0, i)
            last = 2 * NJ - 1
            for J in range(last + 2):
                at_turn = J == NJ
                if J >= 1:
                    split_down(J - 1)
                    if J <= last:
                        load_down(J)
                if J + 1 <= last:
                    split_gate_up(J + 1)
                    if J + 2 <= last:
                        load_gate_up(J + 2)
                if J <= last:
                    if at_turn:
                        for m in range(HT):
                            norm_tile(1, m)
                            d_used = down(J - 1, m)
                        f_free[(J - 1) % 2] = d_used
                        h2_st = leave.normalise(range(0, 4), acc_done)
                        gate_up(J, 0)
                        acc_ok.update(leave.store(0, range(0, 4), h2_st))
                        for i in range(0, 4):
                            load_acc(1, i)
                        h2_st = leave.normalise(range(4, HT), acc_done)
                        n_free = gate_up(J, 1)
                        acc_ok.update(leave.store(0, range(4, HT), h2_st))
                        for i in range(4, HT):
                            load_acc(1, i)
                    else:
                        gate_up(J, 0)
                        n_free = gate_up(J, 1)
                if J >= 1 and not at_turn:
                    for m in range(HT):
                        d_used = down(J - 1, m)
                    f_free[(J - 1) % 2] = d_used
            pr.hold("sp", [acc_ok[i] for i in range(HT)])
            pr.emit()
        project(env, leave)


BLOCKS = (("v", 1024, W5, "tok"), ("k", 512, W5, "T"), ("q", 0, W5, "T"), ("ag", 1536, W5, "tok"),
          ("gqk", 2048, W5, "T"), ("gv", 2560, W5, "tok"), ("glr", 3584, 16, "T"),
          ("gg", 3072, W5, "tok"))


def project(env, leave):
    pr, sb, t, bank = (env[k] for k in ("pr", "sb", "t", "bank"))
    for name, _, w, kind in BLOCKS:
        env["p_" + name] = env["scratch"]("p_" + name, [w, TOK] if kind == "T" else [TOK, w])
    with ExitStack() as st:
        hT_hi = sb(st, "hT_hi", [P, KT, HALF], F32R)
        hT_lo = sb(st, "hT_lo", [P, KT, HALF], F32R)
        hr = sb(st, "h2_ring", [P, 2, D])
        wst = sb(st, "pw_stage", [P, 2, 2, W5])
        w_hi = sb(st, "pw_hi", [P, 2, KT, W5], F32R)
        w_lo = sb(st, "pw_lo", [P, 2, KT, W5], F32R)
        o_sb = sb(st, "p_ring", [P, 4, W5])
        wv = t["w_in_2"][0].rearrange("(k p) c -> p k c", p=P)
        h_free, h_ok, h2_ok = [None] * 2, {}, {}
        w_ok, w_free, st_free = {}, [None, None], [None, None]
        bank_free, o_free, cnt = {b: None for b in range(8)}, [None] * 4, 0
        nb = len(BLOCKS)
        runs = [(half, b) for half in range(2) for b in range(nb)]

        def weights(n, pieces=range(4)):
            _, c0, w, _ = BLOCKS[runs[n][1]]
            i = n % 2
            for piece in pieces:
                x, ks = piece % 2, slice(2 * piece, 2 * piece + 2)
                ld = pr.load(f"pw_in{x}", wst[:, x, :, 0:w], wv[:, ks, c0:c0 + w], st_free[x])
                st_free[x] = split_pair(pr, "pw", w_hi[:, i, ks, 0:w], w_lo[:, i, ks, 0:w],
                                        wst[:, x, :, 0:w], ld, w_free[i])
                w_ok.setdefault(n, []).append(st_free[x])

        def tile_in(half, i, b2, used=None):
            x, r0 = i % 2, half * HALF + i * P
            ld = pr.load(f"h2_in{x}", hr[:, x, :], env["h2"][r0:r0 + P, :], h_free[x], h2_ok.get(half))
            h_ok[half, i], h_free[x] = transposed_halves(
                env, "hT", i, hr[:, x, :], hT_hi, hT_lo, bank_free, b2, ld, used)

        def product(n, tiles, lhs, rhs, scale, func, dst, rows=P):
            nonlocal cnt
            bk, o = cnt % 6, cnt % 4
            cnt += 1
            done = pr.pe("proj_mm", contraction(bank(bk), lhs, rhs), w_ok[n],
                         [h_ok[runs[n][0], i] for i in tiles], bank_free[bk])
            ev = bank_free[bk] = pr.act("proj_out", lambda e: e.activation(
                o_sb[0:rows, o, :], bank(bk)[0:rows, :], func, scale=scale), done, o_free[o])
            o_free[o] = pr.load(f"proj_st{o}", dst, o_sb[0:rows, o, :], ev, q="pool")
            return done

        def across(n, m):
            half, b = runs[n]
            name, i = BLOCKS[b][0], n % 2
            ms = slice(m * P, (m + 1) * P)
            return product(
                n, [m], [(hT_hi[:, k, ms], hT_lo[:, k, ms]) for k in range(KT)],
                [(w_hi[:, i, k, :], w_lo[:, i, k, :]) for k in range(KT)], 1.0,
                ACT.Silu if name in ("ag", "gg") else ACT.Copy,
                env["p_" + name][half * HALF + m * P:half * HALF + (m + 1) * P, :])

        def along(n, c, nh):
            half, b = runs[n]
            name, _, w, _ = BLOCKS[b]
            i, rows, cs = n % 2, min(w, P), slice(c * P, (c + 1) * P)
            t0, ts_ = half * HALF + nh * W5, slice(nh * W5, (nh + 1) * W5)
            scale = -0.125 if name == "q" else 0.125 if name == "gqk" and c < 2 else 1.0
            return product(
                n, range(4 * nh, 4 * nh + 4),
                [(w_hi[:, i, k, cs], w_lo[:, i, k, cs]) for k in range(KT)],
                [(hT_hi[:, k, ts_], hT_lo[:, k, ts_]) for k in range(KT)], scale, ACT.Copy,
                env["p_" + name][c * P:c * P + rows, t0:t0 + W5], rows)

        weights(0)
        tile_in(0, 0, (6, 7))
        used = {}
        g = [None, None]
        for n, (half, b) in enumerate(runs):
            name, _, w, kind = BLOCKS[b]
            if n + 1 < len(runs) and b != 0:
                weights(n + 1)
            if n in (1, 2):
                g[n - 1] = leave.normalise(range(4 * (n - 1), 4 * n), {})
            if n == 2:
                stores = leave.store(1, range(0, 4), g[0])
            if n == 3:
                stores.update(leave.store(1, range(4, HT), g[1]))
            if kind == "T":
                for c in range(max(1, w // P)):
                    for nh in range(2):
                        done = along(n, c, nh)
            else:
                for m in range(HT):
                    if b == 0 and half == 0 and m + 1 < HT:
                        tile_in(0, m + 1, (6, 7))
                    if b == 0 and m == 2:
                        weights(n + 1)
                    if n == nb - 1 and m >= 1:
                        if m == 1:
                            h2_ok[1] = list(stores.values())
                        tile_in(1, m - 1, (6, 7), done)
                    done = across(n, m)
                if n == nb - 1:
                    tile_in(1, HT - 1, (6, 7), done)
            w_free[n % 2] = done
        pr.hold("sp", o_free)
        pr.emit()


def band_attention(env):
    pr, sb, t, bank, banks, ident = (env[k] for k in ("pr", "sb", "t", "bank", "banks", "ident"))
    env["mix"] = mix = env["scratch"]("mix", [TOK, D])
    ext_d = env["scratch"]("ext", [NHEAD, EXT])
    skew = env["scratch"]("skew", [NHEAD, P, EXT])
    n_rel = 2 * CLIP + 1
    with ExitStack() as st:
        bias = sb(st, "bias", [P, NHEAD, BAND_W])
        rel = sb(st, "rel", [NHEAD, n_rel])
        ext = sb(st, "ext_sb", [NHEAD, EXT])
        q_src = sb(st, "q_src", [P, TOK])
        k_src = sb(st, "k_src", [P, TOK])
        q_st = sb(st, "q_stack", [P, 2, TOK], F32R)
        k_hi = sb(st, "k_hi", [P, 2, TOK], F32R)
        k_lo = sb(st, "k_lo", [P, 2, TOK], F32R)
        v_src = sb(st, "v_src", [P, NT, 2, AD])
        v_hl = sb(st, "v_hl", [P, 2, NT, 2, 2, AD], F32R)
        ag = sb(st, "ag_sb", [P, 2, NT, P])
        S = sb(st, "S_sb", [P, 3, BAND_W])
        E = sb(st, "E_sb", [P, 3, BAND_W])
        ET_hi = sb(st, "ET_hi", [P, 3, BAND_W], F32R)
        ET_lo = sb(st, "ET_lo", [P, 3, BAND_W], F32R)
        o = sb(st, "att_sb", [P, 2, NT, P])
        lo_half = sb(st, "lo_half", [P, 2, AD])
        mx = sb(st, "mx", [P, 8, 3])

        r_ok = pr.load("rel_in", rel[:, :], t["rel_bias_2"][0])
        flat_n = EXT - n_rel
        a_ = rel[:, :]
        e1 = pr.dve("ext", lambda e: e.tensor_scalar(ext[:, 0:flat_n], bass.AP(
            tensor=a_.tensor, offset=a_.offset + n_rel - 1, ap=[list(a_.ap[0]), [0, flat_n]]),
            -1.0, None, ALU.mult, ALU.bypass), r_ok)
        e2 = pr.dve("ext", lambda e: e.tensor_scalar(ext[:, flat_n:EXT], bass.AP(
            tensor=a_.tensor, offset=a_.offset + n_rel - 1, ap=[list(a_.ap[0]), [-1, n_rel]]),
            -1.0, None, ALU.mult, ALU.bypass), e1)
        s1 = pr.load("ext_st", ext_d[:, :], ext[:, :], e2)
        s2 = pr.load("skew_st", skew[:, :, :], bass.AP(
            tensor=ext_d[:, :].tensor, offset=0, ap=[[EXT, NHEAD], [0, P], [1, EXT]]), s1)
        b_in = pr.load("bias_in", bias[:, :, :], bass.AP(
            tensor=skew[:, :, :].tensor, offset=P - 1,
            ap=[[EXT - 1, P], [P * EXT, NHEAD], [1, BAND_W]]), s2)
        b1 = pr.dve("bias_end", lambda e: e.memset(bias[0:64, :, BAND_W - 64:BAND_W], -NEG), b_in)
        bias_ok = pr.dve("bias_end", lambda e: e.memset(bias[64:P, :, 0:64], -NEG), b1)

        src_ok, src_free, head_ok, head_free = {}, None, {}, [None] * 2
        v_ok, v_free, v_src_ok, v_src_free = {}, [None] * 2, {}, None
        ag_ok, ag_free, o_free = {}, [None] * 2, [None] * 2
        s_done, s_free, m_ok, S_free, e_ok, E_free = {}, None, {}, [None] * 3, {}, [None] * 3
        t_done, t_free, hi_ok, et_ok, ET_free = {}, [None] * 2, {}, {}, [None] * 3
        r_ok, pv_free = {}, [None] * 2
        units = [(h, qt) for h in range(NHEAD) for qt in range(NT)]

        def load_head(h):
            rows = slice(h * AD, (h + 1) * AD)
            src_ok[h] = [pr.load(f"{n}_in", buf[AD * c:AD * (c + 1), :], env["p_" + n][rows, :],
                                 src_free) for n, buf in (("q", q_src), ("k", k_src))
                         for c in range(2)]
            head_ok[h] = []
            if h % 2 == 0:
                hp, cs = h // 2, slice(h * AD, (h + 2) * AD)
                v_src_ok[hp] = pr.load("v_in", v_src[:, :, :, :].rearrange(
                    "p m h c -> p m (h c)"), env["p_v"][:, cs].rearrange(
                    "(m p) c -> p m c", p=P), v_src_free)
                v_ok[hp] = []
                ag_ok[hp] = pr.load(f"ag_in{hp % 2}", ag[:, hp % 2, :, :], env["p_ag"][
                    :, cs].rearrange("(m p) c -> p m c", p=P), ag_free[hp % 2])

        def split_head(h, piece):
            nonlocal src_free, v_src_free
            what, n = divmod(piece, 4)
            i, ns = h % 2, slice(n * W5, (n + 1) * W5)
            if what == 0:
                ok = split_pair(pr, "k_split", k_hi[:, i, ns], k_lo[:, i, ns], k_src[:, ns],
                                src_ok[h], head_free[i])
                head_ok[h].append(ok)
            elif what == 1:
                a1 = pr.act("q_hi", lambda e: e.activation(q_st[:, i, ns], q_src[:, ns], ACT.Copy),
                            src_ok[h], head_free[i])
                low = slice(AD, P)
                ok = pr.dve("q_lo", lambda e: e.tensor_tensor(
                    q_st[low, i, ns], q_src[low, ns], q_st[low, i, ns].bitcast(F32),
                    ALU.subtract), a1)
                head_ok[h].append(ok)
                src_free = ok
            elif h % 2 == 0:
                hp, ms = h // 2, slice(4 * n, 4 * n + 4)
                v_src_free = split_pair(pr, "v_split", v_hl[:, hp % 2, ms, :, 0, :],
                                        v_hl[:, hp % 2, ms, :, 1, :], v_src[:, ms, :, :],
                                        v_src_ok[hp], v_free[hp % 2])
                v_ok[hp].append(v_src_free)

        def geometry(u):
            h, qt = units[u]
            nk = min(qt + 1, BAND_T)
            return h, qt, nk, qt + 1 - nk, nk * P

        def joined(pb, W):
            return pb[:, :, :].rearrange("p a b -> p (a b)")[:, 0:W]

        def scores(u):
            h, qt, nk, k0, W = geometry(u)
            i, pb = h % 2, banks[0]
            fns = []
            for c in range(0, W, W5):
                w = min(c + W5, W) - c
                ks = slice(k0 * P + c, k0 * P + c + w)
                for part, kk in enumerate((k_lo, k_hi)):
                    fns.append(mm(pb[:, c // W5, 0:w], q_st[:, i, qt * P:(qt + 1) * P],
                                  kk[:, i, ks], part == 0, part == 1))
            s_done[u] = pr.pe("score_mm", last_of(fns), head_ok[h], s_free)
            if qt == NT - 1:
                head_free[i] = s_done[u]

        def maximum(u):
            nonlocal s_free
            h, qt, nk, k0, W = geometry(u)
            x = u % 3
            m_ok[u] = s_free = pr.dve("score_max", lambda e: e.tensor_tensor_reduce(
                S[:, x, 0:W], joined(banks[0], W), bias[:, h, BAND_W - W:BAND_W], 1.0, 3e38,
                ALU.add, ALU.min, mx[:, u % 8, 0:1]), s_done[u], bias_ok, S_free[x])

        def exponentials(u):
            h, qt, nk, k0, W = geometry(u)
            x = u % 3
            e_ok[u] = S_free[x] = pr.act("exp", lambda e: e.activation(
                E[:, x, 0:W], S[:, x, 0:W], ACT.Exp, scale=-1.0, bias=mx[:, u % 8, 0:1],
                accum_out=mx[:, u % 8, 1:2]), m_ok[u], E_free[x])

        def turn_e(u):
            h, qt, nk, k0, W = geometry(u)
            x, pb = u % 3, banks[1 + u % 2]
            t_done[u] = E_free[x] = pr.pe("E_turn2", last_of([
                (lambda e, j=j: e.transpose(pb[:, j // 4, (j % 4) * P:(j % 4 + 1) * P],
                                            E[:, x, j * P:(j + 1) * P], ident[:, :]))
                for j in range(nk)]), e_ok[u], t_free[u % 2])
            hi_ok[u] = pr.act("ET_hi", lambda e: e.activation(
                ET_hi[:, x, 0:W], joined(pb, W), ACT.Copy), t_done[u], ET_free[x])
            r_ok[u] = pr.dve("sum_recip", lambda e: e.reciprocal(
                mx[:, u % 8, 2:3], mx[:, u % 8, 1:2]), e_ok[u])

        def lower(u):
            h, qt, nk, k0, W = geometry(u)
            x = u % 3
            et_ok[u] = t_free[u % 2] = pr.dve("ET_lo", lambda e: e.tensor_tensor(
                ET_lo[:, x, 0:W], joined(banks[1 + u % 2], W), ET_hi[:, x, 0:W].bitcast(F32),
                ALU.subtract), hi_ok[u], ET_free[x])

        def values(u):
            h, qt, nk, k0, W = geometry(u)
            hp, x, y = h // 2, u % 3, u % 2
            i, rows = hp % 2, slice(AD * (h % 2), AD * (h % 2 + 1))
            pb = bank(6 + y)
            done = pr.pe("pv_mm", last_of([
                mm(pb[:, 0:P], half[:, x, j * P:(j + 1) * P],
                   v_hl[:, i, k0 + j, h % 2, :, :].rearrange("p a c -> p (a c)"),
                   j == 0 and half is ET_lo, j == nk - 1 and half is ET_hi)
                for j in range(nk) for half in (ET_lo, ET_hi)]), et_ok[u], v_ok[hp], pv_free[y])
            ET_free[x] = done
            b = pr.dve("att_halves", lambda e: e.tensor_copy(lo_half[:, y, :], pb[:, AD:P]), done)
            pv_free[y] = f = pr.dve("att_sum", lambda e: e.tensor_tensor(
                lo_half[:, y, :], lo_half[:, y, :], pb[:, 0:AD], ALU.add), b)
            f = pr.dve("att_out", lambda e: e.scalar_tensor_tensor(
                o[:, i, qt, rows], lo_half[:, y, :], mx[:, u % 8, 2:3], ag[:, i, qt, rows],
                ALU.mult, ALU.mult), f, r_ok[u], o_free[i], ag_ok[hp])
            if qt == NT - 1 and h % 2 == 1:
                v_free[i], ag_free[i] = done, f
                o_free[i] = pr.load(f"att_st{i}", mix[:, hp * P:(hp + 1) * P].rearrange(
                    "(m p) c -> p m c", p=P), o[:, i, :, :], f)

        load_head(0)
        for piece in range(12):
            split_head(0, piece)
        n = len(units)
        for u in range(n + 4):
            h, qt = units[u] if u < n else (NHEAD, 0)
            if h + 1 < NHEAD:
                if qt == 2:
                    load_head(h + 1)
                if 4 <= qt < 16:
                    split_head(h + 1, qt - 4)
            if 3 <= u < n + 3:
                lower(u - 3)
            if u < n:
                scores(u)
                maximum(u)
            if 1 <= u <= n:
                exponentials(u - 1)
            if 2 <= u < n + 2:
                turn_e(u - 2)
            if u >= 4:
                values(u - 4)
        pr.hold("sp", o_free)
        pr.emit()


def gated_linear_attention(env, out_w):
    pr, sb, t, bank, banks, ident, col = (env[k] for k in (
        "pr", "sb", "t", "bank", "banks", "ident", "col"))
    C = 64
    NC = TOK // C
    UT = 4
    UC = UT * P // C
    NU = NT // UT
    mix = env["mix"]
    with ExitStack() as st:
        q, k, L, eL, eN, qf, tmp = (sb(st, n, [P, 2, W5]) for n in (
            "gq", "gk", "gL", "eL", "eN", "q_fwd", "g_tmp"))
        reset = sb(st, "reset", [P, W5])
        lend = sb(st, "lend", [P, 2, UC])
        dec = sb(st, "dec", [P, 2, UC])
        v = sb(st, "gv_sb", [P, 2, UT, 2 * P])
        gate = sb(st, "gg_sb", [P, 2, UT, 2 * P])
        raw = sb(st, "o_raw", [P, 2, UT, 2 * P])
        lr_ = sb(st, "glr_sb", [16, TOK])
        gw = sb(st, "w_gg", [16, 2 * P])
        mask = sb(st, "tri", [P, C])
        att = sb(st, "g_att", [P, 2, 2, C])
        kdT = sb(st, "kdT", [P, 2, P])
        state = sb(st, "g_state", [P, 4, P])
        ssq = sb(st, "g_ss", [P, 2, UT, 2])
        junk = sb(st, "g_junk", [P, 2, P])
        gn = sb(st, "g_gain", [P, 4 * P])
        w_st = sb(st, "ow_stage", [P, 2, D])
        l_in = [pr.load("glr_in", lr_[:, :], env["p_glr"][:, :]),
                pr.load("glr_in", gw[:, :], t["w_gla_gate_2"][0])]
        rows = t["rows"]
        n_in = pr.load("ggain_in", gn[:, :], bass.AP(
            tensor=rows.tensor, offset=rows.offset + ROWS["gla_g"], ap=[[0, P], [1, 4 * P]]))
        m1 = pr.pool("g_const", lambda e: e.memset(reset[:, :], 1.0))
        m2 = pr.pool("g_const", lambda e: e.memset(reset[:, 0:W5:C], 0.0), m1)
        m3 = pr.pool("g_const", lambda e: e.memset(mask[:, :], 1.0), m2)
        for c in range(2):
            m3 = pr.pool("g_const", lambda e, c=c: e.affine_select(
                out=mask[C * c:C * (c + 1), :], in_=mask[C * c:C * (c + 1), :],
                compare_op=ALU.is_ge, fill=0.0, base=0, pattern=[[1, C]],
                channel_multiplier=-1), m3)
        const_ok = gg_last = m3
        units = [(hp, n) for hp in range(2) for n in range(NU)]
        S, used = {}, [[], []]
        w_free = [None, None]

        def fetch(u):
            hp, n = units[u]
            i, ts_ = u % 2, slice(n * W5, (n + 1) * W5)
            vs = slice(hp * 2 * P, (hp + 1) * 2 * P)
            w = list(used[i])
            S[u] = dict(
                qk=[pr.load(f"gqk_in{i}", buf[:, i, :], env["p_gqk"][r0 + hp * P:r0 + (hp + 1) * P,
                                                                    ts_], w)
                    for r0, buf in ((0, q), (2 * P, k))],
                v=pr.load(f"gv_in{i}", v[:, i, :, :], env["p_gv"][ts_, vs].rearrange(
                    "(m p) c -> p m c", p=P), w),
                gate=pr.load(f"gg_in{i}", gate[:, i, :, :], env["p_gg"][ts_, vs].rearrange(
                    "(m p) c -> p m c", p=P), w), w=w)

        sc = 1.0 / 16.0

        def prepare(u, part):
            nonlocal gg_last
            hp, n = units[u]
            i, s = u % 2, S[u]
            L_, T_, eL_, eN_, q_, k_, qf_ = (x[:, i, :] for x in (L, tmp, eL, eN, q, k, qf))
            if part == 0:
                d = pr.pe("glogit_mm", mm(bank(5), gw[:, hp * P:(hp + 1) * P],
                                          lr_[:, n * W5:(n + 1) * W5]), l_in, S.get("logit"))
                a = S["logit"] = s["L"] = pr.act("glogit", lambda e: e.activation(
                    L_, bank(5), ACT.Identity, bias=col("bgate", hp)), d, s["w"])
                a = pr.act("g_abs", lambda e: e.activation(T_, L_, ACT.Abs), a)
                a = pr.act("g_exp", lambda e: e.activation(T_, T_, ACT.Exp, scale=-1.0), a)
                s["ln"] = pr.act("g_ln", lambda e: e.activation(T_, T_, ACT.Ln, bias=1.0), a)
                for hh in range(2):
                    o_ = slice(hh * P, (hh + 1) * P)
                    g_ = gn[:, hp * 2 * P + hh * P:hp * 2 * P + (hh + 1) * P]
                    g_ = bass.AP(tensor=g_.tensor, offset=g_.offset,
                                 ap=[list(g_.ap[0]), [0, UT], [1, P]])
                    gg_last = s["gg"] = pr.pool("g_gate", lambda e, o_=o_, g_=g_: e.tensor_tensor(
                        gate[:, i, :, o_], gate[:, i, :, o_], g_, ALU.mult), s["gate"], n_in,
                        gg_last)
            elif part == 1:
                b = pr.dve("g_logsig", lambda e: e.scalar_tensor_tensor(
                    T_, L_, 0.0, T_, ALU.min, ALU.subtract), s["ln"], s["L"])
                b = s["L"] = pr.dve("g_cumsum", lambda e: e.tensor_tensor_scan(
                    L_, reset[:, :], T_, 0.0, ALU.mult, ALU.add), b, const_ok)
                s["eL"] = pr.act("g_eL", lambda e: e.activation(eL_, L_, ACT.Exp, scale=sc), b)
                s["eN"] = pr.act("g_eN", lambda e: e.activation(eN_, L_, ACT.Exp, scale=-sc), b)
                b = pr.dve("g_lend", lambda e: e.tensor_copy(lend[:, i, :], L[:, i, C - 1:W5:C]), b)
                s["dec"] = pr.act("g_dec", lambda e: e.activation(dec[:, i, :], lend[:, i, :],
                                                                  ACT.Exp, scale=sc), b)
                b = pr.dve("g_left", lambda e: e.tensor_tensor(
                    T_.rearrange("p (n c) -> p n c", c=C), spread(lend[:, i, :], C),
                    L_.rearrange("p (n c) -> p n c", c=C), ALU.subtract), b)
                s["left"] = pr.act("g_kdecay", lambda e: e.activation(T_, T_, ACT.Exp, scale=sc), b)
            else:
                def mul(o, x, y, *w):
                    return pr.dve("g_mul", lambda e: e.tensor_tensor(o, x, y, ALU.mult), *w)

                s["kd"] = mul(T_, T_, k_, s["left"], s["qk"])
                s["qf"] = mul(qf_, q_, eL_, s["eL"])
                mul(eL_, k_, eL_, s["qf"])
                qn = mul(q_, q_, eN_, s["eN"])
                s["kn"] = mul(eN_, k_, eN_, qn)

        w_ok = []

        def split_w(kt):
            x = kt % 2
            ld = pr.load(f"ow_in{x}", w_st[:, x, :], t["w_out_2"][0, kt * P:(kt + 1) * P, :],
                         w_free[x])
            w_free[x] = split_pair(pr, "ow", out_w[0][:, kt, :], out_w[1][:, kt, :], w_st[:, x, :],
                                   ld)
            w_ok.append(w_free[x])

        att_ok, att_free, kd_free, kdT_ok = {}, [None] * 2, [None] * 2, {}
        a_free, kv_free, o_free, kt_free = None, [None] * 2, None, None
        state_ok, state_free, sq_last = {}, [None] * 4, [None, None]
        raw_st = [None] * 2

        def inner(m):
            nonlocal a_free, kt_free
            y, u, i, m0 = m % 2, m // UT, m // UT % 2, m % UT * P
            s = S[u]
            done = []
            for hh in range(2):
                r = slice(C * hh, C * (hh + 1))
                fns = []
                for c in range(2):
                    ts_ = slice(m0 + C * c, m0 + C * (c + 1))
                    for w, (l_, r_) in enumerate(((eN, qf), (eL, q))):
                        fns.append(mm(bank(hh)[C * c:C * (c + 1), w * C:(w + 1) * C],
                                      l_[r, i, ts_], r_[r, i, ts_]))
                done.append(pr.pe("g_att_mm", last_of(fns), s["kn"], a_free))
            oks = []
            for hh in range(2):
                a1 = pr.act("g_anti", lambda e, hh=hh: e.activation(
                    att[:, y, hh, :], bank(hh)[:, C:2 * C], ACT.Copy), done[hh], att_free[y])
                oks.append(pr.dve("g_causal", lambda e, hh=hh: e.copy_predicated(
                    att[:, y, hh, :], mask[:, :].bitcast(U32), bank(hh)[:, 0:C]),
                    a1, done[hh], const_ok))
            a_free = att_ok[m] = oks
            tr = pr.pe("kd_turn", turns(bank(2), [tmp[:, i, m0:m0 + P]], ident), s["kd"], kt_free)
            kdT_ok[m] = kt_free = pr.act("kdT_out", lambda e: e.activation(
                kdT[:, y, :], bank(2)[:, 0:P], ACT.Copy), tr, kd_free[y])

        def carry(m):
            y, u = m % 2, m // UT
            i, s = u % 2, S[u]
            for c in range(2):
                n = 2 * m + c
                if n % NC == NC - 1:
                    continue
                if n % NC == 0:
                    state_ok[n] = pr.dve("g_state", lambda e, n=n: e.memset(state[:, n % 4, :], 0.0),
                                         state_free[n % 4])
                r = slice(C * c, C * (c + 1))
                kb = bank(3 + c)
                kd_free[y] = done = pr.pe("kv_mm", last_of([
                    mm(kb[C * hh:C * (hh + 1), 0:P], kdT[r, y, C * hh:C * (hh + 1)],
                       v[r, i, m % UT, hh * P:(hh + 1) * P]) for hh in range(2)]),
                    kdT_ok[m], s["v"], kv_free[c])
                state_ok[n + 1] = kv_free[c] = pr.dve("g_state", lambda e, n=n, kb=kb:
                    e.scalar_tensor_tensor(
                        state[:, (n + 1) % 4, :], state[:, n % 4, :], dec[:, i, n % UC:n % UC + 1],
                        kb[:, 0:P], ALU.mult, ALU.add),
                    done, s["dec"], state_ok[n], state_free[(n + 1) % 4])

        def outer(m):
            nonlocal o_free
            y, u = m % 2, m // UT
            i, s, m_ = u % 2, S[u], m % UT
            for hh in range(2):
                r = slice(C * hh, C * (hh + 1))
                for c in range(2):
                    n = 2 * m + c
                    rc = slice(C * c, C * (c + 1))
                    ts_ = slice(m_ * P + C * c, m_ * P + C * (c + 1))
                    ob = bank(6 + c)[rc, hh * P:(hh + 1) * P]
                    a1 = pr.pe("g_o_mm", mm(ob, att[rc, y, hh, :], v[rc, i, m_, hh * P:(hh + 1) * P],
                                            True, False), att_ok[m], s["v"], o_free)
                    o_done = state_free[n % 4] = pr.pe(
                        "g_o_mm", mm(ob, qf[r, i, ts_], state[r, n % 4, :], False, True),
                        a1, state_ok[n], s["qf"])
            att_free[y] = o_done
            o_free = [pr.dve("g_raw", lambda e, c=c: e.tensor_copy(
                raw[C * c:C * (c + 1), i, m_, :], bank(6 + c)[C * c:C * (c + 1), 0:2 * P]), o_done,
                raw_st[i]) for c in range(2)]
            for hh in range(2):
                sq_last[hh] = s["sq"] = pr.act("g_sq", lambda e, hh=hh: e.activation(
                    junk[:, hh, :], raw[:, i, m_, hh * P:(hh + 1) * P], ACT.Square,
                    accum_out=ssq[:, i, m_, hh:hh + 1]), o_free, sq_last[hh])
            if m_ == UT - 1:
                used[i] = [o_done, s["sq"]] + o_free

        def finish(u):
            hp, n = units[u]
            i = u % 2
            r_ok = rstd_from_sums(pr, "g_n", ssq[:, i], ssq[:, i], 1.0 / P, EPS, S[u]["sq"])
            for m_ in range(UT):
                for hh in range(2):
                    s_ = slice(hh * P, (hh + 1) * P)
                    f = pr.dve("g_final", lambda e, m_=m_, hh=hh, s_=s_: e.scalar_tensor_tensor(
                        raw[:, i, m_, s_], raw[:, i, m_, s_], ssq[:, i, m_, hh:hh + 1],
                        gate[:, i, m_, s_], ALU.mult, ALU.mult), r_ok, S[u]["gg"])
            used[i].append(f)
            raw_st[i] = pr.load(f"gla_st{i}", mix[n * W5:(n + 1) * W5, W5 + hp * 2 * P:
                                                  W5 + (hp + 1) * 2 * P].rearrange(
                "(m p) c -> p m c", p=P), raw[:, i, :, :], f)

        nt = len(units) * UT
        fetch(0)
        for part in range(3):
            prepare(0, part)
        fetch(1)
        for m in range(nt + 1):
            u, m_ = divmod(m, UT)
            if m < nt:
                inner(m)
            if m >= 1:
                carry(m - 1)
                outer(m - 1)
            if m_ == 0 and u >= 1:
                finish(u - 1)
                if u + 1 < len(units):
                    fetch(u + 1)
            if m < nt and m_ >= 1 and u + 1 < len(units):
                prepare(u + 1, m_ - 1)
            if m % 4 == 2 and m // 4 < KT:
                split_w(m // 4)
        pr.hold("sp", raw_st)
        pr.emit()


def output_block(env, out_w):
    pr, sb, t, bank, banks, ident = (env[k] for k in ("pr", "sb", "t", "bank", "banks", "ident"))
    KP = 2
    NR = 4
    with ExitStack() as st:
        g_hi = sb(st, "og_hi", [P, KT, D], F32R)
        g_lo = sb(st, "og_lo", [P, KT, D], F32R)
        q_hi = sb(st, "oq_hi", [P, KP, D], F32R)
        q_lo = sb(st, "oq_lo", [P, KP, D], F32R)
        mix = sb(st, "mix_ring", [P, 2, D])
        x_hi = sb(st, "mT_hi", [P, KT, P], F32R)
        x_lo = sb(st, "mT_lo", [P, KT, P], F32R)
        y_hi = sb(st, "rT_hi", [P, KT, P], F32R)
        y_lo = sb(st, "rT_lo", [P, KT, P], F32R)
        pin = sb(st, "p_ring", [P, 3, KP * P])
        p_hi = sb(st, "pT_hi", [P, KP, P], F32R)
        p_lo = sb(st, "pT_lo", [P, KP, P], F32R)
        r = sb(st, "r_ring", [P, NR, D])
        g = sb(st, "ple_g", [P, 2, W5])
        bp, bp_ok = row_in(env, st, "b_ple")
        lg, lg_ok = row_in(env, st, "ln_g")
        lb, lb_ok = row_in(env, st, "ln_b")
        st6 = sb(st, "st6o", [P, 2, 12])
        mv = sb(st, "mvo", [P, 2, 2])
        rl = sb(st, "rlo", [P, 2, 2])
        m_in, r_in, p_in = {}, {}, {}
        m_free, r_free, p_free = [None] * 2, [None] * NR, [None] * 3
        x_ok, y_ok, pt_ok, x_used, y_used, pt_used = {}, {}, {}, None, None, None
        free = {b: None for b in range(8)}
        r_ok, g_free, gw_ok, qw_ok, last_pool = {}, [None] * 2, [], [], None

        def fetch(n):
            rows = slice(n * P, (n + 1) * P)
            m_in[n] = pr.load(f"mix_in{n % 2}", mix[:, n % 2, :], env["mix"][rows, :], m_free[n % 2])
            r_in[n] = pr.load(f"r_in{n % NR}", r[:, n % NR, :], env["h2"][rows, :], r_free[n % NR])
            p_in[n] = pr.load(f"p_in{n % 3}", pin[:, n % 3, :], t["p_2"][0, 0, rows, :], p_free[n % 3])

        def weights():
            for k in range(KP + KT):
                x = 2 + k % 2
                w, kk, hi, lo, oks = ((t["w_ple_2"], k, q_hi, q_lo, qw_ok) if k < KP else
                                      (t["w_ple_gate_2"], k - KP, g_hi, g_lo, gw_ok))
                ld = pr.load(f"ow_in{x}", r[:, x, :], w[0, kk * P:(kk + 1) * P, :], r_free[x])
                r_free[x] = split_pair(pr, "og", hi[:, kk, :], lo[:, kk, :], r[:, x, :], ld)
                oks.append(r_free[x])

        def turn_mix(n):
            x_ok[n], m_free[n % 2] = transposed_halves(
                env, "mT", 0, mix[:, n % 2, :], x_hi, x_lo, free, (4, 5), m_in[n], x_used)

        def residual(n):
            nonlocal x_used
            x = n % NR
            r_ok[n] = []
            for c in range(2):
                cs = slice(c * W5, (c + 1) * W5)
                x_used = pr.pe("wo2_mm", contraction(
                    bank(c), [(x_hi[:, k, :], x_lo[:, k, :]) for k in range(KT)],
                    [(out_w[0][:, k, cs], out_w[1][:, k, cs]) for k in range(KT)]), x_ok[n], free[c])
                free[c] = pr.dve("r_mix", lambda e, c=c, cs=cs: e.scalar_tensor_tensor(
                    r[:, x, cs], r[:, x, cs], ALPHA, bank(c), ALU.mult, ALU.add), x_used, r_in[n])
                r_ok[n].append(free[c])

        def turn_r_p(n):
            y_ok[n], _ = transposed_halves(env, "rT", 0, r[:, n % NR, :], y_hi, y_lo, free, (6, 7),
                                           r_ok[n], y_used)
            tr = p_free[n % 3] = pr.pe("pT_turn", turns(bank(4), [
                pin[:, n % 3, k * P:(k + 1) * P] for k in range(KP)], ident), p_in[n], free[4])
            pt_ok[n] = free[4] = split_pair(
                pr, "pT", p_hi[:, :, :], p_lo[:, :, :],
                bank(4)[:, 0:KP * P].rearrange("p (j c) -> p j c", j=KP), tr, pt_used)

        def gates(n):
            nonlocal y_used, pt_used
            x, fin = n % NR, []
            pd = []
            for c in range(2):
                cs = slice(c * W5, (c + 1) * W5)
                pd.append(pr.pe("ple_mm", contraction(
                    bank(2 + c), [(p_hi[:, k, :], p_lo[:, k, :]) for k in range(KP)],
                    [(q_hi[:, k, cs], q_lo[:, k, cs]) for k in range(KP)]), qw_ok, pt_ok[n],
                    free[2 + c]))
            pt_used = pd[1]
            for c in range(2):
                cs, gb = slice(c * W5, (c + 1) * W5), 6 + c
                y_used = pr.pe("gate_mm", contraction(
                    bank(gb), [(y_hi[:, k, :], y_lo[:, k, :]) for k in range(KT)],
                    [(g_hi[:, k, cs], g_lo[:, k, cs]) for k in range(KT)]), gw_ok, y_ok[n],
                    free[gb])
                a = free[gb] = pr.dve("gate_b", lambda e, c=c, cs=cs, gb=gb: e.tensor_tensor(
                    g[:, c, :], bank(gb), bp[:, cs], ALU.add), y_used, bp_ok, g_free[c])
                a = pr.act("gate_sig", lambda e, c=c: e.activation(g[:, c, :], g[:, c, :],
                                                                   ACT.Sigmoid), a)
                a = free[2 + c] = pr.dve("gate_p", lambda e, c=c: e.tensor_tensor(
                    g[:, c, :], g[:, c, :], bank(2 + c), ALU.mult), a, pd[c])
                g_free[c] = pr.dve("r_gate", lambda e, c=c, cs=cs: e.tensor_tensor(
                    r[:, x, cs], r[:, x, cs], g[:, c, :], ALU.add), a, y_ok[n])
                fin.append(g_free[c])
            return fin

        def leave(n, fin):
            nonlocal last_pool
            x, i = n % NR, n % 2
            mv_ok = layer_norm_stats(pr, "lo", r[:, x, :], st6[:, i, :], mv[:, i, :], fin)
            b = rstd_from_sums(pr, "lor", rl[:, i, 0:1], mv[:, i, 1:2], 1.0, LN_EPS, mv_ok)
            b = pr.dve("lo_shift", lambda e: e.scalar_tensor_tensor(
                rl[:, i, 1:2], mv[:, i, 0:1], -1.0, rl[:, i, 0:1], ALU.mult, ALU.mult), b)
            b = pr.act("o_n", lambda e: e.activation(
                r[:, x, :], r[:, x, :], ACT.Identity, scale=rl[:, i, 0:1], bias=rl[:, i, 1:2]), b)
            b = pr.pool("o_g", lambda e: e.tensor_tensor(r[:, x, :], r[:, x, :], lg[:, :], ALU.mult),
                        b, lg_ok, last_pool)
            b = last_pool = pr.pool("o_b", lambda e: e.tensor_tensor(
                r[:, x, :], r[:, x, :], lb[:, :], ALU.add), b, lb_ok)
            r_free[x] = pr.load(f"out_st{x}", t["out"][0, n * P:(n + 1) * P, :], r[:, x, :], b)

        fetch(0)
        fetch(1)
        turn_mix(0)
        weights()
        for n in range(NT + 1):
            if n < NT:
                residual(n)
            if n >= 1:
                turn_r_p(n - 1)
            if n + 1 < NT:
                turn_mix(n + 1)
            if n + 2 < NT:
                fetch(n + 2)
            if n >= 1:
                leave(n - 1, gates(n - 1))
        pr.hold("sp", r_free)
        pr.emit()


def columns(a):
    return np.ascontiguousarray(a.reshape(-1, P).T)


def laid_out(inp):
    f = {k: np.asarray(v) for k, v in inp.items()}
    pairs = {"g1": f["norm1_g"], "mixg": np.concatenate([f["ssm_norm_g"], f["pool_norm_g"]], -1),
             "pscale": f["pool_scale"], "glub": f["ssm_glu_b"], "bgate": f["b_gla_gate_2"],
             "lr": f["ssm_lambda_re"], "li": f["ssm_lambda_im"],
             "log_step": np.repeat(f["ssm_log_step"], PS)}
    at, parts, n = {}, [], 0
    for name, a in pairs.items():
        c = columns(a)
        at[name] = n
        n += c.shape[1]
        parts.append(c)
    out = {"cols": np.concatenate(parts, 1)}

    def per_pair(a):
        return a.reshape(NQ, P, H).transpose(1, 0, 2)

    out["B_re"], out["B_im"] = per_pair(f["ssm_b_re"][0]), per_pair(f["ssm_b_im"][0])
    out["C_re"] = per_pair(f["ssm_c_re"][0].transpose(0, 2, 1))
    out["C_im"] = per_pair(f["ssm_c_im"][0].transpose(0, 2, 1))
    out["d"] = f["ssm_d"][0].T
    glu = np.zeros((P, 4, P), f["ssm_glu_w"].dtype)
    for g in range(G):
        q, r = g // 8, H * (g % 8)
        glu[r:r + H, q, r:r + H] = f["ssm_glu_w"][0, g]
    out["glu_w"] = glu
    out["rows"] = np.concatenate([f[k].reshape(-1) for k in (
        "norm2_g", "final_norm_g", "ln_in_g_2", "ln_in_b_2", "b_ple_gate_2", "ln_g_2", "ln_b_2",
        "gla_norm_g_2")])
    for k in ("x", "meta_tokens", "w_in", "pool_w", "w_out", "w_gate", "w_up", "w_down", "p_2",
              "w_in_2", "w_gla_gate_2", "rel_bias_2", "w_out_2", "w_ple_2", "w_ple_gate_2"):
        out[k] = f[k]
    return {k: np.ascontiguousarray(v) for k, v in out.items()}, at


ROWS = {n: i * D for i, n in enumerate(("g2", "gf", "lin_g", "lin_b", "b_ple", "ln_g", "ln_b",
                                        "gla_g"))}


def kernel(**inputs):
    import concourse.bacc as bacc
    from concourse.bass_utils import run_bass_kernel_spmd

    nc = bacc.Bacc("TRN2", target_bir_lowering=False, num_devices=1)
    arrays, at = laid_out(inputs)
    t = {"_cols": at, "_show": ()}
    for name, a in arrays.items():
        t[name] = nc.dram_tensor(f"in_{name}", a.shape, F32, kind="ExternalInput").ap()
    t["out"] = nc.dram_tensor("out", (1, TOK, D), F32, kind="ExternalOutput").ap()
    build(nc, t)
    r = run_bass_kernel_spmd(nc, [{f"in_{k}": v for k, v in arrays.items()}], core_ids=[0])
    return r.results[0]["out"]
```

```python
import math
from contextlib import ExitStack

import numpy as np

import concourse.bass as bass
from concourse import mybir

F32 = mybir.dt.float32
F32R = mybir.dt.float32r
U32 = mybir.dt.uint32
ALU = mybir.AluOpType
ACT = mybir.ActivationFunctionType
AX = mybir.AxisListType

P = 128
D = 1024
KT = D // P
TOK = 2048
META = 16
NT = TOK // P
CH = 8
NCH = (TOK + META) // CH
MCH = META // CH
G, H, PS = 32, 16, 64
NQ = G // 2
W5 = 512
DFF = 2816
NJ = DFF // P
HALF = TOK // 2
HT = HALF // P
NWIN = 4
EPS = 1e-6
LN_EPS = 1e-5
BAND_T = 5
BAND_W = BAND_T * P
NHEAD = 8
AD = 64
CLIP = 128
EXT = 768
ALPHA = 2.0 ** 0.25
NEG = -1e30
TWO_PI_HI = 6.28125
TWO_PI_LO = 2 * math.pi - TWO_PI_HI
ROUND = 1.5 * 2.0 ** 23
PI_LOW = 3.1415925


def flat(waits):
    for w in waits:
        if isinstance(w, list):
            yield from flat(w)
        elif w is not None:
            yield w


class Program:

    def __init__(self, nc, ctx):
        self.nc, self.ctx = nc, ctx
        self.sems, self.count, self.waited = [], [], {}
        self.idle = {}
        self.fresh()

    def fresh(self):
        self.queue = {e: [] for e in ("pe", "act", "dve", "pool", "sp")}
        self.at = {}

    def _sem(self, engine, name, by):
        kind = (engine, by)
        if name in self.at:
            assert self.at[name][1] == kind, name
            return self.at[name][0]
        if self.idle.get(kind):
            n = self.idle[kind].pop(0)
        else:
            n = len(self.sems)
            self.sems.append(self.ctx.enter_context(self.nc.semaphore(
                f"{engine}_{'dma' if by == 16 else 'step'}{n}")))
            self.count.append(0)
        self.at[name] = (n, kind)
        return n

    def step(self, engine, name, run, waits, by=1):
        n = self._sem(engine, name, by)
        self.queue[engine].append((self.needed(engine, waits), run, self.sems[n], by))
        self.count[n] += by
        return (n, self.count[n])

    def needed(self, engine, waits):
        top = {}
        for n, value in flat(waits):
            top[n] = max(value, top.get(n, 0))
        need = [(n, v) for n, v in top.items() if v > self.waited.get((engine, n), 0)]
        for n, v in need:
            self.waited[(engine, n)] = v
        return [(self.sems[n], v) for n, v in need]

    def hold(self, engine, *waits):
        self.queue[engine].append((self.needed(engine, waits), None, None, 0))

    def pe(self, name, run, *waits):
        return self.step("pe", name, run, waits)

    def act(self, name, run, *waits):
        return self.step("act", name, run, waits)

    def dve(self, name, run, *waits):
        return self.step("dve", name, run, waits)

    def pool(self, name, run, *waits):
        return self.step("pool", name, run, waits)

    def load(self, name, out, in_, *waits, q="sp"):
        return self.step(q, name, lambda e: e.dma_start(out, in_), waits, 16)

    def emit(self):
        queue = self.queue

        def play(items):
            def body(eng):
                for need, run, sem, by in items:
                    for s, v in need:
                        eng.wait_ge(s, v)
                    if run is not None:
                        run(eng).then_inc(sem, by)
            return body

        with self.nc.Block() as block:
            block.sync(play(queue["sp"]))
            block.gpsimd(play(queue["pool"]))
            block.scalar(play(queue["act"]))
            block.vector(play(queue["dve"]))
            block.tensor(play(queue["pe"]))
        for n, kind in self.at.values():
            self.idle.setdefault(kind, []).append(n)
        self.fresh()


def products(e, out, lhs, rhs, first, last):
    e.matmul(out, lhs[1], rhs[0], start=first, stop=False)
    e.matmul(out, lhs[0], rhs[1], start=False, stop=False)
    return e.matmul(out, lhs[0], rhs[0], start=False, stop=last)


def contraction(out, lhs, rhs):
    def run(e):
        n = len(lhs)
        for k in range(n):
            ins = products(e, out, lhs[k], rhs[k], k == 0, k == n - 1)
        return ins
    return run


def contraction_steps(pr, name, out, lhs, rhs, by_tile, *waits):
    for k in range(len(lhs)):
        done = pr.pe(name, lambda e, k=k: products(e, out, lhs[k], rhs[k], k == 0,
                                                   k == len(lhs) - 1), by_tile[k], *waits)
    return done


def turns(out, tiles, ident):
    def run(e):
        for j, tile in enumerate(tiles):
            ins = e.transpose(out[:, j * P:(j + 1) * P], tile, ident[:, :])
        return ins
    return run


def split_pair(pr, tag, hi, lo, src, *waits):
    a = pr.act(f"{tag}_hi", lambda e: e.activation(hi, src, ACT.Copy), *waits)
    return pr.dve(f"{tag}_lo", lambda e: e.tensor_tensor(lo, src, hi.bitcast(F32), ALU.subtract),
                  a, *waits)


def spread(ap, n):
    return bass.AP(tensor=ap.tensor, offset=ap.offset, ap=[list(x) for x in ap.ap] + [[0, n]])


def last_of(fns):
    def run(e):
        for f in fns:
            ins = f(e)
        return ins
    return run


def mm(out, l, r, first=True, last=True):
    return lambda e: e.matmul(out, l, r, start=first, stop=last)


def build(nc, t):
    ctx = ExitStack()
    with ctx:
        pr = Program(nc, ctx)
        dram = {}

        def scratch(name, shape):
            dram[name] = nc.dram_tensor(name, shape, F32, kind="Internal")
            return dram[name]

        uses = {}

        def sb(stack, name, shape, dt=F32, side=None):
            uses[name] = uses.get(name, 0) + 1
            n = name if uses[name] == 1 else f"{name}_{uses[name]}"
            return stack.enter_context(nc.sbuf_tensor(n, shape, dt, side=side))

        rs2 = sb(ctx, "rs2", [P, NT])
        h1 = scratch("h1", [TOK, D])
        h2 = scratch("h2", [TOK, D])
        u_meta = scratch("u_meta", [META, W5])
        banks = [ctx.enter_context(nc.psum_tensor(f"bank{i}", [P, 2, W5], F32)) for i in range(4)]

        def bank(i):
            return banks[i // 2][:, i % 2, :]

        ident = sb(ctx, "ident", [P, P])
        cols = sb(ctx, "cols", [P, t["cols"].shape[1]])
        c_at = t["_cols"]

        def col(name, i=0, n=1):
            return cols[:, c_at[name] + i:c_at[name] + i + n]

        z0 = pr.pool("ident_zero", lambda e: e.memset(ident[:, :], 0.0))
        ident_ok = pr.pool("ident", lambda e: e.affine_select(
            out=ident[:, :], in_=ident[:, :], compare_op=ALU.not_equal, fill=1.0, base=0,
            pattern=[[-1, P]], channel_multiplier=1), z0)
        cols_ok = pr.load("cols_in", cols[:, :], t["cols"])
        env = dict(pr=pr, sb=sb, scratch=scratch, dram=dram, bank=bank, banks=banks, ident=ident,
                   col=col, t=t, ident_ok=ident_ok, cols_ok=cols_ok, h1=h1, h2=h2, u_meta=u_meta,
                   nc=nc, ctx=ctx, rs2=rs2)
        block1_mixers(env)
        feed_forward(env)
        band_attention(env)
        out_w = [sb(ctx, f"ow_{n}", [P, KT, D], F32R, "right") for n in ("hi", "lo")]
        ple_w = [sb(ctx, f"oq_{n}", [P, 2, D], F32R, "right") for n in ("hi", "lo")]
        gated_linear_attention(env, out_w, ple_w)
        output_block(env, out_w, ple_w)


def rstd_from_sums(pr, tag, out, tmp, scale, eps, *waits):
    a = pr.dve(f"{tag}_ms", lambda e: e.tensor_scalar(tmp, tmp, scale, eps, ALU.mult, ALU.add), *waits)
    b = pr.act(f"{tag}_root", lambda e: e.activation(tmp, tmp, ACT.Sqrt), a)
    return pr.dve(f"{tag}_rstd", lambda e: e.reciprocal(out, tmp), b)


def block1_mixers(env):
    sb = env["sb"]
    with ExitStack() as right:
        with ExitStack() as left:
            vT = sb(left, "vT", [P, NWIN, META + TOK])
            with ExitStack() as keep_u:
                u_grp = sb(keep_u, "u_grp", [P, 2, G, CH, H])
                input_projection(env, u_grp, vT)
                g_tok = ssm(env, right, u_grp)
            yT = sb(right, "yT", [P, KT, TOK], side="right")
            gate_and_pool(env, g_tok, vT, yT)
        w_out_stage(env, yT)


def input_projection(env, u_grp, vT):
    pr, sb, t, bank, ident, col = (env[k] for k in ("pr", "sb", "t", "bank", "ident", "col"))
    ident_ok, cols_ok = env["ident_ok"], env["cols_ok"]
    NX = 3
    with ExitStack() as st:
        w_hi = sb(st, "win_hi", [P, KT, D], F32R)
        w_lo = sb(st, "win_lo", [P, KT, D], F32R)
        w_st = sb(st, "win_stage", [P, 2, D])
        xr = sb(st, "x_ring", [P, NX, D])
        xT_hi = sb(st, "xT_hi", [P, 2, KT, P], F32R)
        xT_lo = sb(st, "xT_lo", [P, 2, KT, P], F32R)
        v_tok = sb(st, "v_tok", [P, 2, W5])
        um = sb(st, "um", [P, W5])
        junk = sb(st, "sq_junk", [P, D])
        ss = sb(st, "ss", [P, NT + 1])
        rs = sb(st, "rs", [P, NT + 1])

        xv = t["x"][0].rearrange("(b p s) d -> b s p d", b=2, s=CH)
        meta_zero = pr.dve("meta_zero", lambda e: e.memset(xr[:, 0, :], 0.0))
        split = []

        def split_w(k):
            i = k % 2
            ld = pr.load(f"win_in{i}", w_st[:, i, :], t["w_in"][0, k * P:(k + 1) * P, :],
                         split[k - 2] if k >= 2 else None)
            hi = pr.act("win_hi", lambda e: e.activation(
                w_hi[:, k, :], w_st[:, i, :], ACT.Copy, scale=col("g1", k)), ld, cols_ok)
            split.append(pr.dve("win_lo", lambda e: e.scalar_tensor_tensor(
                w_lo[:, k, :], w_st[:, i, :], col("g1", k), w_hi[:, k, :].bitcast(F32),
                ALU.mult, ALU.subtract), hi, ld, cols_ok))

        tiles = [-1] + list(range(NT))
        loaded, slot_free, rs_ok = {}, {}, {}
        turned, xT_free, xT_ok = [None, None], [None, None], {}
        uv_free, v_ok, v_free, vt_free = [None, None], {}, [None, None], [None, None]

        def fetch(n):
            i, r = n % NX, tiles[n]
            if r < 0:
                loaded[n] = pr.load(f"x_in{i}", xr[0:META, i, :], t["meta_tokens"], meta_zero)
            else:
                loaded[n] = pr.load(f"x_in{i}", xr[:, i, :], xv[r // CH, r % CH], slot_free.get(i))

        def turn(n):
            i, x2 = n % NX, n % 2
            ready = [loaded[n], meta_zero]
            sq = pr.act("x_sq", lambda e: e.activation(
                junk[:, :], xr[:, i, :], ACT.Square, accum_out=ss[:, n:n + 1]), ready)
            oks = []
            for g in range(2):
                tr = pr.pe("x_turn", turns(bank(g), [xr[:, i, k * P:(k + 1) * P]
                                                     for k in range(4 * g, 4 * g + 4)], ident),
                           ready, ident_ok, turned[g])
                src = bank(g).rearrange("p (j c) -> p j c", j=4)
                turned[g] = split_pair(pr, "xT", xT_hi[:, x2, 4 * g:4 * g + 4, :],
                                       xT_lo[:, x2, 4 * g:4 * g + 4, :], src, tr, xT_free[x2])
                oks.append(turned[g])
            slot_free[i] = [sq, tr]
            xT_ok[n] = oks
            rs_ok[n] = sq

        def roots(ns):
            a, b = ns[0], ns[-1] + 1
            ok = rstd_from_sums(pr, "n1", rs[:, a:b], ss[:, a:b], 1.0 / D, EPS, rs_ok[ns[-1]])
            for n in ns:
                rs_ok[n] = ok

        def multiply(n):
            x2, r = n % 2, tiles[n]
            outs = [bank(2 + 2 * x2), bank(3 + 2 * x2)]
            done = []
            for part in range(2):
                cs = slice(part * W5, (part + 1) * W5)
                lhs = [(xT_hi[:, x2, k, :], xT_lo[:, x2, k, :]) for k in range(KT)]
                rhs = [(w_hi[:, k, cs], w_lo[:, k, cs]) for k in range(KT)]
                if n == 0:
                    done.append(contraction_steps(pr, "win_mm", outs[part], lhs, rhs, split,
                                                  xT_ok[n]))
                else:
                    done.append(pr.pe("win_mm", contraction(outs[part], lhs, rhs), xT_ok[n],
                                      uv_free[x2]))
            xT_free[x2] = done[1]
            scale = rs[:, n:n + 1]
            dst, src = um[:, :], outs[0]
            if r >= 0:
                dst = u_grp[:, r // CH, :, r % CH, :]
                src = src.rearrange("p (g h) -> p g h", h=H)
            u = pr.act("u_out", lambda e: e.activation(dst, src, ACT.Copy, scale=scale),
                       done[0], rs_ok[n])
            if r < 0:
                env["u_meta_ok"] = pr.load("u_meta_st", env["u_meta"][:, :], um[0:META, :], u,
                                           q="pool")
            v_ok[n] = pr.dve("v_out", lambda e: e.tensor_scalar(
                v_tok[:, x2, :], outs[1], scale, None, ALU.mult), done[1], rs_ok[n], v_free[x2])
            uv_free[x2] = [u, v_ok[n]]

        def turn_v(n):
            x2, r = n % 2, tiles[n]
            tb = bank(6 + x2)
            vt = pr.pe("v_turn", turns(tb, [v_tok[:, x2, j * P:(j + 1) * P] for j in range(NWIN)],
                                       ident), v_ok[n], vt_free[x2])
            src = tb.rearrange("p (j c) -> p j c", j=NWIN)
            if r < 0:
                dst, src = vT[:, :, 0:META], src[:, :, 0:META]
            else:
                lo = META + (r // CH) * HALF + r % CH
                dst = vT[:, :, lo:lo + CH * (P - 1) + 1:CH]
            v_free[x2] = vt
            vt_free[x2] = pr.dve("vT_out", lambda e: e.tensor_copy(dst, src), vt)

        n_all = len(tiles)
        fetch(0)
        fetch(1)
        for k in range(KT):
            split_w(k)
            if k == 2:
                turn(0)
                fetch(2)
        skew_st = skewed_bias(env, st)
        for n in range(1, n_all + 2):
            if n < n_all:
                turn(n)
                if n + 2 < n_all:
                    fetch(n + 2)
            if n == 1:
                roots([0, 1])
            elif n < n_all:
                roots([n])
            if 1 <= n <= n_all:
                multiply(n - 1)
            if n >= 2:
                turn_v(n - 2)
        pr.hold("sp", env["u_meta_ok"], skew_st)
        pr.emit()


def ssm(env, right, u_grp):
    with ExitStack() as st:
        pr, sb = env["pr"], env["sb"]
        tab = dict(
            Vr=sb(st, "Vr", [P, NQ, (CH + 1) * H]), Vi=sb(st, "Vi", [P, NQ, (CH + 1) * H]),
            Er=sb(st, "Er", [P, NQ, P]), Ei=sb(st, "Ei", [P, NQ, P]),
            M=sb(st, "M_intra", [P, G, P]),
            Tc=sb(st, "Tc", [P, NQ, NCH]), Ts=sb(st, "Ts", [P, NQ, NCH]),
            rho=sb(st, "rho", [P, NQ]),
            um8=sb(st, "um8", [P, MCH, G]))
        ssm_tables(env, tab)
        g_tok = sb(right, "g_tok", [P, 2, CH, W5], F32, "right")
        ssm_run(env, tab, u_grp, g_tok)
    return g_tok


def ssm_tables(env, tab):
    pr, sb, t, bank, ident, col = (env[k] for k in ("pr", "sb", "t", "bank", "ident", "col"))
    TW = 64
    with ExitStack() as st:
        W = [sb(st, f"W{c}", [P, NQ, CH, H]) for c in "ri"]
        tmp = sb(st, "tab_tmp", [P, 4, NQ * H])
        T_tmp = sb(st, "T_tmp", [P, 4, NQ * TW])
        K = sb(st, "K", [P, G, P])
        B = [sb(st, f"B{c}", [P, NQ, H]) for c in "ri"]
        bb = [sb(st, f"Bbar{c}", [P, NQ, H]) for c in "ri"]
        sm = sb(st, "tab_small", [P, 24, NQ])
        d_sb = sb(st, "d_sb", [H, G])
        dd = sb(st, "d_diag", [H, G, H])
        s_ = [sm[:, i, :] for i in range(24)]
        (step, mag, ang, c1, sn, ar, ai, nai, nr, den, cr, ci, t1, t2, t3, t4, rd, r1, r2, kq, lr,
         wr, wi, _) = s_
        Vr, Vi = (tab[k][:, :, :].rearrange("p q (j h) -> p q j h", h=H) for k in ("Vr", "Vi"))
        in_ok = [pr.load("B_in", B[0][:, :, :], t["B_re"]), pr.load("B_in", B[1][:, :, :], t["B_im"]),
                 pr.load("B_in", Vr[:, :, 0, :], t["C_re"]), pr.load("B_in", Vi[:, :, 0, :], t["C_im"]),
                 pr.load("B_in", d_sb[:, :], t["d"])]
        um = env["u_meta"]
        for c in range(MCH):
            for s in range(CH):
                um_ok = pr.load("um8_in", tab["um8"][H * s:H * (s + 1), c, :], bass.AP(
                    tensor=um[:, :].tensor, offset=(c * CH + s) * W5, ap=[[1, H], [H, G]]))
        chain, g_chain = [None], [None]

        def v(fn, *waits):
            chain[0] = pr.dve("tables", fn, chain[0], *waits)

        def a(fn, *waits):
            chain[0] = pr.act("tables_act", fn, chain[0], *waits)

        def tt(o, x, y, op, *waits):
            v(lambda e: e.tensor_tensor(o, x, y, op), *waits)

        def ts(o, x, k1, k2, op1, op2, *waits):
            v(lambda e: e.tensor_scalar(o, x, k1, k2, op1, op2), *waits)

        def stt(o, x, k, y, op1, op2):
            v(lambda e: e.scalar_tensor_tensor(o, x, k, y, op1, op2))

        def gt(o, x, y, op, *waits):
            g_chain[0] = pr.pool("T_table", lambda e: e.tensor_tensor(o, x, y, op), g_chain[0],
                                 *waits)

        def complex_product(outr, outi, xr, xi, yr, yi, tmps, tt=tt):
            p1, p2, p3, p4 = tmps
            tt(p1, xr, yr, ALU.mult)
            tt(p2, xi, yi, ALU.mult)
            tt(p3, xr, yi, ALU.mult)
            tt(p4, xi, yr, ALU.mult)
            tt(outr, p1, p2, ALU.subtract)
            tt(outi, p3, p4, ALU.add)

        def reduced_sin(out, shift):
            ts(kq, ang, shift, 1 / (2 * math.pi), ALU.add, ALU.mult)
            ts(kq, kq, ROUND, None, ALU.add, ALU.bypass)
            ts(kq, kq, ROUND, None, ALU.subtract, ALU.bypass)
            stt(r1, kq, -TWO_PI_HI, ang, ALU.mult, ALU.add)
            stt(r1, kq, -TWO_PI_LO, r1, ALU.mult, ALU.add)
            ts(r1, r1, shift, None, ALU.add, ALU.bypass)
            ts(r1, r1, PI_LOW, -PI_LOW, ALU.min, ALU.max)
            a(lambda e: e.activation(out, r1, ACT.Sin))

        ts(lr, col("lr", 0, NQ), -1e-4, None, ALU.min, ALU.bypass, env["cols_ok"])
        li = col("li", 0, NQ)
        a(lambda e: e.activation(step, col("log_step", 0, NQ), ACT.Exp))
        tt(t1, lr, step, ALU.mult)
        a(lambda e: e.activation(mag, t1, ACT.Exp))
        a(lambda e: e.activation(tab["rho"][:, :], t1, ACT.Exp, scale=float(CH)))
        tt(ang, li, step, ALU.mult)
        reduced_sin(sn, 0.0)
        reduced_sin(c1, math.pi / 2)
        tt(ar, mag, c1, ALU.mult)
        tt(ai, mag, sn, ALU.mult)
        ts(nai, ai, -1.0, None, ALU.mult, ALU.bypass)
        ts(nr, ar, -1.0, None, ALU.add, ALU.bypass)
        tt(den, lr, lr, ALU.mult)
        tt(t1, li, li, ALU.mult)
        tt(den, den, t1, ALU.add)
        v(lambda e: e.reciprocal(rd, den))
        tt(t1, nr, lr, ALU.mult)
        tt(t2, ai, li, ALU.mult)
        tt(t1, t1, t2, ALU.add)
        tt(cr, t1, rd, ALU.mult)
        tt(t1, ai, lr, ALU.mult)
        tt(t2, nr, li, ALU.mult)
        tt(t1, t1, t2, ALU.subtract)
        tt(ci, t1, rd, ALU.mult)

        def over(x, n):
            return spread(x, n)

        def tmps(n, buf):
            return [buf[:, i, 0:NQ * n].rearrange("p (q n) -> p q n", q=NQ) for i in range(4)]

        t16 = tmps(H, tmp)
        pr_wait = in_ok
        tt(bb[0][:, :, :], B[0][:, :, :], over(cr, H), ALU.mult, pr_wait)
        complex_product(bb[0][:, :, :], bb[1][:, :, :], over(cr, H), over(ci, H),
                        B[0][:, :, :], B[1][:, :, :], t16)
        small_ok = chain[0]
        m_zero = pr.pool("M_zero", lambda e: e.memset(tab["M"][:, :, :], 0.0))

        def gt_first(o, x, y, op):
            gt(o, x, y, op, small_ok)

        small = tmps(1, T_tmp)
        squares = [x[:, :, 0] for x in small]
        complex_product(wr, wi, c1, sn, c1, sn, squares, tt=gt_first)
        complex_product(wr, wi, wr, wi, wr, wi, squares, tt=gt)
        complex_product(wr, wi, wr, wi, wr, wi, squares, tt=gt)
        Tc, Ts = tab["Tc"], tab["Ts"]

        def g(fn):
            g_chain[0] = pr.pool("T_table", fn, g_chain[0])

        g(lambda e: e.memset(Tc[:, :, 0], 1.0))
        g(lambda e: e.memset(Ts[:, :, 0], 0.0))
        g(lambda e: e.tensor_copy(Tc[:, :, 1], wr))
        g(lambda e: e.tensor_copy(Ts[:, :, 1], wi))
        n = 2
        while n < NCH:
            h = n // 2
            complex_product(Tc[:, :, n], Ts[:, :, n], Tc[:, :, h], Ts[:, :, h], Tc[:, :, h],
                            Ts[:, :, h], squares, tt=gt)
            m = min(n, NCH - n)
            if m > TW:
                g_half = g_chain[0]
            for lo in range(1, min(m, TW + 1), TW):
                hi = min(lo + TW, m)
                complex_product(Tc[:, :, n + lo:n + hi], Ts[:, :, n + lo:n + hi],
                                Tc[:, :, lo:hi], Ts[:, :, lo:hi], over(Tc[:, :, n], hi - lo),
                                over(Ts[:, :, n], hi - lo), tmps(hi - lo, T_tmp), tt=gt)
            n *= 2
        ts(Vi[:, :, 0, :], Vi[:, :, 0, :], -1.0, None, ALU.mult, ALU.bypass)
        for j in range(CH):
            complex_product(Vr[:, :, j + 1, :], Vi[:, :, j + 1, :], over(ar, H), over(nai, H),
                            Vr[:, :, j, :], Vi[:, :, j, :], t16)
        v_ok = chain[0]
        k_ok = []
        kfree = [None, None]
        for g0 in range(0, G, 8):
            b = 4 + 2 * ((g0 // 8) % 2)
            for side in range(2):
                fns = []
                rows = slice(PS * side, PS * (side + 1))
                for j in range(4):
                    o, q = bank(b + side)[0:H, j * P:(j + 1) * P], g0 // 2 + j
                    for c, V in ((0, tab["Vr"]), (1, tab["Vi"])):
                        fns.append(mm(o, bb[c][rows, q, :], V[rows, q, 0:P], c == 0, c == 1))
                done = pr.pe("K_mm", last_of(fns), v_ok, kfree[(g0 // 8) % 2])
                k_ok.append(pr.act("K_out", lambda e, b=b, g0=g0, side=side: e.activation(
                    K[0:H, g0 + side:g0 + 8:2, :],
                    bank(b + side)[0:H, :].rearrange("p (j c) -> p j c", j=4), ACT.Copy),
                    done))
            kfree[(g0 // 8) % 2] = k_ok[-2:]
        for c in range(2):
            v(lambda e, c=c: e.tensor_copy(W[c][:, :, CH - 1, :], bb[c][:, :, :]))
        for s in range(CH - 1, 0, -1):
            complex_product(W[0][:, :, s - 1, :], W[1][:, :, s - 1, :], over(ar, H), over(ai, H),
                            W[0][:, :, s, :], W[1][:, :, s, :], t16)
        w_ok = chain[0]
        k_all = list(k_ok)
        tt(dd[:, :, :], over(d_sb[:, :], H), bass.AP(
            tensor=ident[:, :].tensor, offset=ident[:, :].offset,
            ap=[list(ident[0:H, :].ap[0]), [0, G], [1, H]]), ALU.mult)
        tt(K[0:H, :, 0:H], K[0:H, :, 0:H], dd[:, :, :], ALU.add, k_all)
        k_ok = chain[0]
        for s in range(CH):
            tab["M_ok"] = pr.load("M_in", tab["M"][H * s:H * (s + 1), :, H * s:P],
                                  K[0:H, :, 0:P - H * s], k_ok, m_zero, k_all)
        n, m = NCH // 2 // TW * TW, 2 * TW
        chain[0] = [chain[0], g_half]
        for lo in range(TW + 1, m, H):
            hi = min(lo + H, m)
            complex_product(Tc[:, :, n + lo:n + hi], Ts[:, :, n + lo:n + hi], Tc[:, :, lo:hi],
                            Ts[:, :, lo:hi], over(Tc[:, :, n], hi - lo), over(Ts[:, :, n], hi - lo),
                            tmps(hi - lo, tmp))
        free = [None] * 4
        n = 0
        e_ok = []
        for c, E in ((0, tab["Er"]), (1, tab["Ei"])):
            for q0 in range(0, NQ, 4):
                b = n % 4
                tr = pr.pe("E_turn", turns(bank(b), [W[c][:, q, :, :] for q in range(q0, q0 + 4)],
                                           ident), w_ok, env["ident_ok"], free[b])
                free[b] = pr.act("E_out", lambda e, E=E, q0=q0, b=b: e.activation(
                    E[:, q0:q0 + 4, :], bank(b).rearrange("p (j c) -> p j c", j=4), ACT.Copy), tr)
                n += 1
        e_ok = free[(n - 1) % 4]
        tab.update(ok=chain[0], e_ok=e_ok)
        pr.hold("sp", tab["M_ok"], um_ok)
        with env["nc"].allow_non_contiguous_dma(reason="the meta tokens' 8192 values"):
            pr.emit()


def ssm_run(env, tab, u_grp, g_tok):
    pr, sb, t, bank, ident = (env[k] for k in ("pr", "sb", "t", "bank", "ident"))
    with ExitStack() as st:
        um8 = tab["um8"]
        U = sb(st, "U_ring", [P, 3, 2, NCH])
        z = sb(st, "z", [P, 4, NCH])
        R = sb(st, "R_ring", [P, 2, 2, NCH])
        S = sb(st, "S_ring", [P, 3, 2, NCH - MCH])
        zz = sb(st, "S_tmp", [P, 4, NCH - MCH])
        y = sb(st, "y_ring", [P, 2, 2, 2 * P])
        NX1 = NCH - 1
        Ur, X_ok, U_ok, S_ok, y_ok, z_ok = {}, {}, {}, {}, {}, {}
        U_free, x_free, R_free, S_free = [None] * 3, [None] * 2, [None] * 2, [None] * 3
        y_free, ut_free, yb_free, yt_free = [None] * 2, [None] * 2, [None], [None]
        last = [None]

        def enter(q):
            i, j = q % 2, q % 3
            ub = bank(0)
            tiles = [u_grp[:, b, g, :, :] for g in (2 * q, 2 * q + 1) for b in range(2)]
            tr = pr.pe("U_turn", turns(ub, tiles, ident), ut_free[0])
            c = pr.act("U_out", lambda e: e.activation(
                U[:, j, :, MCH:NCH], ub.rearrange("p (g c) -> p g c", g=2), ACT.Copy),
                tr, U_free[j])
            m = pr.dve("U_meta", lambda e: e.tensor_copy(
                U[:, j, :, 0:MCH], um8[:, :, 2 * q:2 * q + 2].rearrange("p c g -> p g c")), U_free[j])
            ut_free[0] = c
            U_ok[q] = [c, m]
            Ur[q] = tr
            fns = []
            for r, E in ((0, tab["Er"]), (1, tab["Ei"])):
                for g in range(2):
                    fns.append(mm(bank(2 + 2 * i + r)[PS * g:PS * (g + 1), 0:NX1],
                                  E[:, q, PS * g:PS * (g + 1)], U[:, j, g, 0:NX1]))
            X_ok[q] = pr.pe("X_mm", last_of(fns), U_ok[q], x_free[i])

        def recur(q):
            i, j = q % 2, q % 3
            xr, xi = bank(2 + 2 * i)[:, 0:NX1], bank(3 + 2 * i)[:, 0:NX1]
            c, s = tab["Tc"][:, q, 1:NCH], tab["Ts"][:, q, 1:NCH]
            z_ = [z[:, k, 0:NX1] for k in range(4)]

            def tt(o, a, b, op, *w):
                return pr.dve("turn_in", lambda e: e.tensor_tensor(o, a, b, op), *w)

            tt(z_[0], xr, c, ALU.mult, X_ok[q], tab["ok"])
            a2 = tt(z_[1], xi, s, ALU.mult)
            tt(z_[2], xi, c, ALU.mult)
            x_free[i] = a4 = tt(z_[3], xr, s, ALU.mult)
            tt(z_[0], z_[0], z_[1], ALU.add, a2)
            a6 = tt(z_[2], z_[2], z_[3], ALU.subtract, a4)
            rho = bass.AP(tensor=tab["rho"][:, :].tensor, offset=tab["rho"][:, q:q + 1].offset,
                          ap=[list(tab["rho"][:, q:q + 1].ap[0]), [0, NX1]])
            for k in range(2):
                r_ok = pr.dve("scan", lambda e, k=k: e.tensor_tensor_scan(
                    R[:, i, k, 0:NX1], rho, z_[2 * k], 0.0, ALU.mult, ALU.add), a6, R_free[i])
            c2, s2 = tab["Tc"][:, q, MCH:NCH], tab["Ts"][:, q, MCH:NCH]
            Rr, Ri = R[:, i, 0, 1:NX1], R[:, i, 1, 1:NX1]
            w = [zz[:, k, 0:NCH - MCH] for k in range(4)]

            def gt(o, a, b, op, *ws):
                last[0] = pr.pool("turn_back", lambda e: e.tensor_tensor(o, a, b, op), last[0], *ws)
                return last[0]

            gt(w[0], Rr, c2, ALU.mult, r_ok)
            g2 = gt(w[1], Ri, s2, ALU.mult)
            gt(w[2], Rr, s2, ALU.mult)
            R_free[i] = g4 = gt(w[3], Ri, c2, ALU.mult)
            gt(S[:, j, 0, 0:NCH - MCH], w[0], w[1], ALU.subtract, g2, S_free[j])
            S_ok[q] = gt(S[:, j, 1, 0:NCH - MCH], w[2], w[3], ALU.add, g4)

        def leave(q):
            i, j = q % 2, q % 3
            n = NCH - MCH
            fns = []
            for g in range(2):
                o, rows = bank(6 + g)[:, 0:n], slice(PS * g, PS * (g + 1))
                fns.append(mm(o, tab["M"][:, 2 * q + g, :], U[:, j, g, MCH:NCH], True, False))
                fns.append(mm(o, tab["Vr"][rows, q, H:H + P], S[rows, j, 0, 0:n], False, False))
                fns.append(mm(o, tab["Vi"][rows, q, H:H + P], S[rows, j, 1, 0:n], False, True))
            done = pr.pe("y_mm", last_of(fns), S_ok[q], tab["M_ok"], U_ok[q], yb_free[0])
            U_free[j] = S_free[j] = done
            y_ok[q] = yb_free[0] = pr.act("gelu", lambda e: e.activation(
                y[:, i, :, :], env["banks"][3][:, :, 0:n], ACT.Gelu_apprx_tanh),
                done, y_free[i])

        def back(q):
            i = q % 2
            tb = bank(1)
            tr = pr.pe("y_turn", turns(tb, [y[:, i, g, b * P:(b + 1) * P] for g in range(2)
                                            for b in range(2)], ident), y_ok[q], yt_free[0])
            y_free[i] = tr
            src = tb.rearrange("p (g b s h) -> p g b s h", g=2, b=2, s=CH)
            for b in range(2):
                dst = g_tok[:, b, :, 2 * H * q:2 * H * (q + 1)].rearrange("p s (g h) -> p g s h", g=2)
                yt_free[0] = pr.act("y_out", lambda e, b=b, dst=dst: e.activation(
                    dst, src[:, :, b, :, :], ACT.Copy), tr)

        for q in range(NQ + 3):
            if q < NQ:
                enter(q)
                recur(q)
            if 2 <= q < NQ + 2:
                leave(q - 2)
            if q >= 3:
                back(q - 3)
        pr.emit()


def gate_and_pool(env, g_tok, vT, yT):
    pr, sb, t, bank, ident, col = (env[k] for k in ("pr", "sb", "t", "bank", "ident", "col"))
    L = META + TOK
    with ExitStack() as st:
        win = [sb(st, f"win_{c}", [P, L]) for c in "ab"]
        p = sb(st, "pooled", [P, 2, TOK])
        gT = sb(st, "gT", [P, 2, W5])
        sg = sb(st, "sg", [P, 2, W5])
        pw = sb(st, "pool_w_sb", [P, NWIN, P])
        gw = sb(st, "glu_w_sb", [P, 4, P])
        gw_ok = pr.load("glu_w_in", gw[:, :, :], t["glu_w"])
        pw_ok = pr.load("pool_w_in", pw[:, :, :], t["pool_w"][0].rearrange("k c d -> c k d"))
        turn_free, glu_free, g_free, s_free = ([None] * 2 for _ in range(4))
        pool_free, p_free, p_ok = [None] * 4, [None] * 2, {}
        chain = None

        def window_steps(k):
            w, cur, d, bufs, steps = 2 << k, vT[:, k, :], 1, [win[0][:, :], win[1][:, :]], []

            def double(nxt, cur, d):
                def go():
                    nonlocal chain
                    s0 = 2 * d - 1
                    chain = pr.dve("window", lambda e: e.tensor_tensor(
                        nxt[:, s0:L], cur[:, s0:L], cur[:, s0 - d:L - d], ALU.add), chain)
                return go

            while d < w:
                nxt = bufs[0]
                bufs.reverse()
                steps.append(double(nxt, cur, d))
                cur, d = nxt, 2 * d

            def less(cur):
                def go():
                    nonlocal chain
                    chain = p_ok[k] = pr.dve("pooled", lambda e: e.scalar_tensor_tensor(
                        p[:, k % 2, :], cur[:, META:L], 1.0 / w, vT[:, k, META:L], ALU.mult,
                        ALU.subtract), chain, p_free[k % 2])
                return go

            return steps + [less(cur)]

        def pool_product(k, n):
            mmd = p_free[k % 2] = pr.pe("pool_mm", mm(
                bank(4 + n), pw[:, k, :], p[:, k % 2, n * W5:(n + 1) * W5]), p_ok[k], pw_ok,
                pool_free[n])
            dst = yT[:, 4 + k, :].rearrange("d (b s p) -> d b p s", b=2, s=CH)[
                :, n // 2, 64 * (n % 2):64 * (n % 2) + 64, :]
            pool_free[n] = pr.act("yp_out", lambda e: e.activation(
                dst, bank(4 + n).rearrange("d (p s) -> d p s", s=CH), ACT.Copy,
                scale=col("pscale", k)), mmd)

        def turn_g(n):
            q, m = divmod(n, 4)
            i = n % 2
            tr = pr.pe("g_turn", turns(bank(i), [g_tok[:, r // CH, r % CH, q * P:(q + 1) * P]
                                                 for r in range(4 * m, 4 * m + 4)], ident),
                       turn_free[i])
            turn_free[i] = pr.act("gT_out", lambda e: e.activation(
                gT[:, i, :], bank(i), ACT.Copy), tr, g_free[i])

        def gate(n):
            q, m = divmod(n, 4)
            i = n % 2
            done = pr.pe("glu_mm", mm(bank(2 + i), gw[:, q, :], gT[:, i, :]), turn_free[i], gw_ok,
                         glu_free[i])
            glu_free[i] = pr.act("glu_sig", lambda e: e.activation(
                sg[:, i, :], bank(2 + i), ACT.Sigmoid, bias=col("glub", q)), done, s_free[i])
            s_free[i] = pr.dve("ys_out", lambda e: e.tensor_tensor(
                yT[:, q, m * W5:(m + 1) * W5], gT[:, i, :], sg[:, i, :], ALU.mult), glu_free[i])
            g_free[i] = [s_free[i], done]

        for go in window_steps(0):
            go()
        steps = []
        for n in range(17):
            k, m = divmod(n, 4)
            if m == 0 and k + 1 < NWIN:
                steps += window_steps(k + 1)
            if n < 16:
                turn_g(n)
                pool_product(k, m)
            if n >= 1:
                gate(n - 1)
            for _ in range(2 if m == 3 and len(steps) > 1 else 1):
                if steps:
                    steps.pop(0)()
        pr.emit()


def skewed_bias(env, st):
    pr, sb, t = env["pr"], env["sb"], env["t"]
    ext_d = env["scratch"]("ext", [NHEAD, EXT])
    skew = env["skew"] = env["scratch"]("skew", [NHEAD, P, EXT])
    n_rel = 2 * CLIP + 1
    rel = sb(st, "rel", [NHEAD, n_rel])
    ext = sb(st, "ext_sb", [NHEAD, EXT])
    r_ok = pr.load("rel_in", rel[:, :], t["rel_bias_2"][0])
    flat_n = EXT - n_rel
    a_ = rel[:, :]
    e1 = pr.dve("ext", lambda e: e.tensor_scalar(ext[:, 0:flat_n], bass.AP(
        tensor=a_.tensor, offset=a_.offset + n_rel - 1, ap=[list(a_.ap[0]), [0, flat_n]]),
        -1.0, None, ALU.mult, ALU.bypass), r_ok)
    e2 = pr.dve("ext", lambda e: e.tensor_scalar(ext[:, flat_n:EXT], bass.AP(
        tensor=a_.tensor, offset=a_.offset + n_rel - 1, ap=[list(a_.ap[0]), [-1, n_rel]]),
        -1.0, None, ALU.mult, ALU.bypass), e1)
    s1 = pr.load("ext_st", ext_d[:, :], ext[:, :], e2, q="pool")
    return pr.load("skew_st", skew[:, :, :], bass.AP(
        tensor=ext_d[:, :].tensor, offset=0, ap=[[EXT, NHEAD], [0, P], [1, EXT]]), s1, q="pool")


def w_out_stage(env, yT):
    pr, sb, t, bank, col = (env[k] for k in ("pr", "sb", "t", "bank", "col"))
    NX, NB = 3, 7
    with ExitStack() as st:
        w_hi = sb(st, "wout_hi", [P, KT, D], F32R)
        w_lo = sb(st, "wout_lo", [P, KT, D], F32R)
        w_st = sb(st, "wout_stage", [P, 2, D])
        y_hi = sb(st, "y_hi", [P, 2, KT, P], F32R)
        y_lo = sb(st, "y_lo", [P, 2, KT, P], F32R)
        sq = sb(st, "y_sq", [P, KT, P])
        s4 = sb(st, "y_sq4", [P, 2, 2, P])
        s2 = sb(st, "y_sq2", [P, 2, P])
        rs = sb(st, "rs_mix", [P, NT, 2])
        ones = sb(st, "ones_col", [P, 1])
        xr = sb(st, "x_res", [P, NX, D])
        rs2 = env["rs2"][:, :]
        xv = t["x"][0].rearrange("(b p s) d -> b s p d", b=2, s=CH)
        hv = env["h1"][:, :].rearrange("(b p s) d -> b s p d", b=2, s=CH)
        one_ok = pr.pool("ones_col", lambda e: e.memset(ones[:, :], 1.0))
        w_ok, st_free, x_free, x_in = [], [None] * 2, [None] * NX, {}
        y_ok, y_used, rs_ok, free = {}, [None] * 2, {}, [None] * NB
        sq_free, s4_free, s2_free, sum_free = None, None, None, None
        cnt = 0

        def fetch(n):
            x_in[n] = pr.load(f"x_res_in{n % NX}", xr[:, n % NX, :], xv[n // CH, n % CH],
                              x_free[n % NX])

        def split_w(k):
            i = k % 2
            ld = pr.load(f"wout_in{i}", w_st[:, i, :], t["w_out"][0, k * P:(k + 1) * P, :],
                         st_free[i])
            a = pr.act("wout_hi", lambda e: e.activation(
                w_hi[:, k, :], w_st[:, i, :], ACT.Copy, scale=col("mixg", k)), ld)
            st_free[i] = pr.dve("wout_lo", lambda e: e.scalar_tensor_tensor(
                w_lo[:, k, :], w_st[:, i, :], col("mixg", k), w_hi[:, k, :].bitcast(F32),
                ALU.mult, ALU.subtract), a)
            w_ok.append(st_free[i])

        def split_y(n):
            nonlocal sq_free, s4_free
            i, src = n % 2, yT[:, :, n * P:(n + 1) * P]
            y_ok[n] = split_pair(pr, "y", y_hi[:, i], y_lo[:, i], src, y_used[i])
            a = pr.act("y_sq", lambda e: e.activation(sq[:, :, :], src, ACT.Square), sq_free)
            four = sq[:, :, :].rearrange("p (m k) c -> p m k c", m=2)
            sq_free = a = pr.dve("y_sq4", lambda e: e.tensor_tensor(
                s4[:, :, :, :], four[:, :, 0:2, :], four[:, :, 2:4, :], ALU.add), a)
            s4_free = pr.dve("y_sq2", lambda e: e.tensor_tensor(
                s2[:, :, :], s4[:, :, 0, :], s4[:, :, 1, :], ALU.add), a, s2_free)

        def root(n):
            nonlocal s2_free, sum_free
            s2_free = pr.pe("y_sum", last_of([mm(bank(7)[:, m:m + 1], s2[:, m, :], ones[:, :])
                                              for m in range(2)]), s4_free, one_ok, sum_free)
            out = rs[:, n, :]
            sum_free = pr.dve("y_ms", lambda e: e.tensor_scalar(
                out, bank(7)[:, 0:2], 1.0 / W5, EPS, ALU.mult, ALU.add), s2_free)
            b = pr.act("y_root", lambda e: e.activation(out, out, ACT.Sqrt), sum_free)
            rs_ok[n] = pr.dve("y_rstd", lambda e: e.reciprocal(out, out), b)

        def multiply(n, part):
            nonlocal cnt
            i, ks, outs = n % 2, slice(4 * part, 4 * part + 4), []
            for half in range(2):
                b = cnt % NB
                cnt += 1
                cs = slice(half * W5, (half + 1) * W5)
                lhs = [(y_hi[:, i, k, :], y_lo[:, i, k, :]) for k in range(KT)[ks]]
                rhs = [(w_hi[:, k, cs], w_lo[:, k, cs]) for k in range(KT)[ks]]
                if n == 0:
                    done = contraction_steps(pr, "wout_mm", bank(b), lhs, rhs, w_ok[ks], y_ok[n])
                else:
                    done = pr.pe("wout_mm", contraction(bank(b), lhs, rhs), y_ok[n], free[b])
                outs.append((b, done))
            return outs

        def add(n, part, outs, was):
            x, oks = n % NX, []
            for half, (b, done) in enumerate(outs):
                cs = slice(half * W5, (half + 1) * W5)
                free[b] = pr.dve("h1", lambda e, b=b, cs=cs: e.scalar_tensor_tensor(
                    xr[:, x, cs], bank(b), rs[:, n, part:part + 1], xr[:, x, cs], ALU.mult,
                    ALU.add), done, rs_ok[n], x_in[n], was)
                oks.append(free[b])
            return oks

        split_w(0)
        split_y(0)
        fetch(0)
        for k in range(1, KT):
            split_w(k)
            if k == 2:
                root(0)
        fetch(1)
        last_sq = None
        for n in range(NT):
            x = n % NX
            outs = multiply(n, 0)
            if n + 1 < NT:
                split_y(n + 1)
            first = add(n, 0, outs, None)
            outs = multiply(n, 1)
            if n + 1 < NT:
                root(n + 1)
            y_used[n % 2] = outs[1][1]
            done = add(n, 1, outs, first)
            last_sq = pr.act("h1_sq", lambda e, x=x, n=n: e.activation(
                w_st[:, 0, :], xr[:, x, :], ACT.Square, accum_out=rs2[:, n:n + 1]), done,
                st_free[0], last_sq)
            x_free[x] = [last_sq, pr.load(f"h1_st{x}", hv[n // CH, n % CH], xr[:, x, :], done,
                                          q="act")]
            if n + 2 < NT:
                fetch(n + 2)
        rstd_from_sums(pr, "n2", rs2, rs2, 1.0 / D, EPS, last_sq)
        pr.hold("sp", x_free)
        pr.emit()


def row_in(env, stack, name):
    buf = env["sb"](stack, f"row_{name}", [P, D])
    return buf, row_load(env, name, buf)


def row_load(env, name, buf):
    rows = env["t"]["rows"]
    src = bass.AP(tensor=rows.tensor, offset=rows.offset + ROWS[name], ap=[[0, P], [1, D]])
    return env["pr"].load(f"row_{name}", buf[:, :], src)


def transposed_halves(env, tag, i, z, hi, lo, turned, banks2, *waits):
    pr, bank, ident = env["pr"], env["bank"], env["ident"]
    oks = []
    for g in range(2):
        b = banks2[g]
        tr = pr.pe(f"{tag}_turn", turns(bank(b), [z[:, k * P:(k + 1) * P]
                                                  for k in range(4 * g, 4 * g + 4)], ident),
                   turned.get(b), *waits)
        turned[b] = split_pair(pr, tag, hi[:, 4 * g:4 * g + 4, i * P:(i + 1) * P],
                               lo[:, 4 * g:4 * g + 4, i * P:(i + 1) * P],
                               bank(b).rearrange("p (j c) -> p j c", j=4), tr)
        oks.append(turned[b])
    return oks, tr


def layer_norm_stats(pr, tag, x, st6, mv, *waits):
    for h in range(2):
        s = pr.dve(f"{tag}_st", lambda e, h=h: e.bn_stats(st6[:, 6 * h:6 * h + 6],
                                                         x[:, h * W5:(h + 1) * W5]), *waits)
    return pr.dve(f"{tag}_mv", lambda e: e.bn_aggr(mv, st6), s)


class Leaving:

    def __init__(self, env, stack, acc):
        sb = env["sb"]
        self.env, self.acc = env, acc
        self.gf, self.lg, self.lb = (sb(stack, f"row_{n}", [P, D]) for n in ("gf", "lin_g", "lin_b"))
        self.junk = sb(stack, "h_junk", [P, D])
        self.ss = sb(stack, "ssf", [P, HT])
        self.st6 = sb(stack, "st6", [P, HT, 12])
        self.mv = sb(stack, "mv", [P, HT, 2])
        self.rl = sb(stack, "rl", [P, HT])
        self.shift = sb(stack, "shift", [P, HT])
        self.junk_free = None
        self.h2v = env["h2"][:, :].rearrange("(b p s) d -> b s p d", b=2, s=CH)

    def fetch_rows(self):
        self.gf_ok, self.lg_ok, self.lb_ok = (
            row_load(self.env, n, buf) for n, buf in (("gf", self.gf), ("lin_g", self.lg),
                                                      ("lin_b", self.lb)))

    def normalise(self, tiles, ready):
        pr, acc = self.env["pr"], self.acc
        ts_ = slice(tiles[0], tiles[-1] + 1)
        for i in tiles:
            sq = self.junk_free = pr.act("h_sq", lambda e, i=i: e.activation(
                self.junk[:, :], acc[:, i, :], ACT.Square, accum_out=self.ss[:, i:i + 1]),
                ready.get(i), self.junk_free)
            y = pr.dve("h_gf", lambda e, i=i: e.tensor_tensor(
                acc[:, i, :], acc[:, i, :], self.gf[:, :], ALU.mult), sq, self.gf_ok)
            mv_ok = layer_norm_stats(pr, "li", acc[:, i, :], self.st6[:, i, :], self.mv[:, i, :], y)
        ss, mean, var = self.ss[:, ts_], self.mv[:, ts_, 0], self.mv[:, ts_, 1]
        a = pr.dve("li_eps", lambda e: e.tensor_scalar(ss, ss, LN_EPS / D, LN_EPS * EPS, ALU.mult,
                                                      ALU.add), sq)
        a = pr.dve("li_var", lambda e: e.tensor_tensor(ss, ss, var, ALU.add), a, mv_ok)
        a = pr.act("li_root", lambda e: e.activation(ss, ss, ACT.Sqrt), a)
        a = pr.dve("li_rstd", lambda e: e.reciprocal(self.rl[:, ts_], ss), a)
        a = pr.dve("li_shift", lambda e: e.scalar_tensor_tensor(
            self.shift[:, ts_], mean, -1.0, self.rl[:, ts_], ALU.mult, ALU.mult), a)
        out, g = {}, None
        for i in tiles:
            n = pr.act("h2_n", lambda e, i=i: e.activation(
                acc[:, i, :], acc[:, i, :], ACT.Identity, scale=self.rl[:, i:i + 1],
                bias=self.shift[:, i:i + 1]), a)
            g = out[i] = pr.pool("h2_g", lambda e, i=i: e.tensor_tensor(
                acc[:, i, :], acc[:, i, :], self.lg[:, :], ALU.mult), n, self.lg_ok, g)
        return out

    def store(self, half, tiles, g):
        pr, acc, out = self.env["pr"], self.acc, {}
        for i in tiles:
            b = pr.dve("h2_b", lambda e, i=i: e.tensor_tensor(
                acc[:, i, :], acc[:, i, :], self.lb[:, :], ALU.add), g[i], self.lb_ok)
            out[i] = pr.load(f"h2_st{i}", self.h2v[half, i], acc[:, i, :], b)
        return out


def feed_forward(env):
    pr, sb, t, bank, banks = (env[k] for k in ("pr", "sb", "t", "bank", "banks"))
    with ExitStack() as keep:
        acc = sb(keep, "ff_acc", [P, HT, D])
        leave = Leaving(env, keep, acc)
        with ExitStack() as st:
            g2, g2_ok = row_in(env, st, "g2")
            n_hi = sb(st, "n2_hi", [P, KT, HALF], F32R)
            n_lo = sb(st, "n2_lo", [P, KT, HALF], F32R)
            z = sb(st, "z2", [P, 3, D])
            wst = sb(st, "ff_stage", [P, 3, D])
            wg_hi = sb(st, "gate_up_hi", [P, 2, 2, D], F32R)
            wg_lo = sb(st, "gate_up_lo", [P, 2, 2, D], F32R)
            wd_hi = sb(st, "down_hi", [P, D], F32R)
            wd_lo = sb(st, "down_lo", [P, D], F32R)
            f_hi = sb(st, "ff_hi", [P, 2, HALF], F32R)
            f_lo = sb(st, "ff_lo", [P, 2, HALF], F32R)
            sil = sb(st, "silu", [P, 2, W5])
            ff = sb(st, "ff", [P, 2, W5])
            gate = t["w_gate"][0].rearrange("(k p) f -> p k f", p=P)
            up = t["w_up"][0].rearrange("(k p) f -> p k f", p=P)
            h1v = env["h1"][:, :].rearrange("(b p s) d -> b s p d", b=2, s=CH)
            gu_in, gu_ok, gu_used, gu_st_free = {}, {}, [None, None], None
            d_in, d_ok, d_used, d_st_free = {}, {}, None, None
            f_ok, f_free = {}, [None, None]
            bank_free, sil_free, ff_free = {b: None for b in range(8)}, [None] * 2, [None] * 2
            n_ok, n_free, z_free, acc_ok, acc_done = [[], []], None, [None] * 3, {}, {}
            h1_in, z_ok = {}, {}

            def js(J):
                return slice(J % NJ * P, (J % NJ + 1) * P)

            def load_gate_up(J):
                gu_in[J] = [pr.load("gate_up_in", wst[:, m, :].rearrange("p (k f) -> p k f", f=P),
                                    w[:, :, js(J)], gu_st_free) for m, w in enumerate((gate, up))]

            def split_gate_up(J):
                nonlocal gu_st_free
                i = J % 2
                gu_ok[J] = gu_st_free = split_pair(pr, "gate_up", wg_hi[:, i], wg_lo[:, i],
                                                   wst[:, 0:2], gu_in[J], gu_used[i])

            def load_down(J):
                d_in[J] = pr.load("down_in", wst[:, 2, :], t["w_down"][0, js(J), :], d_st_free)

            def split_down(J):
                nonlocal d_st_free
                d_ok[J] = d_st_free = split_pair(pr, "down", wd_hi[:, :], wd_lo[:, :],
                                                 wst[:, 2, :], d_in[J], d_used)

            def fetch_tile(half, i):
                x = i % 3
                h1_in[i] = pr.load(f"h1_in{x}", z[:, x, :], h1v[half, i], z_free[x])

            def scale_tile(half, i):
                x, r = i % 3, half * HT + i
                z_ok[i] = pr.dve("z2", lambda e: e.scalar_tensor_tensor(
                    z[:, x, :], z[:, x, :], env["rs2"][:, r:r + 1], g2[:, :], ALU.mult, ALU.mult),
                    h1_in[i], g2_ok)

            def turn_tile(i):
                x = i % 3
                oks, z_free[x] = transposed_halves(env, "n2T", i, z[:, x, :], n_hi, n_lo, bank_free,
                                                   (2 * (i % 2), 2 * (i % 2) + 1), z_ok[i], n_free)
                n_ok[i // 4] = oks if i % 4 == 0 else n_ok[i // 4] + oks

            def load_acc(half, i):
                acc_ok[i] = pr.load(f"acc_in{i}", acc[:, i, :], h1v[half, i], acc_ok.get(i))

            def gate_up(J, nh):
                i, cs = J % 2, slice(nh * W5, (nh + 1) * W5)
                done = []
                for m in range(2):
                    done.append(pr.pe("gate_up_mm", contraction(
                        bank(2 * nh + m),
                        [(wg_hi[:, i, m, k * P:(k + 1) * P], wg_lo[:, i, m, k * P:(k + 1) * P])
                         for k in range(KT)],
                        [(n_hi[:, k, cs], n_lo[:, k, cs]) for k in range(KT)]),
                        gu_ok[J], n_ok[nh], bank_free[2 * nh + m]))
                s = pr.act("silu", lambda e: e.activation(sil[:, nh, :], bank(2 * nh), ACT.Silu),
                           done[0], sil_free[nh])
                bank_free[2 * nh] = s
                f = pr.dve("ff", lambda e: e.tensor_tensor(
                    ff[:, nh, :], sil[:, nh, :], bank(2 * nh + 1), ALU.mult), s, done[1],
                    ff_free[nh])
                bank_free[2 * nh + 1] = sil_free[nh] = f
                ff_free[nh] = split_pair(pr, "ff", f_hi[:, i, cs], f_lo[:, i, cs], ff[:, nh, :], f,
                                         f_free[i])
                f_ok[J, nh] = ff_free[nh]
                gu_used[i] = done[1]
                return done[1]

            def down(J, m, pairs=(2, 3, 0)):
                i, d = J % 2, pairs[m % len(pairs)]
                rows = slice(m * P, (m + 1) * P)
                done = pr.pe("down_mm", last_of([contraction(
                    bank(2 * d + nh), [(f_hi[:, i, rows], f_lo[:, i, rows])],
                    [(wd_hi[:, nh * W5:(nh + 1) * W5], wd_lo[:, nh * W5:(nh + 1) * W5])])
                    for nh in range(2)]), d_ok[J], f_ok[J, m // 4], bank_free[2 * d],
                    bank_free[2 * d + 1])
                bank_free[2 * d] = bank_free[2 * d + 1] = acc_done[m] = pr.dve(
                    "ff_acc", lambda e: e.tensor_tensor(
                        acc[:, m, :].rearrange("p (a b) -> p a b", a=2),
                        acc[:, m, :].rearrange("p (a b) -> p a b", a=2), banks[d][:, :, :],
                        ALU.add), done, acc_ok[m])
                return done

            for i in range(3):
                fetch_tile(0, i)
            load_gate_up(0)
            scale_tile(0, 0)
            for i in range(HT):
                if i + 1 < HT:
                    scale_tile(0, i + 1)
                turn_tile(i)
                if i + 3 < HT:
                    fetch_tile(0, i + 3)
                if i == 2:
                    split_gate_up(0)
            load_gate_up(1)
            load_down(0)
            for i in range(HT):
                load_acc(0, i)
            leave.fetch_rows()
            last = 2 * NJ - 1
            for J in range(last + 2):
                at_turn = J == NJ
                if J >= 1:
                    split_down(J - 1)
                    if J <= last:
                        load_down(J)
                if J + 1 <= last:
                    split_gate_up(J + 1)
                    if J + 2 <= last:
                        load_gate_up(J + 2)
                if J == NJ - 1:
                    for i in range(3):
                        fetch_tile(1, i)
                if at_turn:
                    scale_tile(1, 0)
                    for m in range(HT):
                        if m + 1 < HT:
                            scale_tile(1, m + 1)
                        turn_tile(m)
                        if m + 3 < HT:
                            fetch_tile(1, m + 3)
                        d_used = down(J - 1, m, (2, 3))
                    f_free[(J - 1) % 2] = d_used
                    h2_st = leave.normalise(range(0, 4), acc_done)
                if J == NJ + 1:
                    h2_st = leave.normalise(range(4, HT), acc_done)
                if J <= last:
                    gate_up(J, 0)
                    if J == NJ + 1:
                        acc_ok.update(leave.store(0, range(4, HT), h2_st))
                        for i in range(4, HT):
                            load_acc(1, i)
                    n_free = gate_up(J, 1)
                if at_turn:
                    acc_ok.update(leave.store(0, range(0, 4), h2_st))
                    for i in range(0, 4):
                        load_acc(1, i)
                if J >= 1 and not at_turn:
                    for m in range(HT):
                        d_used = down(J - 1, m)
                    f_free[(J - 1) % 2] = d_used
            pr.hold("sp", [acc_ok[i] for i in range(HT)])
            pr.emit()
        project(env, leave)


BLOCKS = (("v", 1024, W5, "tok"), ("k", 512, W5, "T"), ("q", 0, W5, "T"), ("ag", 1536, W5, "tok"),
          ("gqk", 2048, W5, "T"), ("gv", 2560, W5, "tok"), ("glr", 3584, 16, "T"),
          ("gg", 3072, W5, "tok"))


def project(env, leave):
    pr, sb, t, bank = (env[k] for k in ("pr", "sb", "t", "bank"))
    for name, _, w, kind in BLOCKS:
        env["p_" + name] = env["scratch"]("p_" + name, [w, TOK] if kind == "T" else [TOK, w])
    with ExitStack() as st:
        hT_hi = sb(st, "hT_hi", [P, KT, HALF], F32R)
        hT_lo = sb(st, "hT_lo", [P, KT, HALF], F32R)
        hr = sb(st, "h2_ring", [P, 2, D])
        wst = sb(st, "pw_stage", [P, 2, 2, W5])
        w_hi = sb(st, "pw_hi", [P, 2, KT, W5], F32R)
        w_lo = sb(st, "pw_lo", [P, 2, KT, W5], F32R)
        o_sb = sb(st, "p_ring", [P, 4, W5])
        wv = t["w_in_2"][0].rearrange("(k p) c -> p k c", p=P)
        h_free, h_ok, h2_ok = [None] * 2, {}, {}
        w_ok, w_free, st_free = {}, [None, None], [None, None]
        bank_free, o_free, cnt = {b: None for b in range(8)}, [None] * 4, 0
        nb = len(BLOCKS)
        runs = [(half, b) for half in range(2) for b in range(nb)]

        def weights(n, pieces=range(4)):
            _, c0, w, _ = BLOCKS[runs[n][1]]
            i = n % 2
            for piece in pieces:
                x, ks = piece % 2, slice(2 * piece, 2 * piece + 2)
                ld = pr.load(f"pw_in{x}", wst[:, x, :, 0:w], wv[:, ks, c0:c0 + w], st_free[x])
                st_free[x] = split_pair(pr, "pw", w_hi[:, i, ks, 0:w], w_lo[:, i, ks, 0:w],
                                        wst[:, x, :, 0:w], ld, w_free[i])
                w_ok.setdefault(n, []).append(st_free[x])

        def tile_in(half, i, b2, used=None):
            x, r0 = i % 2, half * HALF + i * P
            ld = pr.load(f"h2_in{x}", hr[:, x, :], env["h2"][r0:r0 + P, :], h_free[x], h2_ok.get(half))
            h_ok[half, i], h_free[x] = transposed_halves(
                env, "hT", i, hr[:, x, :], hT_hi, hT_lo, bank_free, b2, ld, used)

        def product(n, tiles, lhs, rhs, scale, func, dst, rows=P):
            nonlocal cnt
            bk, o = cnt % 6, cnt % 4
            cnt += 1
            done = pr.pe("proj_mm", contraction(bank(bk), lhs, rhs), w_ok[n],
                         [h_ok[runs[n][0], i] for i in tiles], bank_free[bk])
            ev = bank_free[bk] = pr.act("proj_out", lambda e: e.activation(
                o_sb[0:rows, o, :], bank(bk)[0:rows, :], func, scale=scale), done, o_free[o])
            o_free[o] = pr.load(f"proj_st{o}", dst, o_sb[0:rows, o, :], ev, q="pool")
            return done

        def across(n, m):
            half, b = runs[n]
            name, i = BLOCKS[b][0], n % 2
            ms = slice(m * P, (m + 1) * P)
            return product(
                n, [m], [(hT_hi[:, k, ms], hT_lo[:, k, ms]) for k in range(KT)],
                [(w_hi[:, i, k, :], w_lo[:, i, k, :]) for k in range(KT)], 1.0,
                ACT.Silu if name in ("ag", "gg") else ACT.Copy,
                env["p_" + name][half * HALF + m * P:half * HALF + (m + 1) * P, :])

        def along(n, c, nh):
            half, b = runs[n]
            name, _, w, _ = BLOCKS[b]
            i, rows, cs = n % 2, min(w, P), slice(c * P, (c + 1) * P)
            t0, ts_ = half * HALF + nh * W5, slice(nh * W5, (nh + 1) * W5)
            scale = -0.125 if name == "q" else 0.125 if name == "gqk" and c < 2 else 1.0
            return product(
                n, range(4 * nh, 4 * nh + 4),
                [(w_hi[:, i, k, cs], w_lo[:, i, k, cs]) for k in range(KT)],
                [(hT_hi[:, k, ts_], hT_lo[:, k, ts_]) for k in range(KT)], scale, ACT.Copy,
                env["p_" + name][c * P:c * P + rows, t0:t0 + W5], rows)

        weights(0)
        tile_in(0, 0, (6, 7))
        used = {}
        g = [None, None]
        for n, (half, b) in enumerate(runs):
            name, _, w, kind = BLOCKS[b]
            if n + 1 < len(runs) and b != 0:
                weights(n + 1)
            if n in (1, 2):
                g[n - 1] = leave.normalise(range(4 * (n - 1), 4 * n), {})
            if n == 2:
                stores = leave.store(1, range(0, 4), g[0])
            if n == 3:
                stores.update(leave.store(1, range(4, HT), g[1]))
            if kind == "T":
                for c in range(max(1, w // P)):
                    for nh in range(2):
                        done = along(n, c, nh)
            else:
                for m in range(HT):
                    if b == 0 and half == 0 and m + 1 < HT:
                        tile_in(0, m + 1, (6, 7))
                    if b == 0 and m == 2:
                        weights(n + 1)
                    if n == nb - 1 and m >= 1:
                        if m == 1:
                            h2_ok[1] = list(stores.values())
                        tile_in(1, m - 1, (6, 7), done)
                    done = across(n, m)
                if n == nb - 1:
                    tile_in(1, HT - 1, (6, 7), done)
            w_free[n % 2] = done
        pr.hold("sp", o_free)
        pr.emit()


def band_attention(env):
    pr, sb, t, bank, banks, ident = (env[k] for k in ("pr", "sb", "t", "bank", "banks", "ident"))
    env["mix"] = mix = env["scratch"]("mix", [TOK, D])
    skew = env["skew"]
    with ExitStack() as st:
        bias = sb(st, "bias", [P, NHEAD, BAND_W])
        q_src = sb(st, "q_src", [P, TOK])
        k_src = sb(st, "k_src", [P, TOK])
        q_st = sb(st, "q_stack", [P, 2, TOK], F32R)
        k_hi = sb(st, "k_hi", [P, 2, TOK], F32R)
        k_lo = sb(st, "k_lo", [P, 2, TOK], F32R)
        v_src = sb(st, "v_src", [P, NT, 2, AD])
        v_hl = sb(st, "v_hl", [P, 2, NT, 2, 2, AD], F32R)
        ag = sb(st, "ag_sb", [P, 2, NT, P])
        S = sb(st, "S_sb", [P, 3, BAND_W])
        E = sb(st, "E_sb", [P, 3, BAND_W])
        ET_hi = sb(st, "ET_hi", [P, 3, BAND_W], F32R)
        ET_lo = sb(st, "ET_lo", [P, 3, BAND_W], F32R)
        o = sb(st, "att_sb", [P, 2, NT, P])
        lo_half = sb(st, "lo_half", [P, 2, AD])
        mx = sb(st, "mx", [P, 8, 3])

        bias_ok, bias_in = {}, {}

        def load_bias(h, n):
            bias_in[h] = pr.load(f"bias_in{h}", bias[:, h:h + n, :], bass.AP(
                tensor=skew[:, :, :].tensor, offset=P - 1 + h * P * EXT,
                ap=[[EXT - 1, P], [P * EXT, n], [1, BAND_W]]))

        def end_bands(h, n):
            pr.dve("bias_end", lambda e: e.memset(
                bias[0:64, h:h + n, BAND_W - 64:BAND_W], -NEG), bias_in[h])
            ok = pr.dve("bias_end", lambda e: e.memset(bias[64:P, h:h + n, 0:64], -NEG), bias_in[h])
            for x in range(h, h + n):
                bias_ok[x] = ok

        src_ok, src_free, head_ok, head_free = {}, None, {}, [None] * 2
        v_ok, v_free, v_src_ok, v_src_free = {}, [None] * 2, {}, None
        ag_ok, ag_free, o_free = {}, [None] * 2, [None] * 2
        s_done, s_free, m_ok, S_free, e_ok, E_free = {}, None, {}, [None] * 3, {}, [None] * 3
        t_done, t_free, hi_ok, et_ok, ET_free = {}, [None] * 2, {}, {}, [None] * 3
        r_ok, pv_free = {}, [None] * 2
        units = [(h, qt) for h in range(NHEAD) for qt in range(NT)]

        def load_head(h):
            rows = slice(h * AD, (h + 1) * AD)
            src_ok[h] = [pr.load(f"{n}_in", buf[AD * c:AD * (c + 1), :], env["p_" + n][rows, :],
                                 src_free) for n, buf in (("q", q_src), ("k", k_src))
                         for c in range(2)]
            head_ok[h] = []
            if h % 2 == 0:
                hp, cs = h // 2, slice(h * AD, (h + 2) * AD)
                v_src_ok[hp] = pr.load("v_in", v_src[:, :, :, :].rearrange(
                    "p m h c -> p m (h c)"), env["p_v"][:, cs].rearrange(
                    "(m p) c -> p m c", p=P), v_src_free)
                v_ok[hp] = []
                ag_ok[hp] = pr.load(f"ag_in{hp % 2}", ag[:, hp % 2, :, :], env["p_ag"][
                    :, cs].rearrange("(m p) c -> p m c", p=P), ag_free[hp % 2])

        def split_head(h, piece):
            nonlocal src_free, v_src_free
            what, n = divmod(piece, 4)
            i, ns = h % 2, slice(n * W5, (n + 1) * W5)
            if what == 0:
                ok = split_pair(pr, "k_split", k_hi[:, i, ns], k_lo[:, i, ns], k_src[:, ns],
                                src_ok[h], head_free[i])
                head_ok[h].append(ok)
            elif what == 1:
                a1 = pr.act("q_hi", lambda e: e.activation(q_st[:, i, ns], q_src[:, ns], ACT.Copy),
                            src_ok[h], head_free[i])
                low = slice(AD, P)
                ok = pr.dve("q_lo", lambda e: e.tensor_tensor(
                    q_st[low, i, ns], q_src[low, ns], q_st[low, i, ns].bitcast(F32),
                    ALU.subtract), a1)
                head_ok[h].append(ok)
                src_free = ok
            elif h % 2 == 0:
                hp, ms = h // 2, slice(4 * n, 4 * n + 4)
                v_src_free = split_pair(pr, "v_split", v_hl[:, hp % 2, ms, :, 0, :],
                                        v_hl[:, hp % 2, ms, :, 1, :], v_src[:, ms, :, :],
                                        v_src_ok[hp], v_free[hp % 2])
                v_ok[hp].append(v_src_free)

        def geometry(u):
            h, qt = units[u]
            nk = min(qt + 1, BAND_T)
            return h, qt, nk, qt + 1 - nk, nk * P

        def joined(pb, W):
            return pb[:, :, :].rearrange("p a b -> p (a b)")[:, 0:W]

        def scores(u):
            h, qt, nk, k0, W = geometry(u)
            i, pb = h % 2, banks[0]
            fns = []
            for c in range(0, W, W5):
                w = min(c + W5, W) - c
                ks = slice(k0 * P + c, k0 * P + c + w)
                for part, kk in enumerate((k_lo, k_hi)):
                    fns.append(mm(pb[:, c // W5, 0:w], q_st[:, i, qt * P:(qt + 1) * P],
                                  kk[:, i, ks], part == 0, part == 1))
            s_done[u] = pr.pe("score_mm", last_of(fns), head_ok[h], s_free)
            if qt == NT - 1:
                head_free[i] = s_done[u]

        def maximum(u):
            nonlocal s_free
            h, qt, nk, k0, W = geometry(u)
            x = u % 3
            m_ok[u] = s_free = pr.dve("score_max", lambda e: e.tensor_tensor_reduce(
                S[:, x, 0:W], joined(banks[0], W), bias[:, h, BAND_W - W:BAND_W], 1.0, 3e38,
                ALU.add, ALU.min, mx[:, u % 8, 0:1]), s_done[u], bias_ok[h], S_free[x])

        def exponentials(u):
            h, qt, nk, k0, W = geometry(u)
            x = u % 3
            e_ok[u] = S_free[x] = pr.act("exp", lambda e: e.activation(
                E[:, x, 0:W], S[:, x, 0:W], ACT.Exp, scale=-1.0, bias=mx[:, u % 8, 0:1],
                accum_out=mx[:, u % 8, 1:2]), m_ok[u], E_free[x])

        def turn_e(u):
            h, qt, nk, k0, W = geometry(u)
            x, pb = u % 3, banks[1 + u % 2]
            t_done[u] = E_free[x] = pr.pe("E_turn2", last_of([
                (lambda e, j=j: e.transpose(pb[:, j // 4, (j % 4) * P:(j % 4 + 1) * P],
                                            E[:, x, j * P:(j + 1) * P], ident[:, :]))
                for j in range(nk)]), e_ok[u], t_free[u % 2])
            hi_ok[u] = pr.act("ET_hi", lambda e: e.activation(
                ET_hi[:, x, 0:W], joined(pb, W), ACT.Copy), t_done[u], ET_free[x])
            r_ok[u] = pr.dve("sum_recip", lambda e: e.reciprocal(
                mx[:, u % 8, 2:3], mx[:, u % 8, 1:2]), e_ok[u])

        def lower(u):
            h, qt, nk, k0, W = geometry(u)
            x = u % 3
            et_ok[u] = t_free[u % 2] = pr.dve("ET_lo", lambda e: e.tensor_tensor(
                ET_lo[:, x, 0:W], joined(banks[1 + u % 2], W), ET_hi[:, x, 0:W].bitcast(F32),
                ALU.subtract), hi_ok[u], ET_free[x])

        def values(u):
            h, qt, nk, k0, W = geometry(u)
            hp, x, y = h // 2, u % 3, u % 2
            i, rows = hp % 2, slice(AD * (h % 2), AD * (h % 2 + 1))
            pb = bank(6 + y)
            done = pr.pe("pv_mm", last_of([
                mm(pb[:, 0:P], half[:, x, j * P:(j + 1) * P],
                   v_hl[:, i, k0 + j, h % 2, :, :].rearrange("p a c -> p (a c)"),
                   j == 0 and half is ET_lo, j == nk - 1 and half is ET_hi)
                for j in range(nk) for half in (ET_lo, ET_hi)]), et_ok[u], v_ok[hp], pv_free[y])
            ET_free[x] = done
            b = pr.dve("att_halves", lambda e: e.tensor_copy(lo_half[:, y, :], pb[:, AD:P]), done)
            pv_free[y] = f = pr.dve("att_sum", lambda e: e.tensor_tensor(
                lo_half[:, y, :], lo_half[:, y, :], pb[:, 0:AD], ALU.add), b)
            f = pr.dve("att_out", lambda e: e.scalar_tensor_tensor(
                o[:, i, qt, rows], lo_half[:, y, :], mx[:, u % 8, 2:3], ag[:, i, qt, rows],
                ALU.mult, ALU.mult), f, r_ok[u], o_free[i], ag_ok[hp])
            if qt == NT - 1 and h % 2 == 1:
                v_free[i], ag_free[i] = done, f
                o_free[i] = pr.load(f"att_st{i}", mix[:, hp * P:(hp + 1) * P].rearrange(
                    "(m p) c -> p m c", p=P), o[:, i, :, :], f)

        load_head(0)
        load_bias(0, 1)
        for piece in range(12):
            split_head(0, piece)
        load_bias(1, NHEAD - 1)
        end_bands(0, 1)
        n = len(units)
        for u in range(n + 4):
            h, qt = units[u] if u < n else (NHEAD, 0)
            if h + 1 < NHEAD:
                if qt == 2:
                    load_head(h + 1)
                if qt == NT - 1 and h == 0:
                    end_bands(1, NHEAD - 1)
                if 4 <= qt < 16:
                    split_head(h + 1, qt - 4)
            if 3 <= u < n + 3:
                lower(u - 3)
            if u < n:
                scores(u)
                maximum(u)
            if 1 <= u <= n:
                exponentials(u - 1)
            if 2 <= u < n + 2:
                turn_e(u - 2)
            if u >= 4:
                values(u - 4)
        pr.hold("sp", o_free)
        pr.emit()


def gated_linear_attention(env, out_w, ple_w):
    pr, sb, t, bank, banks, ident, col = (env[k] for k in (
        "pr", "sb", "t", "bank", "banks", "ident", "col"))
    C = 64
    NC = TOK // C
    UT = 4
    UC = UT * P // C
    NU = NT // UT
    NA, NS = 3, 6
    mix = env["mix"]
    with ExitStack() as st:
        q, k, L, eL, eN, qf, tmp = (sb(st, n, [P, 2, W5]) for n in (
            "gq", "gk", "gL", "eL", "eN", "q_fwd", "g_tmp"))
        reset = sb(st, "reset", [P, W5])
        lend = sb(st, "lend", [P, 2, UC])
        dec = sb(st, "dec", [P, 2, UC])
        v = sb(st, "gv_sb", [P, 2, UT, 2 * P])
        gate = sb(st, "gg_sb", [P, 2, UT, 2 * P])
        raw = sb(st, "o_raw", [P, 2, UT, 2 * P])
        lr_ = sb(st, "glr_sb", [16, TOK])
        gw = sb(st, "w_gg", [16, 2 * P])
        mask = sb(st, "tri", [P, C])
        logs = sb(st, "log_sig", [P, 2, TOK])
        lgt = sb(st, "g_logit", [P, 2, TOK])
        att = sb(st, "g_att", [P, NA, 2, C])
        kdT = sb(st, "kdT", [P, 2, P])
        state = sb(st, "g_state", [P, NS, P])
        ssq = sb(st, "g_ss", [P, 2, UT, 2])
        junk = sb(st, "g_junk", [P, 2, P])
        gn = sb(st, "g_gain", [P, 4 * P])
        w_st = sb(st, "ow_stage", [P, 2, D])
        l_in = [pr.load("glr_in", lr_[:, :], env["p_glr"][:, :]),
                pr.load("glr_in", gw[:, :], t["w_gla_gate_2"][0])]
        rows = t["rows"]
        n_in = pr.load("ggain_in", gn[:, :], bass.AP(
            tensor=rows.tensor, offset=rows.offset + ROWS["gla_g"], ap=[[0, P], [1, 4 * P]]))
        m1 = pr.pool("g_const", lambda e: e.memset(reset[:, :], 1.0))
        m2 = pr.pool("g_const", lambda e: e.memset(reset[:, 0:W5:C], 0.0), m1)
        m3 = pr.pool("g_const", lambda e: e.memset(mask[:, :], 1.0), m2)
        for c in range(2):
            m3 = pr.pool("g_const", lambda e, c=c: e.affine_select(
                out=mask[C * c:C * (c + 1), :], in_=mask[C * c:C * (c + 1), :],
                compare_op=ALU.is_ge, fill=0.0, base=0, pattern=[[1, C]],
                channel_multiplier=-1), m3)
        const_ok = gg_last = m3
        units = [(hp, n) for hp in range(2) for n in range(NU)]
        S, used = {}, [[], []]
        w_free = [None, None]

        def fetch(u):
            hp, n = units[u]
            i, ts_ = u % 2, slice(n * W5, (n + 1) * W5)
            vs = slice(hp * 2 * P, (hp + 1) * 2 * P)
            w = list(used[i])
            S[u] = dict(
                qk=[pr.load(f"gqk_in{i}", buf[:, i, :], env["p_gqk"][r0 + hp * P:r0 + (hp + 1) * P,
                                                                    ts_], w)
                    for r0, buf in ((0, q), (2 * P, k))],
                v=pr.load(f"gv_in{i}", v[:, i, :, :], env["p_gv"][ts_, vs].rearrange(
                    "(m p) c -> p m c", p=P), w),
                gate=pr.load(f"gg_in{i}", gate[:, i, :, :], env["p_gg"][ts_, vs].rearrange(
                    "(m p) c -> p m c", p=P), w), w=w)

        sc = 1.0 / 16.0

        log_ok, logit = {}, {}
        for hp in range(2):
            logit[hp] = []
            for n in range(4):
                b, ns = 4 * hp + n, slice(n * W5, (n + 1) * W5)
                d = pr.pe("glogit_mm", mm(bank(b), gw[:, hp * P:(hp + 1) * P], lr_[:, ns]), l_in)
                if hp == 0:
                    ev = pr.act("glogit0", lambda e, b=b, ns=ns: e.activation(
                        lgt[:, 0, ns], bank(b), ACT.Identity, bias=col("bgate", 0)), d)
                else:
                    ev = pr.dve("glogit1", lambda e, b=b, ns=ns: e.tensor_scalar(
                        lgt[:, 1, ns], bank(b), col("bgate", 1), None, ALU.add, ALU.bypass), d)
                logit[hp].append(ev)

        def log_sigmoid(hp):
            L_, T_ = lgt[:, hp, :], logs[:, hp, :]
            a = pr.act("g_abs", lambda e: e.activation(T_, L_, ACT.Abs), logit[hp])
            a = pr.act("g_exp", lambda e: e.activation(T_, T_, ACT.Exp, scale=-1.0), a)
            a = pr.act("g_ln", lambda e: e.activation(T_, T_, ACT.Ln, bias=1.0), a)
            log_ok[hp] = pr.dve("g_logsig", lambda e: e.scalar_tensor_tensor(
                T_, L_, 0.0, T_, ALU.min, ALU.subtract), a)

        def prepare(u, part):
            nonlocal gg_last
            hp, n = units[u]
            i, s = u % 2, S[u]
            L_, T_, eL_, eN_, q_, k_, qf_ = (x[:, i, :] for x in (L, tmp, eL, eN, q, k, qf))
            if part == 0:
                for hh in range(2):
                    o_ = slice(hh * P, (hh + 1) * P)
                    g_ = gn[:, hp * 2 * P + hh * P:hp * 2 * P + (hh + 1) * P]
                    g_ = bass.AP(tensor=g_.tensor, offset=g_.offset,
                                 ap=[list(g_.ap[0]), [0, UT], [1, P]])
                    gg_last = s["gg"] = pr.pool("g_gate", lambda e, o_=o_, g_=g_: e.tensor_tensor(
                        gate[:, i, :, o_], gate[:, i, :, o_], g_, ALU.mult), s["gate"], n_in,
                        gg_last)
            elif part == 1:
                b = pr.dve("g_cumsum", lambda e: e.tensor_tensor_scan(
                    L_, reset[:, :], logs[:, hp, n * W5:(n + 1) * W5], 0.0, ALU.mult, ALU.add),
                    log_ok[hp], const_ok, s["w"])
                s["eL"] = pr.act("g_eL", lambda e: e.activation(eL_, L_, ACT.Exp, scale=sc), b)
                s["eN"] = pr.act("g_eN", lambda e: e.activation(eN_, L_, ACT.Exp, scale=-sc), b)
                b = pr.dve("g_lend", lambda e: e.tensor_copy(lend[:, i, :], L[:, i, C - 1:W5:C]), b)
                s["dec"] = pr.act("g_dec", lambda e: e.activation(dec[:, i, :], lend[:, i, :],
                                                                  ACT.Exp, scale=sc), b)
                b = pr.dve("g_left", lambda e: e.tensor_tensor(
                    T_.rearrange("p (n c) -> p n c", c=C), spread(lend[:, i, :], C),
                    L_.rearrange("p (n c) -> p n c", c=C), ALU.subtract), b)
                s["left"] = pr.act("g_kdecay", lambda e: e.activation(T_, T_, ACT.Exp, scale=sc), b)
            else:
                def mul(o, x, y, *w):
                    return pr.dve("g_mul", lambda e: e.tensor_tensor(o, x, y, ALU.mult), *w)

                s["kd"] = mul(T_, T_, k_, s["left"], s["qk"])
                s["qf"] = mul(qf_, q_, eL_, s["eL"])
                mul(eL_, k_, eL_, s["qf"])
                qn = mul(q_, q_, eN_, s["eN"])
                s["kn"] = mul(eN_, k_, eN_, qn)

        def split_w(kt):
            x = kt % 2
            w, pair, k_ = (t["w_out_2"], out_w, kt) if kt < KT else (t["w_ple_2"], ple_w, kt - KT)
            ld = pr.load(f"ow_in{x}", w_st[:, x, :], w[0, k_ * P:(k_ + 1) * P, :], w_free[x])
            w_free[x] = split_pair(pr, "ow", pair[0][:, k_, :], pair[1][:, k_, :], w_st[:, x, :],
                                   ld)

        att_ok, att_free, kd_free, kdT_ok = {}, [None] * NA, [None] * 2, {}
        kt_free = o_free = logit[1]
        a_free, kv_free = [logit[0], logit[1] + logit[0]], [logit[0], logit[1]]
        state_ok, state_free, sq_last = {}, [None] * NS, [None, None]
        raw_st = [None] * 2

        def inner(m):
            nonlocal kt_free
            y, u, i, m0 = m % 2, m // UT, m // UT % 2, m % UT * P
            ab, ay = ((0, 1), (2, 5))[y], m % NA
            s = S[u]
            done = []
            for hh in range(2):
                r = slice(C * hh, C * (hh + 1))
                fns = []
                for c in range(2):
                    ts_ = slice(m0 + C * c, m0 + C * (c + 1))
                    for w, (l_, r_) in enumerate(((eN, qf), (eL, q))):
                        fns.append(mm(bank(ab[hh])[C * c:C * (c + 1), w * C:(w + 1) * C],
                                      l_[r, i, ts_], r_[r, i, ts_]))
                done.append(pr.pe("g_att_mm", last_of(fns), s["kn"], a_free[y]))
            oks = []
            for hh in range(2):
                a1 = pr.act("g_anti", lambda e, hh=hh: e.activation(
                    att[:, ay, hh, :], bank(ab[hh])[:, C:2 * C], ACT.Copy), done[hh],
                    att_free[ay])
                oks.append(pr.dve("g_causal", lambda e, hh=hh: e.copy_predicated(
                    att[:, ay, hh, :], mask[:, :].bitcast(U32), bank(ab[hh])[:, 0:C]),
                    a1, done[hh], const_ok))
            a_free[y] = att_ok[m] = oks
            tr = pr.pe("kd_turn", turns(bank(7), [tmp[:, i, m0:m0 + P]], ident), s["kd"], kt_free)
            kdT_ok[m] = kt_free = pr.act("kdT_out", lambda e: e.activation(
                kdT[:, y, :], bank(7)[:, 0:P], ACT.Copy), tr, kd_free[y])

        def carry(m):
            y, u = m % 2, m // UT
            i, s = u % 2, S[u]
            for c in range(2):
                n = 2 * m + c
                if n % NC == NC - 1:
                    continue
                if n % NC == 0:
                    state_ok[n] = pr.dve("g_state", lambda e, n=n: e.memset(state[:, n % NS, :], 0.0),
                                         state_free[n % NS])
                r = slice(C * c, C * (c + 1))
                kb = bank(3 + c)
                kd_free[y] = done = pr.pe("kv_mm", last_of([
                    mm(kb[C * hh:C * (hh + 1), 0:P], kdT[r, y, C * hh:C * (hh + 1)],
                       v[r, i, m % UT, hh * P:(hh + 1) * P]) for hh in range(2)]),
                    kdT_ok[m], s["v"], kv_free[c])
                state_ok[n + 1] = kv_free[c] = pr.dve("g_state", lambda e, n=n, kb=kb:
                    e.scalar_tensor_tensor(
                        state[:, (n + 1) % NS, :], state[:, n % NS, :], dec[:, i, n % UC:n % UC + 1],
                        kb[:, 0:P], ALU.mult, ALU.add),
                    done, s["dec"], state_ok[n], state_free[(n + 1) % NS])

        def outer(m):
            nonlocal o_free
            ay, u = m % NA, m // UT
            i, s, m_ = u % 2, S[u], m % UT
            o_done = o_free
            for hh in range(2):
                outs = [bank(6)[C * c:C * (c + 1), hh * P:(hh + 1) * P] for c in range(2)]
                a1 = pr.pe("g_o_mm", last_of([
                    mm(outs[c], att[C * c:C * (c + 1), ay, hh, :],
                       v[C * c:C * (c + 1), i, m_, hh * P:(hh + 1) * P], True, False)
                    for c in range(2)]), att_ok[m], s["v"], o_done)
                r = slice(C * hh, C * (hh + 1))
                o_done = pr.pe("g_o_mm", last_of([
                    mm(outs[c], qf[r, i, m_ * P + C * c:m_ * P + C * (c + 1)],
                       state[r, (2 * m + c) % NS, :], False, True)
                    for c in range(2)]), a1, state_ok[2 * m], state_ok[2 * m + 1], s["qf"])
            for c in range(2):
                state_free[(2 * m + c) % NS] = o_done
            att_free[ay] = o_done
            o_free = pr.dve("g_raw", lambda e: e.tensor_copy(
                raw[:, i, m_, :], bank(6)[:, 0:2 * P]), o_done, raw_st[i])
            for hh in range(2):
                sq_last[hh] = s["sq"] = pr.act("g_sq", lambda e, hh=hh: e.activation(
                    junk[:, hh, :], raw[:, i, m_, hh * P:(hh + 1) * P], ACT.Square,
                    accum_out=ssq[:, i, m_, hh:hh + 1]), o_free, sq_last[hh])
            if m_ == UT - 1:
                used[i] = [o_done, s["sq"], o_free]

        def finish(u):
            hp, n = units[u]
            i = u % 2
            r_ok = rstd_from_sums(pr, "g_n", ssq[:, i], ssq[:, i], 1.0 / P, EPS, S[u]["sq"])
            for m_ in range(UT):
                for hh in range(2):
                    s_ = slice(hh * P, (hh + 1) * P)
                    f = pr.dve("g_final", lambda e, m_=m_, hh=hh, s_=s_: e.scalar_tensor_tensor(
                        raw[:, i, m_, s_], raw[:, i, m_, s_], ssq[:, i, m_, hh:hh + 1],
                        gate[:, i, m_, s_], ALU.mult, ALU.mult), r_ok, S[u]["gg"])
            used[i].append(f)
            raw_st[i] = pr.load(f"gla_st{i}", mix[n * W5:(n + 1) * W5, W5 + hp * 2 * P:
                                                  W5 + (hp + 1) * 2 * P].rearrange(
                "(m p) c -> p m c", p=P), raw[:, i, :, :], f)

        nt = len(units) * UT
        fetch(0)
        log_sigmoid(0)
        for part in range(3):
            prepare(0, part)
        for m in range(nt + 2):
            u, m_ = divmod(m, UT)
            if m < nt:
                inner(m)
            if 1 <= m <= nt:
                carry(m - 1)
            if m >= 2:
                outer(m - 2)
            if m_ == 1 and u >= 1:
                finish(u - 1)
            if u + 1 < len(units):
                if m_ == 1:
                    fetch(u + 1)
                    prepare(u + 1, 0)
                    prepare(u + 1, 1)
                if m_ == 2:
                    prepare(u + 1, 2)
            if m == 1:
                log_sigmoid(1)
            if m % 4 == 0 and m // 4 < KT:
                split_w(m // 4)
            if m >= nt:
                split_w(KT + m - nt)
        pr.hold("sp", raw_st)
        pr.emit()


def output_block(env, out_w, ple_w):
    pr, sb, t, bank, banks, ident = (env[k] for k in ("pr", "sb", "t", "bank", "banks", "ident"))
    KP = 2
    NR = 4
    with ExitStack() as st:
        g_hi = sb(st, "og_hi", [P, KT, D], F32R)
        g_lo = sb(st, "og_lo", [P, KT, D], F32R)
        q_hi, q_lo = ple_w
        mix = sb(st, "mix_ring", [P, 2, D])
        x_hi = sb(st, "mT_hi", [P, KT, P], F32R)
        x_lo = sb(st, "mT_lo", [P, KT, P], F32R)
        y_hi = sb(st, "rT_hi", [P, KT, P], F32R)
        y_lo = sb(st, "rT_lo", [P, KT, P], F32R)
        pin = sb(st, "p_ring", [P, 3, KP * P])
        p_hi = sb(st, "pT_hi", [P, KP, P], F32R)
        p_lo = sb(st, "pT_lo", [P, KP, P], F32R)
        r = sb(st, "r_ring", [P, NR, D])
        g = sb(st, "ple_g", [P, 2, W5])
        bp, lg, lb = (sb(st, f"row_{n}", [P, D]) for n in ("b_ple", "ln_g", "ln_b"))
        st6 = sb(st, "st6o", [P, 2, 12])
        mv = sb(st, "mvo", [P, 2, 2])
        rl = sb(st, "rlo", [P, 2, 2])
        m_in, r_in, p_in = {}, {}, {}
        m_free, r_free, p_free = [None] * 2, [None] * NR, [None] * 3
        x_ok, y_ok, pt_ok, x_used, y_used, pt_used = {}, {}, {}, None, None, None
        free = {b: None for b in range(8)}
        r_ok, g_free, gw_ok, last_pool = {}, [None] * 2, [], None

        def fetch(n):
            rows = slice(n * P, (n + 1) * P)
            m_in[n] = pr.load(f"mix_in{n % 2}", mix[:, n % 2, :], env["mix"][rows, :], m_free[n % 2])
            r_in[n] = pr.load(f"r_in{n % NR}", r[:, n % NR, :], env["h2"][rows, :], r_free[n % NR])
            p_in[n] = pr.load(f"p_in{n % 3}", pin[:, n % 3, :], t["p_2"][0, 0, rows, :], p_free[n % 3])

        def weights():
            for k in range(KT):
                x = 2 + k % 2
                ld = pr.load(f"ow_in{x}", r[:, x, :], t["w_ple_gate_2"][0, k * P:(k + 1) * P, :],
                             r_free[x])
                r_free[x] = split_pair(pr, "og", g_hi[:, k, :], g_lo[:, k, :], r[:, x, :], ld)
                gw_ok.append(r_free[x])

        def turn_mix(n):
            x_ok[n], m_free[n % 2] = transposed_halves(
                env, "mT", 0, mix[:, n % 2, :], x_hi, x_lo, free, (4, 5), m_in[n], x_used)

        def residual(n):
            nonlocal x_used
            x = n % NR
            r_ok[n] = []
            for c in range(2):
                cs = slice(c * W5, (c + 1) * W5)
                x_used = pr.pe("wo2_mm", contraction(
                    bank(c), [(x_hi[:, k, :], x_lo[:, k, :]) for k in range(KT)],
                    [(out_w[0][:, k, cs], out_w[1][:, k, cs]) for k in range(KT)]), x_ok[n], free[c])
                free[c] = pr.dve("r_mix", lambda e, c=c, cs=cs: e.scalar_tensor_tensor(
                    r[:, x, cs], r[:, x, cs], ALPHA, bank(c), ALU.mult, ALU.add), x_used, r_in[n])
                r_ok[n].append(free[c])

        def turn_r_p(n):
            y_ok[n], _ = transposed_halves(env, "rT", 0, r[:, n % NR, :], y_hi, y_lo, free, (6, 7),
                                           r_ok[n], y_used)
            tr = p_free[n % 3] = pr.pe("pT_turn", turns(bank(2), [
                pin[:, n % 3, k * P:(k + 1) * P] for k in range(KP)], ident), p_in[n], free[2])
            pt_ok[n] = free[2] = split_pair(
                pr, "pT", p_hi[:, :, :], p_lo[:, :, :],
                bank(2)[:, 0:KP * P].rearrange("p (j c) -> p j c", j=KP), tr, pt_used)

        def gates(n):
            nonlocal y_used, pt_used
            x, fin = n % NR, []
            pd = []
            for c in range(2):
                cs = slice(c * W5, (c + 1) * W5)
                pd.append(pr.pe("ple_mm", contraction(
                    bank(2 + c), [(p_hi[:, k, :], p_lo[:, k, :]) for k in range(KP)],
                    [(q_hi[:, k, cs], q_lo[:, k, cs]) for k in range(KP)]), pt_ok[n],
                    free[2 + c]))
            pt_used = pd[1]
            for c in range(2):
                cs, gb = slice(c * W5, (c + 1) * W5), 6 + c
                y_used = pr.pe("gate_mm", contraction(
                    bank(gb), [(y_hi[:, k, :], y_lo[:, k, :]) for k in range(KT)],
                    [(g_hi[:, k, cs], g_lo[:, k, cs]) for k in range(KT)]), gw_ok, y_ok[n],
                    free[gb])
                a = free[gb] = pr.dve("gate_b", lambda e, c=c, cs=cs, gb=gb: e.tensor_tensor(
                    g[:, c, :], bank(gb), bp[:, cs], ALU.add), y_used, bp_ok, g_free[c])
                a = pr.act("gate_sig", lambda e, c=c: e.activation(g[:, c, :], g[:, c, :],
                                                                   ACT.Sigmoid), a)
                a = free[2 + c] = pr.dve("gate_p", lambda e, c=c: e.tensor_tensor(
                    g[:, c, :], g[:, c, :], bank(2 + c), ALU.mult), a, pd[c])
                g_free[c] = pr.dve("r_gate", lambda e, c=c, cs=cs: e.tensor_tensor(
                    r[:, x, cs], r[:, x, cs], g[:, c, :], ALU.add), a, y_ok[n])
                fin.append(g_free[c])
            return fin

        def leave(n, fin):
            nonlocal last_pool
            x, i = n % NR, n % 2
            mv_ok = layer_norm_stats(pr, "lo", r[:, x, :], st6[:, i, :], mv[:, i, :], fin)
            b = rstd_from_sums(pr, "lor", rl[:, i, 0:1], mv[:, i, 1:2], 1.0, LN_EPS, mv_ok)
            b = pr.dve("lo_shift", lambda e: e.scalar_tensor_tensor(
                rl[:, i, 1:2], mv[:, i, 0:1], -1.0, rl[:, i, 0:1], ALU.mult, ALU.mult), b)
            b = pr.act("o_n", lambda e: e.activation(
                r[:, x, :], r[:, x, :], ACT.Identity, scale=rl[:, i, 0:1], bias=rl[:, i, 1:2]), b)
            b = pr.pool("o_g", lambda e: e.tensor_tensor(r[:, x, :], r[:, x, :], lg[:, :], ALU.mult),
                        b, lg_ok, last_pool)
            b = last_pool = pr.pool("o_b", lambda e: e.tensor_tensor(
                r[:, x, :], r[:, x, :], lb[:, :], ALU.add), b, lb_ok)
            r_free[x] = pr.load(f"out_st{x}", t["out"][0, n * P:(n + 1) * P, :], r[:, x, :], b)

        fetch(0)
        fetch(1)
        turn_mix(0)
        weights()
        bp_ok, lg_ok, lb_ok = (row_load(env, n, buf) for n, buf in (
            ("b_ple", bp), ("ln_g", lg), ("ln_b", lb)))
        for n in range(NT + 1):
            if n < NT:
                residual(n)
            if n >= 1:
                turn_r_p(n - 1)
            if n + 1 < NT:
                turn_mix(n + 1)
            if n + 2 < NT:
                fetch(n + 2)
            if n >= 1:
                leave(n - 1, gates(n - 1))
        pr.hold("sp", r_free)
        pr.emit()


def columns(a):
    return np.ascontiguousarray(a.reshape(-1, P).T)


def laid_out(inp):
    f = {k: np.asarray(v) for k, v in inp.items()}
    pairs = {"g1": f["norm1_g"], "mixg": np.concatenate([f["ssm_norm_g"], f["pool_norm_g"]], -1),
             "pscale": f["pool_scale"], "glub": f["ssm_glu_b"], "bgate": f["b_gla_gate_2"],
             "lr": f["ssm_lambda_re"], "li": f["ssm_lambda_im"],
             "log_step": np.repeat(f["ssm_log_step"], PS)}
    at, parts, n = {}, [], 0
    for name, a in pairs.items():
        c = columns(a)
        at[name] = n
        n += c.shape[1]
        parts.append(c)
    out = {"cols": np.concatenate(parts, 1)}

    def per_pair(a):
        return a.reshape(NQ, P, H).transpose(1, 0, 2)

    out["B_re"], out["B_im"] = per_pair(f["ssm_b_re"][0]), per_pair(f["ssm_b_im"][0])
    out["C_re"] = per_pair(f["ssm_c_re"][0].transpose(0, 2, 1))
    out["C_im"] = per_pair(f["ssm_c_im"][0].transpose(0, 2, 1))
    out["d"] = f["ssm_d"][0].T
    glu = np.zeros((P, 4, P), f["ssm_glu_w"].dtype)
    for g in range(G):
        q, r = g // 8, H * (g % 8)
        glu[r:r + H, q, r:r + H] = f["ssm_glu_w"][0, g]
    out["glu_w"] = glu
    out["rows"] = np.concatenate([f[k].reshape(-1) for k in (
        "norm2_g", "final_norm_g", "ln_in_g_2", "ln_in_b_2", "b_ple_gate_2", "ln_g_2", "ln_b_2",
        "gla_norm_g_2")])
    for k in ("x", "meta_tokens", "w_in", "pool_w", "w_out", "w_gate", "w_up", "w_down", "p_2",
              "w_in_2", "w_gla_gate_2", "rel_bias_2", "w_out_2", "w_ple_2", "w_ple_gate_2"):
        out[k] = f[k]
    return {k: np.ascontiguousarray(v) for k, v in out.items()}, at


ROWS = {n: i * D for i, n in enumerate(("g2", "gf", "lin_g", "lin_b", "b_ple", "ln_g", "ln_b",
                                        "gla_g"))}


def kernel(**inputs):
    import concourse.bacc as bacc
    from concourse.bass_utils import run_bass_kernel_spmd

    nc = bacc.Bacc("TRN2", target_bir_lowering=False, num_devices=1)
    arrays, at = laid_out(inputs)
    t = {"_cols": at}
    for name, a in arrays.items():
        t[name] = nc.dram_tensor(f"in_{name}", a.shape, F32, kind="ExternalInput").ap()
    t["out"] = nc.dram_tensor("out", (1, TOK, D), F32, kind="ExternalOutput").ap()
    build(nc, t)
    r = run_bass_kernel_spmd(nc, [{f"in_{k}": v for k, v in arrays.items()}], core_ids=[0])
    return r.results[0]["out"]
```
